# Optimizing a Trainium2 kernel written in Bass

```python
import math
import jax, jax.numpy as jnp
from jax import lax
import numpy as np

D_MODEL = 2048
BATCH = 1
SEQ = 256
DEPTH = 1

MEM_LEN = 256
EPS = 1e-6
SG_CHUNK = 128
SG_GROUPS = 8
SG_WIDTH = D_MODEL // 2
SG_GROUP_DIM = SG_WIDTH // SG_GROUPS
GLA_HEADS = 4
GLA_DK = D_MODEL // 2
GLA_DV = D_MODEL
GLA_HEAD_K = GLA_DK // GLA_HEADS
GLA_HEAD_V = GLA_DV // GLA_HEADS
GLA_GATE_RANK = 16
GLA_TAU = 16.0
GLA_CHUNK = 64
GLA_LOG_DECAY_MIN = -1.0
XA_HEADS = 4
XA_HEAD_DIM = 128
XA_WIDTH = XA_HEADS * XA_HEAD_DIM
D_FF = 5632
CONV_WIDTH = 3
IN_SPLITS = (2 * SG_WIDTH, GLA_DK, GLA_DK, GLA_DV, GLA_DV, GLA_GATE_RANK, D_MODEL, D_MODEL)
N_IN = 2 * SG_WIDTH + 2 * GLA_DK + 2 * GLA_DV + GLA_GATE_RANK + 2 * D_MODEL


def rmsnorm(x, g):
    xf = x.astype(jnp.float32)
    y = xf * lax.rsqrt(jnp.mean(xf * xf, axis=-1, keepdims=True) + EPS)
    return (y * g.astype(jnp.float32)).astype(x.dtype)

def layernorm(x, g, b):
    xf = x.astype(jnp.float32)
    mu = jnp.mean(xf, axis=-1, keepdims=True)
    xc = xf - mu
    y = xc * lax.rsqrt(jnp.mean(xc * xc, axis=-1, keepdims=True) + EPS)
    return (y * g.astype(jnp.float32) + b.astype(jnp.float32)).astype(x.dtype)

def spatial_gating(u, v, w_s, b_s):
    B, S, _ = v.shape
    n = S // SG_CHUNK
    vc = v.reshape(B, n, SG_CHUNK, SG_GROUPS, SG_GROUP_DIM)
    causal = jnp.tril(jnp.ones((SG_CHUNK, SG_CHUNK), dtype=bool))
    w = jnp.where(causal[None], w_s, 0).astype(v.dtype)
    s = jnp.einsum('gts,bnsge->bntge', w, vc) + b_s.T.astype(v.dtype)[None, None, :, :, None]
    return u * s.reshape(B, S, SG_WIDTH)

def gla_chunked(q, k, v, log_a):
    B, S, H, dk = q.shape
    dv = v.shape[-1]
    n = S // GLA_CHUNK

    def to_chunks(t):
        return t.astype(jnp.float32).reshape(B, n, GLA_CHUNK, H, t.shape[-1]).transpose(1, 0, 3, 2, 4)

    qc = to_chunks(q) * (dk ** -0.5)
    kc = to_chunks(k)
    vc = to_chunks(v)
    bcum = jnp.cumsum(to_chunks(log_a), axis=3)
    b_last = bcum[:, :, :, -1:, :]
    q_in = qc * jnp.exp(bcum)
    k_in = kc * jnp.exp(-bcum)
    k_st = kc * jnp.exp(b_last - bcum)
    causal = jnp.tril(jnp.ones((GLA_CHUNK, GLA_CHUNK), dtype=bool))
    attn = jnp.where(causal, jnp.einsum('nbhcd,nbhsd->nbhcs', q_in, k_in), 0.0)
    o_intra = jnp.einsum('nbhcs,nbhse->nbhce', attn, vc)

    def step(state, xs):
        q_c, k_c, v_c, dec = xs
        o = jnp.einsum('bhcd,bhde->bhce', q_c, state)
        state = state * dec[:, :, 0, :, None] + jnp.einsum('bhcd,bhce->bhde', k_c, v_c)
        return state, o

    init = jnp.zeros((B, H, dk, dv), jnp.float32)
    _, o_inter = lax.scan(step, init, (q_in, k_st, vc, jnp.exp(b_last)))
    o = o_intra + o_inter
    return o.transpose(1, 0, 3, 2, 4).reshape(B, S, H, dv).astype(v.dtype)

def token_mixer(h, w_in, sg_ln_g, sg_ln_b, sg_w, sg_b, gla_w_gate2, gla_b_gate, gla_norm_g,
                w_proj_a, w_proj_b, w_out):
    B, S, _ = h.shape
    idx = [int(i) for i in np.cumsum(IN_SPLITS)[:-1]]
    z = h @ w_in
    z_sg, q, k, v, og, g_lr, m_a, m_b = jnp.split(z, idx, axis=-1)
    z_sg = jax.nn.gelu(z_sg, approximate=False)
    u, vs = jnp.split(z_sg, 2, axis=-1)
    y_a = spatial_gating(u, layernorm(vs, sg_ln_g, sg_ln_b), sg_w, sg_b)
    gate_logit = (g_lr @ gla_w_gate2 + gla_b_gate).astype(jnp.float32)
    log_a = jnp.maximum(jax.nn.log_sigmoid(gate_logit) / GLA_TAU, GLA_LOG_DECAY_MIN)
    o = gla_chunked(q.reshape(B, S, GLA_HEADS, GLA_HEAD_K), k.reshape(B, S, GLA_HEADS, GLA_HEAD_K),
                    v.reshape(B, S, GLA_HEADS, GLA_HEAD_V), log_a.reshape(B, S, GLA_HEADS, GLA_HEAD_K))
    o = rmsnorm(o, gla_norm_g) * jax.nn.silu(og.reshape(B, S, GLA_HEADS, GLA_HEAD_V))
    y_b = o.reshape(B, S, GLA_DV)
    merged = jax.nn.sigmoid(m_a) * (y_a @ w_proj_a) + jax.nn.sigmoid(m_b) * (y_b @ w_proj_b)
    return merged @ w_out

def memory_cross_attention(h, mem_n, wq, wk, wv, wo):
    B, S, _ = h.shape
    M = mem_n.shape[1]
    q = (h @ wq).reshape(B, S, XA_HEADS, XA_HEAD_DIM)
    k = (mem_n @ wk).reshape(B, M, XA_HEADS, XA_HEAD_DIM)
    v = (mem_n @ wv).reshape(B, M, XA_HEADS, XA_HEAD_DIM)
    s = jnp.einsum('bshd,bmhd->bhsm', q, k).astype(jnp.float32) * (XA_HEAD_DIM ** -0.5)
    p = jax.nn.softmax(s, axis=-1).astype(v.dtype)
    o = jnp.einsum('bhsm,bmhd->bshd', p, v).reshape(B, S, XA_WIDTH)
    return o @ wo

def conv_ffn(h, w_up, conv_w, conv_b, w_down):
    hid = h @ w_up
    rhs = conv_w[:, None, :].astype(hid.dtype)
    hid = lax.conv_general_dilated(hid, rhs, window_strides=(1,), padding=[(CONV_WIDTH - 1, 0)],
                                   dimension_numbers=('NWC', 'WIO', 'NWC'),
                                   feature_group_count=2 * D_FF) + conv_b.astype(hid.dtype)
    gate, up = jnp.split(hid, 2, axis=-1)
    return (jax.nn.gelu(gate, approximate=True) * up) @ w_down

def first_inputs(seed: int = 0) -> dict:
    key = jax.random.key(seed)
    ks = jax.random.split(key, 32)
    f32 = jnp.float32

    def nrm(k, shape, scale):
        return jax.random.normal(k, shape, f32) * scale

    def gain(k, shape):
        return 1.0 + 0.1 * jax.random.normal(k, shape, f32)

    L, D = DEPTH, D_MODEL
    return {
        'x': nrm(ks[0], (BATCH, SEQ, D), 1.0),
        'mem': nrm(ks[1], (BATCH, MEM_LEN, D), 1.0),
        'pre_norm_mix': gain(ks[2], (L, D)),
        'w_in': nrm(ks[3], (L, D, N_IN), D ** -0.5),
        'sg_ln_g': gain(ks[4], (L, SG_WIDTH)),
        'sg_ln_b': nrm(ks[5], (L, SG_WIDTH), 0.02),
        'sg_w': nrm(ks[6], (L, SG_GROUPS, SG_CHUNK, SG_CHUNK), SG_CHUNK ** -0.5),
        'sg_b': gain(ks[7], (L, SG_GROUPS, SG_CHUNK)),
        'gla_w_gate2': nrm(ks[8], (L, GLA_GATE_RANK, GLA_DK), GLA_GATE_RANK ** -0.5),
        'gla_b_gate': nrm(ks[9], (L, GLA_DK), 0.1),
        'gla_norm_g': gain(ks[10], (L, GLA_HEAD_V)),
        'w_proj_a': nrm(ks[11], (L, SG_WIDTH, D), SG_WIDTH ** -0.5),
        'w_proj_b': nrm(ks[12], (L, GLA_DV, D), GLA_DV ** -0.5),
        'w_out': nrm(ks[13], (L, D, D), D ** -0.5),
        'post_norm_mix': gain(ks[14], (L, D)),
        'pre_norm_xa': gain(ks[15], (L, D)),
        'mem_norm_g': gain(ks[16], (L, D)),
        'xa_wq': nrm(ks[17], (L, D, XA_WIDTH), D ** -0.5),
        'xa_wk': nrm(ks[18], (L, D, XA_WIDTH), D ** -0.5),
        'xa_wv': nrm(ks[19], (L, D, XA_WIDTH), D ** -0.5),
        'xa_wo': nrm(ks[20], (L, XA_WIDTH, D), XA_WIDTH ** -0.5),
        'post_norm_xa': gain(ks[21], (L, D)),
        'pre_norm_ffn': gain(ks[22], (L, D)),
        'ffn_w_up': nrm(ks[23], (L, D, 2 * D_FF), D ** -0.5),
        'ffn_conv_w': nrm(ks[24], (L, CONV_WIDTH, 2 * D_FF), CONV_WIDTH ** -0.5),
        'ffn_conv_b': nrm(ks[25], (L, 2 * D_FF), 0.02),
        'ffn_w_down': nrm(ks[26], (L, D_FF, D), D_FF ** -0.5),
        'post_norm_ffn': gain(ks[27], (L, D)),
    }

def first_block(x, mem, pre_norm_mix, w_in, sg_ln_g, sg_ln_b, sg_w, sg_b, gla_w_gate2, gla_b_gate,
              gla_norm_g, w_proj_a, w_proj_b, w_out, post_norm_mix, pre_norm_xa, mem_norm_g,
              xa_wq, xa_wk, xa_wv, xa_wo, post_norm_xa, pre_norm_ffn, ffn_w_up, ffn_conv_w,
              ffn_conv_b, ffn_w_down, post_norm_ffn):
    for l in range(DEPTH):
        h = rmsnorm(x, pre_norm_mix[l])
        y = token_mixer(h, w_in[l], sg_ln_g[l], sg_ln_b[l], sg_w[l], sg_b[l], gla_w_gate2[l],
                        gla_b_gate[l], gla_norm_g[l], w_proj_a[l], w_proj_b[l], w_out[l])
        x = x + rmsnorm(y, post_norm_mix[l])
        h = rmsnorm(x, pre_norm_xa[l])
        m = rmsnorm(mem, mem_norm_g[l])
        y = memory_cross_attention(h, m, xa_wq[l], xa_wk[l], xa_wv[l], xa_wo[l])
        x = x + rmsnorm(y, post_norm_xa[l])
        h = rmsnorm(x, pre_norm_ffn[l])
        y = conv_ffn(h, ffn_w_up[l], ffn_conv_w[l], ffn_conv_b[l], ffn_w_down[l])
        x = x + rmsnorm(y, post_norm_ffn[l])
    return x


CHUNK = 64
D_MIX = D_MODEL
ATTN_WIDTH = D_MIX // 2
SSD_WIDTH = D_MIX - ATTN_WIDTH
ATTN_HEAD_DIM = 128
ATTN_Q_HEADS = ATTN_WIDTH // ATTN_HEAD_DIM
ATTN_KV_HEADS = 2
ROPE_THETA = 500000.0
ROPE_PARTIAL_DIV = 4
IDX_HEADS = 16
IDX_HEAD_DIM = 64
IDX_TOPK_MAX = 256
Q_BLOCK = 128
SSD_HEAD_DIM = 64
SSD_HEADS = SSD_WIDTH // SSD_HEAD_DIM
SSD_GROUPS = 4
SSD_HEADS_PER_GROUP = SSD_HEADS // SSD_GROUPS
SSD_STATE = 128
SSD_CONV = 4
SSD_CHUNK = CHUNK
SSD_XBC_WIDTH = SSD_WIDTH + 2 * SSD_GROUPS * SSD_STATE
DEEPNORM_ALPHA = (2.0 * DEPTH) ** 0.25
DEEPNORM_BETA = (8.0 * DEPTH) ** -0.25
LN_EPS = 1e-5
RMS_EPS = 1e-5
IN_WIDTHS = (
    ATTN_Q_HEADS * ATTN_HEAD_DIM,
    ATTN_KV_HEADS * ATTN_HEAD_DIM,
    ATTN_KV_HEADS * ATTN_HEAD_DIM,
    ATTN_WIDTH,
    IDX_HEADS * IDX_HEAD_DIM,
    IDX_HEAD_DIM,
    IDX_HEADS,
    SSD_WIDTH,
    SSD_XBC_WIDTH,
    SSD_HEADS,
)
IN_TOTAL = sum(IN_WIDTHS)
VALUE_COL = 2


def _split_cols(u, widths):
    out, start = [], 0
    for w in widths:
        out.append(u[..., start:start + w])
        start += w
    return out

def _layer_norm(x, g, b):
    x32 = x.astype(jnp.float32)
    mu = jnp.mean(x32, axis=-1, keepdims=True)
    var = jnp.mean(jnp.square(x32 - mu), axis=-1, keepdims=True)
    y = (x32 - mu) * lax.rsqrt(var + LN_EPS) * g.astype(jnp.float32) + b.astype(jnp.float32)
    return y.astype(x.dtype)

def _rope_partial(t, pos):
    d = t.shape[-1]
    rot = d // ROPE_PARTIAL_DIV
    half = rot // 2
    inv = ROPE_THETA ** (-jnp.arange(half, dtype=jnp.float32) * 2.0 / rot)
    ang = pos[:, None] * inv[None, :]
    cos = jnp.cos(ang)[:, None, :]
    sin = jnp.sin(ang)[:, None, :]
    t32 = t.astype(jnp.float32)
    x1 = t32[..., :half]
    x2 = t32[..., half:rot]
    out = jnp.concatenate([x1 * cos - x2 * sin, x2 * cos + x1 * sin, t32[..., rot:]], axis=-1)
    return out.astype(t.dtype)

def _dsa_attention(q, k, v, q_idx, k_idx, w_idx):
    bsz, seq = q.shape[0], q.shape[1]
    topk = min(IDX_TOPK_MAX, seq // 4)
    rep = ATTN_Q_HEADS // ATTN_KV_HEADS
    scale = ATTN_HEAD_DIM ** -0.5
    key_chunk = jnp.arange(seq) // CHUNK
    k_idx32 = k_idx.astype(jnp.float32)
    gather = jax.vmap(lambda a, ix: a[ix])

    def block(i):
        start = i * Q_BLOCK
        sl = lambda a: lax.dynamic_slice_in_dim(a, start, Q_BLOCK, axis=1)
        qb, qib, wb = sl(q), sl(q_idx), sl(w_idx)
        q_chunk = (start + jnp.arange(Q_BLOCK)) // CHUNK
        logits = jax.nn.relu(jnp.einsum('bqhd,bsd->bqhs', qib.astype(jnp.float32), k_idx32))
        score = jnp.einsum('bqhs,bqh->bqs', logits, wb.astype(jnp.float32))
        admissible = key_chunk[None, :] <= q_chunk[:, None]
        score = jnp.where(admissible[None], score, -jnp.inf)
        _, sel = lax.top_k(score, topk)
        valid = key_chunk[sel] <= q_chunk[None, :, None]
        kg = gather(k, sel)
        vg = gather(v, sel)
        qg = qb.reshape(bsz, Q_BLOCK, ATTN_KV_HEADS, rep, ATTN_HEAD_DIM)
        s = jnp.einsum('bqgrd,bqkgd->bqgrk', qg, kg).astype(jnp.float32) * scale
        s = jnp.where(valid[:, :, None, None, :], s, -jnp.inf)
        p = jax.nn.softmax(s, axis=-1).astype(vg.dtype)
        o = jnp.einsum('bqgrk,bqkgd->bqgrd', p, vg)
        return o.reshape(bsz, Q_BLOCK, ATTN_Q_HEADS * ATTN_HEAD_DIM)

    out = lax.map(block, jnp.arange(seq // Q_BLOCK))
    return out.transpose(1, 0, 2, 3).reshape(bsz, seq, ATTN_Q_HEADS * ATTN_HEAD_DIM)

def _causal_depthwise_conv(u, w, b):
    c = u.shape[-1]
    y = lax.conv_general_dilated(u, w[:, None, :], window_strides=(1,), padding=[(SSD_CONV - 1, 0)],
                                 dimension_numbers=('NWC', 'WIO', 'NWC'), feature_group_count=c)
    return y + b

def _ssd_mixer(xbc, z, dt_raw, conv_w, conv_b, dt_bias, a_log, d_skip, norm_w):
    bsz, seq, _ = xbc.shape
    G, R, P, N, l = SSD_GROUPS, SSD_HEADS_PER_GROUP, SSD_HEAD_DIM, SSD_STATE, SSD_CHUNK
    nc = seq // l
    xbc = jax.nn.silu(_causal_depthwise_conv(xbc, conv_w, conv_b))
    xs, bm, cm = _split_cols(xbc, (SSD_WIDTH, G * N, G * N))
    xs = xs.astype(jnp.float32).reshape(bsz, nc, l, G, R, P)
    bm = bm.astype(jnp.float32).reshape(bsz, nc, l, G, N)
    cm = cm.astype(jnp.float32).reshape(bsz, nc, l, G, N)
    dt = jax.nn.softplus(dt_raw.astype(jnp.float32) + dt_bias.astype(jnp.float32))
    dt = dt.reshape(bsz, nc, l, G, R)
    a = -jnp.exp(a_log.astype(jnp.float32)).reshape(G, R)
    xdt = xs * dt[..., None]
    a_cum = jnp.cumsum(dt * a, axis=2)
    seg = a_cum[:, :, :, None] - a_cum[:, :, None, :]
    tril = jnp.tril(jnp.ones((l, l), dtype=bool))[:, :, None, None]
    lmat = jnp.exp(jnp.where(tril, seg, -jnp.inf))
    cb = jnp.einsum('bclgn,bcsgn->bclsg', cm, bm)
    y_diag = jnp.einsum('bclsg,bclsgr,bcsgrp->bclgrp', cb, lmat, xdt)
    decay = jnp.exp(a_cum[:, :, -1:] - a_cum)
    states = jnp.einsum('bcsgn,bcsgr,bcsgrp->bcgrpn', bm, decay, xdt)
    chunk_decay = jnp.exp(a_cum[:, :, -1])

    def step(h, inp):
        st, dec = inp
        return h * dec[..., None, None] + st, h

    h0 = jnp.zeros((bsz, G, R, P, N), jnp.float32)
    _, prev = lax.scan(step, h0, (jnp.moveaxis(states, 1, 0), jnp.moveaxis(chunk_decay, 1, 0)))
    prev = jnp.moveaxis(prev, 0, 1)
    y_off = jnp.einsum('bclgn,bcgrpn,bclgr->bclgrp', cm, prev, jnp.exp(a_cum))
    y = y_diag + y_off + d_skip.astype(jnp.float32).reshape(G, R)[:, :, None] * xs
    y = y.reshape(bsz, seq, SSD_WIDTH)
    g = (y * jax.nn.silu(z.astype(jnp.float32))).reshape(bsz, seq, G, SSD_WIDTH // G)
    g = g * lax.rsqrt(jnp.mean(jnp.square(g), axis=-1, keepdims=True) + RMS_EPS)
    return (g.reshape(bsz, seq, SSD_WIDTH) * norm_w.astype(jnp.float32)).astype(z.dtype)

def second_inputs(seed: int = 0) -> dict:
    key = jax.random.key(seed)
    ks = jax.random.split(key, 12)
    x = jax.random.normal(ks[0], (BATCH, SEQ, D_MODEL), jnp.float32)
    blk_keys = jax.random.split(ks[1], len(IN_WIDTHS))
    blocks = []
    for j, w in enumerate(IN_WIDTHS):
        scale = D_MODEL ** -0.5 * (DEEPNORM_BETA if j == VALUE_COL else 1.0)
        blocks.append(jax.random.normal(blk_keys[j], (DEPTH, D_MODEL, w), jnp.float32) * scale)
    w_in = jnp.concatenate(blocks, axis=-1)
    w_out = jax.random.normal(ks[2], (DEPTH, D_MIX, D_MODEL), jnp.float32) * (D_MIX ** -0.5 * DEEPNORM_BETA)
    conv_w = jax.random.normal(ks[3], (DEPTH, SSD_CONV, SSD_XBC_WIDTH), jnp.float32) * SSD_CONV ** -0.5
    conv_b = 0.01 * jax.random.normal(ks[4], (DEPTH, SSD_XBC_WIDTH), jnp.float32)
    u = jax.random.uniform(ks[5], (DEPTH, SSD_HEADS), jnp.float32)
    dt0 = jnp.exp(u * (math.log(0.1) - math.log(0.001)) + math.log(0.001))
    dt_bias = dt0 + jnp.log(-jnp.expm1(-dt0))
    a_log = jnp.log(jax.random.uniform(ks[6], (DEPTH, SSD_HEADS), jnp.float32, 1.0, 16.0))
    d_skip = 1.0 + 0.1 * jax.random.normal(ks[7], (DEPTH, SSD_HEADS), jnp.float32)
    ssd_norm_w = 1.0 + 0.1 * jax.random.normal(ks[8], (DEPTH, SSD_WIDTH), jnp.float32)
    ln_g = 1.0 + 0.1 * jax.random.normal(ks[9], (DEPTH, D_MODEL), jnp.float32)
    ln_b = 0.01 * jax.random.normal(ks[10], (DEPTH, D_MODEL), jnp.float32)
    return {"x": x, "w_in": w_in, "w_out": w_out, "conv_w": conv_w, "conv_b": conv_b,
            "dt_bias": dt_bias, "a_log": a_log, "d_skip": d_skip, "ssd_norm_w": ssd_norm_w,
            "ln_g": ln_g, "ln_b": ln_b}

def second_block(x, w_in, w_out, conv_w, conv_b, dt_bias, a_log, d_skip, ssd_norm_w, ln_g, ln_b):
    bsz, seq, _ = x.shape
    pos = jnp.arange(seq, dtype=jnp.float32)
    h = x
    for layer in range(DEPTH):
        u = jnp.einsum('bsd,de->bse', h, w_in[layer])
        q, k, v, z_attn, q_idx, k_idx, w_idx, z_ssd, xbc, dt_raw = _split_cols(u, IN_WIDTHS)
        q = _rope_partial(q.reshape(bsz, seq, ATTN_Q_HEADS, ATTN_HEAD_DIM), pos)
        k = _rope_partial(k.reshape(bsz, seq, ATTN_KV_HEADS, ATTN_HEAD_DIM), pos)
        v = v.reshape(bsz, seq, ATTN_KV_HEADS, ATTN_HEAD_DIM)
        q_idx = _rope_partial(q_idx.reshape(bsz, seq, IDX_HEADS, IDX_HEAD_DIM), pos)
        k_idx = _rope_partial(k_idx[:, :, None, :], pos)[:, :, 0, :]
        w_idx = w_idx * (IDX_HEADS ** -0.5 * IDX_HEAD_DIM ** -0.5)
        o_attn = _dsa_attention(q, k, v, q_idx, k_idx, w_idx) * jax.nn.silu(z_attn)
        o_ssd = _ssd_mixer(xbc, z_ssd, dt_raw, conv_w[layer], conv_b[layer], dt_bias[layer],
                           a_log[layer], d_skip[layer], ssd_norm_w[layer])
        mixed = jnp.concatenate([o_attn, o_ssd.astype(o_attn.dtype)], axis=-1)
        sub = jnp.einsum('bse,ed->bsd', mixed, w_out[layer])
        h = _layer_norm(DEEPNORM_ALPHA * h + sub, ln_g[layer], ln_b[layer])
    return h


def setup_inputs(seed=0):
    out = dict(first_inputs(seed))
    for name, value in second_inputs(seed + 1).items():
        if name != "x":
            out[name + "_2"] = value
    return out


def reference(
    x, mem, pre_norm_mix, w_in, sg_ln_g, sg_ln_b, sg_w, sg_b, gla_w_gate2, gla_b_gate,
    gla_norm_g, w_proj_a, w_proj_b, w_out, post_norm_mix, pre_norm_xa, mem_norm_g, xa_wq, xa_wk,
    xa_wv, xa_wo, post_norm_xa, pre_norm_ffn, ffn_w_up, ffn_conv_w, ffn_conv_b, ffn_w_down,
    post_norm_ffn, w_in_2, w_out_2, conv_w_2, conv_b_2, dt_bias_2, a_log_2, d_skip_2,
    ssd_norm_w_2, ln_g_2, ln_b_2,
):
    x = first_block(
        x, mem, pre_norm_mix, w_in, sg_ln_g, sg_ln_b, sg_w, sg_b, gla_w_gate2, gla_b_gate,
        gla_norm_g, w_proj_a, w_proj_b, w_out, post_norm_mix, pre_norm_xa, mem_norm_g, xa_wq,
        xa_wk, xa_wv, xa_wo, post_norm_xa, pre_norm_ffn, ffn_w_up, ffn_conv_w, ffn_conv_b,
        ffn_w_down, post_norm_ffn,
    )
    return second_block(
        x, w_in_2, w_out_2, conv_w_2, conv_b_2, dt_bias_2, a_log_2, d_skip_2, ssd_norm_w_2,
        ln_g_2, ln_b_2,
    )


_drawn_inputs = setup_inputs


def setup_inputs(seed=0):
    import zlib

    import numpy as np

    out = dict(_drawn_inputs(seed))
    spreads = {}
    factors = {'conv_b_2': 8.0, 'd_skip_2': 8.0, 'ssd_norm_w_2': 3.147, 'ln_b_2': 5.571, 'sg_ln_b': 2.875}
    for name, (base, spread) in spreads.items():
        noise = np.random.default_rng([zlib.crc32(name.encode()), seed]).standard_normal(out[name].shape)
        drawn = base * np.exp(spread * noise) if base else spread * noise
        out[name] = __import__('jax').numpy.asarray(drawn.astype(out[name].dtype))
    for name, factor in factors.items():
        out[name] = (out[name] * factor).astype(out[name].dtype)
    return out
```

```python
import math

import numpy as np

import concourse.bass as bass
from concourse import mybir

F = mybir.dt.float32
R = mybir.dt.float32r
ALU = mybir.AluOpType
ACT = mybir.ActivationFunctionType
AX = mybir.AxisListType

SEQ = 256
D = 2048
KC = D // 128
FF = 5632
EPS = 1e-6
LN_EPS = 1e-5
ALPHA = 2.0 ** 0.25
BIG = 1.0e30
GONE = -3.0e38
TOPK = 64

KB = 1024
BASE = 16512

C_ID, C_TRIU, C_GT, C_M64, C_SCAN, C_CA, C_SA, C_CI, C_SI, C_END = 0, 128, 256, 384, 512, 768, 800, 832, 848, 864


def shape_constants():
    c = np.zeros((128, C_END), np.float32)
    i = np.arange(128)
    c[:, C_ID:C_ID + 128] = np.eye(128)
    c[:, C_TRIU:C_TRIU + 128] = i[None, :] >= i[:, None]
    c[:, C_GT:C_GT + 128] = i[:, None] > i[None, :]
    c[:64, C_M64 + 64:C_M64 + 128] = -BIG
    c[:, C_SCAN:C_SCAN + 256] = (np.arange(256) % 64 != 0)
    pos = np.arange(SEQ, dtype=np.float32)
    for rot, cc, cs in ((32, C_CA, C_SA), (16, C_CI, C_SI)):
        half = rot // 2
        inv = np.float32(500000.0) ** (-np.arange(half, dtype=np.float32) * np.float32(2.0) / np.float32(rot))
        ang = (pos[:, None] * inv.astype(np.float32)[None, :]).astype(np.float32)
        for tab, col in ((np.cos(ang), cc), (np.sin(ang), cs)):
            for tb in range(2):
                c[:, col + tb * half:col + (tb + 1) * half] = tab[tb * 128:(tb + 1) * 128]
    return c


def build(nc, I, cst_d, out_d):
    engines = ("pe", "dve", "act", "pool", "sp")
    queue = {e: [] for e in engines}
    sem = {e: nc.alloc_semaphore("s_" + e) for e in engines}
    count = dict.fromkeys(engines, 0)
    seen = {e: {} for e in engines}

    def tokens(w):
        if w is None:
            return []
        if isinstance(w, tuple) and len(w) == 2 and isinstance(w[1], int):
            return [w]
        return [p for x in w for p in tokens(x)]

    def put(e, fn, waits, signal=True):
        todo = []
        for s, n in tokens(waits):
            if seen[e].get(s.num, 0) < n:
                seen[e][s.num] = n
                todo.append((s, n))
        if signal:
            count[e] += 1
        queue[e].append((todo, fn, signal))
        return (sem[e], count[e]) if signal else None

    def tt(out, a, b, op, *w):
        return put("dve", lambda e: e.tensor_tensor(out, a, b, op), w)

    def ts(out, a, s1, op0, s2, op1, *w):
        if op1 is None:
            return put("dve", lambda e: e.tensor_scalar(out, a, s1, None, op0), w)
        return put("dve", lambda e: e.tensor_scalar(out, a, s1, s2, op0, op1), w)

    def stt(out, a, s, b, op0, op1, *w):
        return put("dve", lambda e: e.scalar_tensor_tensor(out=out, in0=a, scalar=s, in1=b, op0=op0, op1=op1), w)

    def vcopy(out, a, *w):
        return put("dve", lambda e: e.tensor_copy(out, a), w)

    def vset(out, v, *w):
        return put("dve", lambda e: e.memset(out, v), w)

    def recip(out, a, *w):
        return put("dve", lambda e: e.reciprocal(out, a), w)

    def reduce(out, a, op, *w):
        return put("dve", lambda e: e.tensor_reduce(out, a, AX.X, op), w)

    def act(out, a, func, *w, bias=0.0, scale=1.0, accum=None):
        if accum is None:
            return put("act", lambda e: e.activation(out, a, func, bias=bias, scale=scale), w)
        return put("act", lambda e: e.activation(out, a, func, bias=bias, scale=scale, accum_out=accum), w)

    last_junk = {}

    def square(junk, a, accum, *w):
        t = act(junk, a, ACT.Square, w, last_junk.get(junk.name), accum=accum)
        last_junk[junk.name] = t
        return t

    def mm(out, l, r, start, stop, *w, sig=False, share=False):
        return put("pe", lambda e: e.matmul(out, l, r, start=start, stop=stop, skip_group_check=share), w, sig)

    def tr(out, a, *w, sig=False):
        return put("pe", lambda e: e.transpose(out, a, ident), w, sig)

    def load(e, out, src, *w):
        nsem[0] += 1
        s = nc.alloc_semaphore(f"s_ld{nsem[0]}")
        put(e, lambda g: g.dma_start(out, src).then_inc(s, 16), w, False)
        return (s, 16)

    nsem = [0]

    nname = [0]

    def at(kb, shape, dt=F):
        nname[0] += 1
        t = nc.alloc_sbuf_tensor_at(f"b{nname[0]}", shape, dt, offset=BASE + int(kb * KB))
        return t[:, :] if len(shape) == 2 else t[:, :, :]

    RAW, SPL, XT, A, B, C, G, DD, M, K0 = 0, 24, 72, 104, 120, 128, 148, 164, 180, 196
    raw = [at(RAW + 8 * i, [128, 2048]) for i in range(3)]
    wh = [at(SPL + 16 * i, [128, 2048], R) for i in range(3)]
    wl = [at(SPL + 16 * i + 8, [128, 2048], R) for i in range(3)]
    xth = at(XT, [128, KC, 256], R)
    xtl = at(XT + 16, [128, KC, 256], R)
    cst = at(K0, [128, C_END])
    ident = cst[:, C_ID:C_ID + 128]
    triu = cst[:, C_TRIU:C_TRIU + 128]
    gt = cst[:, C_GT:C_GT + 128]
    m64 = cst[:, C_M64:C_M64 + 128]
    scan1 = cst[:, C_SCAN:C_SCAN + 256]
    ones = at(K0 + 3.5, [128, 128])
    VT = at(K0 + 4, [128, 6 * 128])
    st = at(K0 + 7, [128, 256])
    glr = at(K0 + 8, [128, 32])
    glrT = at(K0 + 8.125, [16, 256])
    sgb = at(K0 + 9.25, [1, 256])
    dtb = at(K0 + 10.25, [128, 16])
    alog = at(K0 + 10.3125, [128, 16])
    dsk = at(K0 + 10.375, [128, 16])
    dt_ = at(K0 + 10.5, [128, 32])
    adt = at(K0 + 10.625, [128, 32])
    dtmp = at(K0 + 10.75, [128, 32])
    dtm2 = at(K0 + 10.875, [128, 32])
    widx = at(K0 + 11, [128, 32])
    dl1 = at(K0 + 11.125, [128, 32])
    do1 = at(K0 + 11.25, [128, 32])

    used = [0]

    def small(n):
        used[0] += n
        assert used[0] <= 256
        return st[:, used[0] - n:used[0]]

    ps = [[nc.alloc_psum_tensor(f"ps{s}{b}", [128, 512], F)[:, :] for b in range(2)] for s in range(2)]
    ms = [nc.alloc_psum_tensor(f"pm{b}", [128, 512], F)[:, :] for b in range(4)]
    mfree = [[], [], [], []]
    mnext = [0]

    def bank():
        b = mnext[0] % 4
        mnext[0] += 1
        return b, ms[b], mfree[b]

    def v3(ap, n):
        return ap.rearrange("p (a b) -> p a b", b=n)

    def bc(ap, shape):
        return ap.to_broadcast(shape)

    groups = []

    def group(name, w, kcs, cols, kind, xh, xl, ready, evac, chunk=4, k_off=0):
        groups.append(dict(name=name, w=w, kcs=kcs, cols=cols, kind=kind, xh=xh, xl=xl, ready=ready,
                           evac=evac, chunk=chunk, k_off=k_off))

    T = {}
    hooks = {}

    def hook(name, unit, fn):
        hooks.setdefault((name, unit), []).append(fn)

    def run():
        units = []
        for gi, g in enumerate(groups):
            k = 0
            ui = 0
            while k < g["kcs"]:
                nk = min(g["chunk"], g["kcs"] - k)
                units.append((gi, ui, k, nk))
                k += nk
                ui += 1
        n_units = len(units)
        raw_sem = [nc.alloc_semaphore(f"s_raw{i}") for i in range(3)]
        raw_cnt = [0, 0, 0]
        landed, hi, lo, done = {}, {}, {}, {}
        set_free = [[], []]

        def dma(n):
            gi, ui, k, nk = units[n]
            g = groups[gi]
            s = n % 3
            nc_ = sum(c for _, c in g["cols"])
            dst = raw[s][:, 0:nk * nc_].rearrange("p (k c) -> p k c", c=nc_)
            w = [hi.get(n - 3), lo.get(n - 3)]
            o = 0
            k0 = g["k_off"] + k
            for c0, c in g["cols"]:
                src = g["w"][k0 * 128:(k0 + nk) * 128, c0:c0 + c].rearrange("(k p) c -> p k c", p=128)
                d = dst[:, :, o:o + c]
                put("sp", lambda e, d=d, src=src, s=s: e.dma_start(d, src).then_inc(raw_sem[s], 16), w, False)
                raw_cnt[s] += 16
                o += c
            landed[n] = (raw_sem[s], raw_cnt[s])

        def split_hi(n):
            gi, ui, k, nk = units[n]
            s = n % 3
            m = nk * sum(c for _, c in groups[gi]["cols"])
            hi[n] = act(wh[s][:, 0:m], raw[s][:, 0:m], ACT.Copy, landed[n], done.get(n - 3))

        def split_lo(n):
            gi, ui, k, nk = units[n]
            s = n % 3
            m = nk * sum(c for _, c in groups[gi]["cols"])
            lo[n] = tt(wl[s][:, 0:m], raw[s][:, 0:m], wh[s][:, 0:m].bitcast(F), ALU.subtract,
                       landed[n], hi[n], done.get(n - 3))

        def products(n):
            gi, ui, k, nk = units[n]
            g = groups[gi]
            s = n % 3
            pset = ps[gi % 2]
            nc_ = sum(c for _, c in g["cols"])
            h3 = wh[s][:, 0:nk * nc_].rearrange("p (k c) -> p k c", c=nc_)
            l3 = wl[s][:, 0:nk * nc_].rearrange("p (k c) -> p k c", c=nc_)
            w = [hi[n], lo[n]]
            if ui == 0:
                w += [set_free[gi % 2]]
            last_unit = k + nk == g["kcs"]
            for kk in range(nk):
                kg = k + kk
                w = w + [g["ready"](kg)]
                final = kk == nk - 1
                for b in range(2):
                    if g["kind"] == "tok":
                        xs_ = slice(b * 128, b * 128 + 128)
                        trio = [(g["xh"][:, kg, xs_], h3[:, kk, :]), (g["xh"][:, kg, xs_], l3[:, kk, :]),
                                (g["xl"][:, kg, xs_], h3[:, kk, :])]
                        for q, (l, r) in enumerate(trio):
                            tok = mm(pset[b][:, 0:nc_], l, r, kg == 0 and q == 0, kg == g["kcs"] - 1 and q == 2, w,
                                     sig=final and b == 1 and q == 2)
                            w = []
                    else:
                        for f in range(2):
                            cs = slice((2 * b + f) * 128, (2 * b + f + 1) * 128)
                            o = pset[b][:, f * 256:(f + 1) * 256]
                            trio = [(h3[:, kk, cs], g["xh"][:, kg, :]), (h3[:, kk, cs], g["xl"][:, kg, :]),
                                    (l3[:, kk, cs], g["xh"][:, kg, :])]
                            for q, (l, r) in enumerate(trio):
                                tok = mm(o, l, r, kg == 0 and q == 0 and f == 0, kg == g["kcs"] - 1 and q == 2, w,
                                         sig=final and b == 1 and f == 1 and q == 2, share=True)
                                w = []
            done[n] = tok
            T["pe:" + g["name"]] = tok
            if last_unit:
                r = g["evac"](pset, tok)
                set_free[gi % 2] = r

        for n in range(min(3, n_units)):
            dma(n)
        for n in range(min(2, n_units)):
            split_hi(n)
            split_lo(n)
            if n + 3 < n_units:
                dma(n + 3)
        for n in range(n_units):
            gi, ui, k, nk = units[n]
            if n + 2 < n_units:
                split_hi(n + 2)
            for fn in hooks.pop((groups[gi]["name"], ui), []):
                fn()
            if n + 2 < n_units:
                split_lo(n + 2)
                if n + 5 < n_units:
                    dma(n + 5)
            products(n)
        assert not hooks, hooks.keys()

    def rstd_of(ssq, n, eps, *w):
        k = ssq.shape[-1]
        a, b = small(k), small(k)
        t = ts(a, ssq, 1.0 / n, ALU.mult, eps, ALU.add, *w)
        t = act(b, a, ACT.Sqrt, t)
        c = small(k)
        t = recip(c, b, t)
        return c, t

    def to_features(src, gcol, dst_h, dst_l, ready, kcs, src_ok, dst_ok, ranges=None):
        for k2 in range(0, kcs, 2):
            bi, b, fr = bank()
            last = None
            for j in range(2):
                for tb in range(2):
                    last = tr(b[:, j * 256 + tb * 128:j * 256 + tb * 128 + 128],
                              src[:, tb, (k2 + j) * 128:(k2 + j + 1) * 128], fr, src_ok(k2 + j, tb),
                              sig=(j == 1 and tb == 1))
                    fr = []
            if gcol is None:
                th = act(dst_h[:, k2:k2 + 2, :], v3(b, 256), ACT.Copy, last, dst_ok)
                tl = tt(dst_l[:, k2:k2 + 2, :], v3(b, 256), dst_h[:, k2:k2 + 2, :].bitcast(F), ALU.subtract, th, dst_ok)
                ready[k2] = ready[k2 + 1] = [th, tl]
            else:
                t0 = act(dst_h[:, k2, :], b[:, 0:256], ACT.Copy, last, dst_ok, scale=gcol(k2))
                t1 = act(dst_h[:, k2 + 1, :], b[:, 256:512], ACT.Copy, scale=gcol(k2 + 1))
                l0 = stt(dst_l[:, k2, :], b[:, 0:256], gcol(k2), dst_h[:, k2, :].bitcast(F), ALU.mult, ALU.subtract,
                         t1, dst_ok)
                tl = stt(dst_l[:, k2 + 1, :], b[:, 256:512], gcol(k2 + 1), dst_h[:, k2 + 1, :].bitcast(F), ALU.mult,
                         ALU.subtract)
                ready[k2] = [t0, l0]
                ready[k2 + 1] = [t1, tl]
            mfree[bi] = [tl]

    def square_sums(x, junk, ok, junk_ok, n=2048):
        ssq = small(2)
        T["junkB"] = t = [square(junk[:, 0:n], x[:, tb, :], ssq[:, tb:tb + 1], ok[tb], junk_ok) for tb in range(2)]
        return ssq, t

    def prenorm(x, h, junk, gcol, key, ok, h_ok, junk_ok, dst_h=None, dst_l=None, dst_ok=None, scaled_by=None):
        dst_h = xth if dst_h is None else dst_h
        dst_l = xtl if dst_l is None else dst_l
        ssq, t = square_sums(x, junk, ok, junk_ok)
        r, t = rstd_of(ssq, D, EPS, t)
        th = [ts(h[:, tb, :], x[:, tb, :], r[:, tb:tb + 1], ALU.mult, None, None, t, h_ok, ok[tb]) for tb in range(2)]
        T[key] = {}
        to_features(h, gcol, dst_h, dst_l, T[key], KC, lambda k, tb: th[tb], dst_ok)
        return th

    def tok_store(y, part, i, tag, y_ok, add=False, junk=None, junk_ok=None):
        def evac(p, done):
            ts_ = []
            T.setdefault(tag, [])
            for tb in range(2):
                o = y[:, tb, i * 512:(i + 1) * 512]
                if add:
                    t = tt(o, p[tb], o, ALU.add, done, T.get("y0", []))
                else:
                    t = vcopy(o, p[tb], done, y_ok())
                ts_.append(t)
                if part is not None:
                    T[tag].append(square(junk, o, part[:, tb * 4 + i:tb * 4 + i + 1], t, junk_ok and junk_ok()))
            T["y0" if part is None else "yy"] = ts_
            return ts_
        return evac

    def postnorm(y, part, x, gb, tag, x_ok, gb_ok):
        ssq = small(2)
        t = reduce(ssq, v3(part, 4), ALU.add, T[tag])
        r, t = rstd_of(ssq, D, EPS, t)
        out = []
        for tb in range(2):
            a = stt(y[:, tb, :], y[:, tb, :], r[:, tb:tb + 1], gb, ALU.mult, ALU.mult, t, gb_ok)
            out.append(tt(x[:, tb, :], x[:, tb, :], y[:, tb, :], ALU.add, a, x_ok))
        return out

    def on_all(vec):
        return vec.partition_broadcast(128)

    t_cst = load("pool", cst, cst_d)
    t_ones = vset(ones, 1.0)
    x_ap = at(DD, [128, 2, D])
    x_src = I["x"][0].rearrange("(b p) d -> p b d", p=128)
    t_x = [load("act", x_ap[:, tb, :], x_src[:, tb, :]) for tb in range(2)]

    vraw = at(B, [128, 6 * 128])
    tv = []

    t_vz = vset(vraw, 0.0)
    tv.append(t_vz)

    def vec_rows(tile, r0, src, n):
        tv.append(load("pool", vraw[r0:r0 + n, tile * 128:(tile + 1) * 128], src.rearrange("(r p) -> r p", p=128), t_vz))

    vec_rows(0, 0, I["pre_norm_mix"][0], 16)
    vec_rows(0, 16, I["gla_b_gate"][0], 8)
    vec_rows(0, 24, I["gla_norm_g"][0], 4)
    vec_rows(0, 28, I["pre_norm_xa"][0], 16)
    vec_rows(0, 44, I["mem_norm_g"][0], 16)
    vec_rows(0, 60, I["pre_norm_ffn"][0], 16)
    vec_rows(0, 76, I["ssd_norm_w_2"][0], 8)
    vec_rows(0, 84, I["conv_b_2"][0], 16)
    vec_rows(1, 0, I["ffn_conv_b"][0], 88)
    for j in range(3):
        vec_rows(2 + j, 0, I["ffn_conv_w"][0][j], 88)
    for j in range(4):
        vec_rows(5, 16 * j, I["conv_w_2"][0][j], 16)
    sgb8 = at(B + 4, [1, 1024])
    t_sgb = load("pool", sgb8, I["sg_b"][0].rearrange("(o g) t -> o (g t)", o=1))
    t_dtb = load("pool", dtb, on_all(I["dt_bias_2"][0]))
    t_alog = load("pool", alog, on_all(I["a_log_2"][0]))
    t_dsk = load("pool", dsk, on_all(I["d_skip_2"][0]))

    h_ap = at(G, [128, 2, D])
    junk0 = at(M, [128, D])
    bi, b, fr = bank()
    tl = None
    for i in range(4):
        tl = tr(b[:, i * 128:(i + 1) * 128], vraw[:, i * 128:(i + 1) * 128], tv, t_cst, sig=(i == 3))
    t_vt = vcopy(VT[:, 0:512], b, tl)
    mfree[bi] = [t_vt]
    bi, b, fr = bank()
    for i in range(2):
        tl = tr(b[:, i * 128:(i + 1) * 128], vraw[:, (4 + i) * 128:(5 + i) * 128], tv, sig=(i == 1))
    t_vt2 = vcopy(VT[:, 512:768], b[:, 0:256], tl)
    mfree[bi] = [t_vt2]

    def gcols(c0):
        return lambda k: VT[:, c0 + k:c0 + k + 1]

    prenorm(x_ap, h_ap, junk0, gcols(0), "h1", t_x, None, None, dst_ok=[t_vt, t_vt2])

    h1 = lambda k: T["h1"][k]
    w_in = I["w_in"][0]

    def reader(key):
        return lambda k: T[key][k]

    vs = at(A, [128, 2, 1024])
    uT = at(A + 8, [128, 8, 256])
    sgw = at(B, [128, 8, 128])
    sgr = at(C + 16, [128, 8, 128])
    swT = at(G + 8, [128, 8, 128])
    lng = at(G, [128, 1024])
    lnb = at(G + 4, [128, 1024])
    yaTh = at(C, [128, 8, 256], R)
    yaTl = at(C + 8, [128, 8, 256], R)
    yaf = [at(DD + 2 * i, [128, 512]) for i in range(2)]

    def evac_vs(i):
        def f(p, done):
            r = [act(vs[:, tb, i * 512:(i + 1) * 512], p[tb], ACT.Gelu, done) for tb in range(2)]
            T["vs%d" % i] = r
            return r
        return f

    def evac_u(i):
        def f(p, done):
            r = [act(uT[:, 4 * i + 2 * b_:4 * i + 2 * b_ + 2, :], v3(p[b_], 256), ACT.Gelu, done) for b_ in range(2)]
            T["u%d" % i] = r
            return r
        return f

    for i in range(2):
        group("vs%d" % i, w_in, KC, [(1024 + 512 * i, 512)], "tok", xth, xtl, h1, evac_vs(i))
    for i in range(2):
        group("u%d" % i, w_in, KC, [(512 * i, 512)], "feat", xth, xtl, h1, evac_u(i))

    def sg_loads():
        T["lng"] = load("pool", lng, on_all(I["sg_ln_g"][0]), T["pe:vs0"])
        T["lnb"] = load("pool", lnb, on_all(I["sg_ln_b"][0]), T["pe:vs0"])
        T["sgr"] = load("pool", sgr, I["sg_w"][0].rearrange("g t s -> t g s"))
    hook("vs1", 0, sg_loads)

    def sg_turn():
        for g0 in (0, 4):
            bi, b, fr = bank()
            for g in range(4):
                tl = tr(b[:, g * 128:(g + 1) * 128], sgr[:, g0 + g, :], fr, T["sgr"], sig=(g == 3))
                fr = []
            t = tt(swT[:, g0:g0 + 4, :], v3(b, 128), bc(triu.unsqueeze(1), [128, 4, 128]), ALU.mult, tl, T["pe:vs0"])
            mfree[bi] = [t]
            T["swT%d" % (g0 // 4)] = t
    hook("vs1", 3, sg_turn)

    def sg_norm():
        stats = at(DD + 4, [128, 2, 12])
        for tb in range(2):
            tt_ = []
            for i in range(2):
                o = stats[:, tb, 6 * i:6 * i + 6]
                a_ = vs[:, tb, i * 512:(i + 1) * 512]
                tt_.append(put("dve", lambda e, o=o, a_=a_: e.bn_stats(o, a_), [T["vs0"], T["vs1"]]))
            mv = small(2)
            s3 = stats[:, tb, :]
            t = put("dve", lambda e, mv=mv, s3=s3: e.bn_aggr(mv, s3), [tt_])
            r, t2 = rstd_of(mv[:, 1:2], 1.0, EPS, t)
            t3 = ts(vs[:, tb, :], vs[:, tb, :], mv[:, 0:1], ALU.subtract, r, ALU.mult, t2)
            t4 = tt(vs[:, tb, :], vs[:, tb, :], lng, ALU.mult, t3, T["lng"])
            T["vsn%d" % tb] = tt(vs[:, tb, :], vs[:, tb, :], lnb, ALU.add, t4, T["lnb"])
    hook("u0", 1, sg_norm)

    def sg_mix():
        T["yaT"] = {}
        for g0 in range(0, 8, 2):
            bi, b, fr = bank()
            for j in range(2):
                for n in range(2):
                    o = b[:, j * 256 + n * 128:j * 256 + n * 128 + 128]
                    g = g0 + j
                    mm(o, vs[:, n, g * 128:(g + 1) * 128], swT[:, g, :], True, False, fr,
                       T["vsn0"], T["vsn1"], T["swT0"], T["swT1"])
                    fr = []
                    tl = mm(o, ones[0:1, :], sgb8[0:1, g * 128:(g + 1) * 128], False, True, t_ones, t_sgb,
                            sig=(j == 1 and n == 1))
            i = (g0 // 2) % 2
            t = tt(yaf[i], b, uT[:, g0:g0 + 2, :].rearrange("p a b -> p (a b)"), ALU.mult, tl, T["u0"], T["u1"],
                   T.get("yaf%d" % i))
            mfree[bi] = [t]
            th = act(yaTh[:, g0:g0 + 2, :], v3(yaf[i], 256), ACT.Copy, t)
            T["yaf%d" % i] = tl_ = tt(yaTl[:, g0:g0 + 2, :], v3(yaf[i], 256), yaTh[:, g0:g0 + 2, :].bitcast(F),
                                      ALU.subtract, th)
            T["yaT"][g0] = T["yaT"][g0 + 1] = [th, tl_]
    hook("ma0", 2, sg_mix)

    sig_a = at(M, [128, KC, 256])

    def evac_sig(dst, i, tag, ok):
        def f(p, done):
            r = [act(dst[:, 4 * i + 2 * b_:4 * i + 2 * b_ + 2, :], v3(p[b_], 256), ACT.Sigmoid, done, ok())
                 for b_ in range(2)]
            T[tag + str(i)] = r
            return r
        return f

    for i in range(4):
        group("ma%d" % i, w_in, KC, [(8208 + 512 * i, 512)], "feat", xth, xtl, h1,
              evac_sig(sig_a, i, "sa", lambda: None))

    def evac_pa(i):
        def f(p, done):
            r = []
            for b_ in range(2):
                o = sig_a[:, 4 * i + 2 * b_:4 * i + 2 * b_ + 2, :]
                r.append(tt(o, v3(p[b_], 256), o, ALU.mult, done, T["sa%d" % i]))
            T["ma_%d" % i] = r
            return r
        return f

    for i in range(4):
        group("pa%d" % i, I["w_proj_a"][0], 8, [(512 * i, 512)], "feat", yaTh, yaTl, reader("yaT"), evac_pa(i))

    qT = at(A, [128, 8, 256])
    kT = at(A + 8, [128, 8, 256])
    bT = at(B, [128, 8, 256])
    E = at(C, [128, 8, 640])
    tmpG = at(G, [128, 2048])
    wg2 = at(G + 8, [16, 1024])
    v_t = at(DD, [128, 2, D])
    og = at(G, [128, 2, D])
    AT = at(A + 8, [128, 4, 512])
    o_t = at(C, [128, 2, D])
    ybTh = at(A, [128, KC, 256], R)
    ybTl = at(G, [128, KC, 256], R)
    EO = [0, 64, 192, 384]

    def evac_glr(p, done):
        t = [vcopy(glr[:, 16 * tb:16 * tb + 16], p[tb][:, 0:16], done) for tb in range(2)]
        T["glr"] = t
        T["wg2"] = load("pool", wg2, I["gla_w_gate2"][0], T["swT0"], T["swT1"], T["pe:ma1"])
        return t

    group("glr", w_in, KC, [(8192, 16)], "tok", xth, xtl, h1, evac_glr, chunk=16)

    def gate1():
        bi, b, fr = bank()
        for tb in range(2):
            tl = tr(b[0:16, tb * 128:(tb + 1) * 128], glr[:, 16 * tb:16 * tb + 16], fr, T["glr"], sig=(tb == 1))
        T["glrT"] = vcopy(glrT, b[0:16, 0:256], tl)
        mfree[bi] = [T["glrT"]]
    hook("q0", 0, gate1)

    def gate2():
        T["y"] = []
        for d2 in range(0, 8, 2):
            bi, b, fr = bank()
            for j in range(2):
                tl = mm(b[:, 256 * j:256 * j + 256], wg2[0:16, (d2 + j) * 128:(d2 + j + 1) * 128], glrT, True, True,
                        fr, T["glrT"], T["wg2"], sig=(j == 1))
                fr = []
            for j in range(2):
                t = ts(bT[:, d2 + j, :], b[:, 256 * j:256 * j + 256], VT[:, 16 + d2 + j:17 + d2 + j], ALU.add, None,
                       None, tl, T["pe:ma1"], t_vt)
            T["y"].append(t)
            mfree[bi] = [t]
        b2 = bT.rearrange("p a b -> p (a b)")
        t = act(tmpG, b2, ACT.Abs, T["y"], T["pe:pa0"])
        t = act(tmpG, tmpG, ACT.Exp, t, scale=-1.0)
        t = act(tmpG, tmpG, ACT.Ln, t, bias=1.0)
        t = stt(b2, b2, 0.0, tmpG, ALU.min, ALU.subtract, t)
        T["tmpG"] = t
        T["la"] = ts(b2, b2, 1.0 / 16.0, ALU.mult, -1.0, ALU.max, t)
    hook("q0", 2, gate2)

    def gate3():
        tb_ = []
        for d in range(8):
            o, i_ = tmpG[:, d * 256:(d + 1) * 256], bT[:, d, :]
            tb_.append(put("dve", lambda e, o=o, i_=i_: e.tensor_tensor_scan(o, scan1, i_, 0.0, ALU.mult, ALU.add),
                           [T["la"], t_cst]))
        b3 = v3(tmpG, 256)
        T["b"] = tb_
        prev = None
        for i in range(4):
            own = ts(E[:, :, EO[i] + 64 * i:EO[i] + 64 * i + 64], b3[:, :, 64 * i:64 * i + 64], -1.0, ALU.mult, None, None,
                     tb_, T["pe:pa3"])
            if i:
                last = b3[:, :, 64 * i - 1:64 * i]
                prev = tt(E[:, :, EO[i]:EO[i] + 64 * i], E[:, :, EO[i - 1]:EO[i - 1] + 64 * i],
                          bc(last, [128, 8, 64 * i]), ALU.add, prev)
                prev = [prev, own]
            else:
                prev = own
        Ef = E.rearrange("p a b -> p (a b)")
        T["E"] = act(Ef, Ef, ACT.Exp, prev)
        T["eb"] = act(bT.rearrange("p a b -> p (a b)"), tmpG, ACT.Exp, tb_, prev)
    hook("q1", 1, gate3)

    def evac_q(i):
        def f(p, done):
            r = [vcopy(qT[:, 4 * i + 2 * b_:4 * i + 2 * b_ + 2, :], v3(p[b_], 256), done, T["pe:pa3"])
                 for b_ in range(2)]
            T["q%d" % i] = r
            return r
        return f

    def evac_k(i):
        def f(p, done):
            r = [vcopy(kT[:, 4 * i + 2 * b_:4 * i + 2 * b_ + 2, :], v3(p[b_], 256), done) for b_ in range(2)]
            T["k%d" % i] = r
            return r
        return f

    for i in range(2):
        group("q%d" % i, w_in, KC, [(2048 + 512 * i, 512)], "feat", xth, xtl, h1, evac_q(i))
    for i in range(2):
        group("k%d" % i, w_in, KC, [(3072 + 512 * i, 512)], "feat", xth, xtl, h1, evac_k(i))

    def gate_q():
        q2 = qT.rearrange("p a b -> p (a b)")
        T["qs"] = stt(q2, q2, 1.0 / 16.0, bT.rearrange("p a b -> p (a b)"), ALU.mult, ALU.mult, T["eb"], T["q0"], T["q1"])
    hook("k0", 1, gate_q)

    def gate_k():
        T["ks"] = [tt(E[:, :, EO[i]:EO[i] + 64 * (i + 1)], E[:, :, EO[i]:EO[i] + 64 * (i + 1)],
                      kT[:, :, 0:64 * (i + 1)], ALU.mult, T["E"], T["k0"], T["k1"]) for i in range(4)]
        T["ATz"] = vset(AT[:, :, :], 0.0, T["ks"])
    hook("v0", 1, gate_k)

    def gla_scores(hs):
        def f():
            for h in hs:
                bi, b, fr = bank()
                tl = None
                for i in range(4):
                    for sb in range((i // 2) + 1):
                        rows_ = min(64 * (i + 1) - 128 * sb, 128)
                        o = b[0:rows_, 256 * sb + 64 * (i - 2 * sb):256 * sb + 64 * (i - 2 * sb) + 64]
                        for d in range(2):
                            e0 = EO[i] + 128 * sb
                            tl = mm(o, E[:, 2 * h + d, e0:e0 + rows_], qT[:, 2 * h + d, 64 * i:64 * i + 64], d == 0, d == 1,
                                    fr, T["ks"], T["qs"], sig=(i == 3 and sb == 1 and d == 1))
                            fr = []
                bv, av = v3(b, 256), v3(AT[:, h, :], 256)
                t1 = tt(av[0:64, :, 0:64], bv[0:64, :, 0:64], bc(triu[0:64, 0:64].unsqueeze(1), [64, 2, 64]), ALU.mult,
                        tl, T["ATz"])
                t2 = tt(av[:, :, 64:128], bv[:, :, 64:128], bc(triu[:, 64:128].unsqueeze(1), [128, 2, 64]), ALU.mult)
                t3 = vcopy(AT[:, h, 128:256], b[:, 128:256])
                mfree[bi] = [t3]
                T["AT%d" % h] = [t1, t2, t3]
        return f
    hook("v1", 2, gla_scores([0, 1]))
    hook("v2", 0, gla_scores([2, 3]))

    def evac_v(i):
        def f(p, done):
            r = [vcopy(v_t[:, tb, 512 * i:512 * i + 512], p[tb], done, T["yaT"][6]) for tb in range(2)]
            T["v%d" % i] = r
            return r
        return f

    for i in range(4):
        group("v%d" % i, w_in, KC, [(4096 + 512 * i, 512)], "tok", xth, xtl, h1, evac_v(i))

    ossq = small(8)

    def gla_out(h):
        def f():
            for cb in range(2):
                bi, b, fr = bank()
                mm(b, AT[:, h, 128 * cb:128 * cb + 128], v_t[:, 0, 512 * h:512 * h + 512], True, cb == 0, fr,
                   T["AT%d" % h], T["v%d" % h], sig=False)
                if cb == 1:
                    tl = mm(b, AT[:, h, 256:384], v_t[:, 1, 512 * h:512 * h + 512], False, True, sig=True)
                else:
                    queue["pe"][-1] = (queue["pe"][-1][0], queue["pe"][-1][1], True)
                    count["pe"] += 1
                    tl = (sem["pe"], count["pe"])
                o = o_t[:, cb, 512 * h:512 * h + 512]
                allks = [T["AT%d" % j] for j in range(4)]
                t = vcopy(o, b, tl, *allks)
                mfree[bi] = [t]
                j = cb * 4 + h
                T["o%d%d" % (cb, h)] = square(junk_o, o, ossq[:, j:j + 1], t, T["junk_ok"])
            T["go%d" % h] = tl
        return f
    junk_o = at(B + 4, [128, 512])

    def set_junk():
        T["junk_ok"] = T["qs"]
    hook("og0", 0, set_junk)
    for h in range(4):
        hook("og0", h, gla_out(h))

    def evac_og(i):
        def f(p, done):
            r = [act(og[:, tb, 512 * i:512 * i + 512], p[tb], ACT.Silu, done, T["b"], T["E"], T["eb"], T["y"]) for tb in range(2)]
            T["og%d" % i] = r
            return r
        return f

    for i in range(4):
        group("og%d" % i, w_in, KC, [(6144 + 512 * i, 512)], "tok", xth, xtl, h1, evac_og(i))

    def gla_rstd():
        T["or"], T["orok"] = rstd_of(ossq, 512, EPS, [T["o%d%d" % (c, h)] for c in range(2) for h in range(4)])
    hook("og1", 0, gla_rstd)

    def gla_gate(h):
        def f():
            for cb in range(2):
                j = cb * 4 + h
                o = o_t[:, cb, 512 * h:512 * h + 512]
                T["yb%d%d" % (cb, h)] = stt(o, o, T["or"][:, j:j + 1], og[:, cb, 512 * h:512 * h + 512], ALU.mult,
                                            ALU.mult, T["orok"], T["og%d" % h])
        return f
    hook("og1", 2, gla_gate(0))
    hook("og2", 2, gla_gate(1))
    hook("og3", 2, gla_gate(2))
    hook("mb0", 1, gla_gate(3))

    def gla_turn():
        T["ybT"] = {}
        to_features(o_t, lambda k: VT[:, 24 + k % 4:25 + k % 4], ybTh, ybTl, T["ybT"], KC,
                    lambda k, tb: T["yb%d%d" % (tb, k // 4)],
                    [T["yb%d3" % cb] for cb in range(2)] + [T["go3"]])
    hook("mb0", 3, gla_turn)

    sig_b = at(DD, [128, KC, 256])
    for i in range(4):
        group("mb%d" % i, w_in, KC, [(10256 + 512 * i, 512)], "feat", xth, xtl, h1,
              evac_sig(sig_b, i, "sb", lambda: T["go3"]))

    mt = [at(B + 2 * i, [128, 512]) for i in range(2)]
    T["mg"] = {}

    def evac_pb(i):
        def f(p, done):
            r = []
            for b_ in range(2):
                c = slice(4 * i + 2 * b_, 4 * i + 2 * b_ + 2)
                m_ = v3(mt[b_], 256)
                t = tt(m_, v3(p[b_], 256), sig_b[:, c, :], ALU.mult, done, T["sb%d" % i], T.get("mt%d" % b_), T["qs"])
                r.append(t)
                t = tt(m_, m_, sig_a[:, c, :], ALU.add, t, T["ma_%d" % i])
                th = act(xth[:, c, :], m_, ACT.Copy, t, T["pe:mb3"])
                tl_ = tt(xtl[:, c, :], m_, xth[:, c, :].bitcast(F), ALU.subtract, th, T["pe:mb3"])
                T["mt%d" % b_] = tl_
                T["mg"][4 * i + 2 * b_] = T["mg"][4 * i + 2 * b_ + 1] = [th, tl_]
            return r
        return f

    for i in range(4):
        group("pb%d" % i, I["w_proj_b"][0], KC, [(512 * i, 512)], "feat", ybTh, ybTl, reader("ybT"), evac_pb(i))

    xx = at(C, [128, 2, D])
    memTh = at(M, [128, KC, 256], R)
    memTl = at(DD, [128, KC, 256], R)
    junkB = at(B, [128, D])
    junk_wo = at(B + 4, [128, 512])
    junk_xo = at(A + 4, [128, 512])
    junk_dn = at(C + 16, [128, 512])

    def mem_load():
        s = I["mem"][0].rearrange("(b p) d -> p b d", p=128)
        ok = [T["pe:pb0"], T["ybT"][15]]
        T["mem"] = [load("pool", xx[:, tb, :], s[:, tb, :], *ok) for tb in range(2)]
    hook("pb1", 0, mem_load)

    def mem_norm():
        prenorm(xx, xx, junkB, gcols(44), "memT", T["mem"], None,
                [T["mt0"], T["mt1"]], memTh, memTl, [T["mt0"], T["mt1"]])
        s = I["x"][0].rearrange("(b p) d -> p b d", p=128)
        T["x"] = [load("pool", xx[:, tb, :], s[:, tb, :], T["memT"][15]) for tb in range(2)]
        T["gb1"] = load("pool", gb, on_all(I["post_norm_mix"][0]), T["pe:pb3"])
    hook("wo0", 1, mem_norm)

    gb = at(G, [128, D])
    yA = at(A, [128, 2, D])
    part1 = small(8)
    for i in range(4):
        group("wo%d" % i, I["w_out"][0], KC, [(512 * i, 512)], "tok", xth, xtl, reader("mg"),
              tok_store(yA, part1, i, "sq1", lambda: T["pe:pb3"], junk=junk_wo, junk_ok=lambda: T.get("junkB")))

    kxT = at(G + 8, [128, 4, 256])
    vx = at(G + 12, [128, 2, 512])
    qxT = at(A, [128, 4, 256])
    px = at(A + 4, [128, 8, 256])
    pxT = at(B, [128, 8, 256])
    oxh = at(A + 12, [128, 4, 256], R)
    oxl = at(C + 16, [128, 4, 256], R)

    def norm1():
        t = postnorm(yA, part1, xx, gb, "sq1", T["x"], T["gb1"])
        T["x1"] = t
        prenorm(xx, yA, junkB, gcols(28), "h2", t, t, None, dst_ok=T["pe:wo3"])

    def evac_kx(p, done):
        r = [vcopy(kxT[:, 2 * b_:2 * b_ + 2, :], v3(p[b_], 256), done, T["pe:pb3"]) for b_ in range(2)]
        T["kx"] = r
        return r

    def evac_vx(p, done):
        r = [vcopy(vx[:, tb, :], p[tb], done, T["pe:pb3"]) for tb in range(2)]
        T["vx"] = r
        return r

    def evac_qx(p, done):
        r = [vcopy(qxT[:, 2 * b_:2 * b_ + 2, :], v3(p[b_], 256), done, T["h2"][15]) for b_ in range(2)]
        T["qx"] = r
        return r

    group("xk", I["xa_wk"][0], KC, [(0, 512)], "feat", memTh, memTl, reader("memT"), evac_kx)
    hook("xk", 0, norm1)
    group("xq", I["xa_wq"][0], KC, [(0, 512)], "feat", xth, xtl, reader("h2"), evac_qx)
    group("xv", I["xa_wv"][0], KC, [(0, 512)], "tok", memTh, memTl, reader("memT"), evac_vx)

    XS = 128.0 ** -0.5
    mxx, nmx, sx, rx = small(8), small(8), small(8), small(8)

    def xa_scores():
        tx = []
        for h in range(4):
            bi, b, fr = bank()
            for tb in range(2):
                tl = mm(b[:, 256 * tb:256 * tb + 256], qxT[:, h, 128 * tb:128 * tb + 128], kxT[:, h, :], True, True,
                        fr, T["qx"], T["kx"], sig=(tb == 1))
                fr = []
            t = reduce(mxx[:, 2 * h:2 * h + 2], v3(b, 256), ALU.max, tl)
            t = ts(nmx[:, 2 * h:2 * h + 2], mxx[:, 2 * h:2 * h + 2], -XS, ALU.mult, None, None, t)
            for tb in range(2):
                j = 2 * h + tb
                t2 = act(px[:, j, :], b[:, 256 * tb:256 * tb + 256], ACT.Exp, t, T["h2"][15], bias=nmx[:, j:j + 1],
                         scale=XS, accum=sx[:, j:j + 1])
            mfree[bi] = [t2]
            tx.append(t2)
        t = recip(rx, sx, tx)
        T["px"] = tt(px, px, bc(rx.unsqueeze(2), [128, 8, 256]), ALU.mult, t)
    hook("xv", 1, xa_scores)

    def xa_turn():
        T["pxT"] = []
        for h in range(4):
            bi, b, fr = bank()
            for mc in range(2):
                for tb in range(2):
                    tl = tr(b[:, 256 * mc + 128 * tb:256 * mc + 128 * tb + 128], px[:, 2 * h + tb, 128 * mc:128 * mc + 128],
                            fr, T["px"], sig=(mc == 1 and tb == 1))
                    fr = []
            t = vcopy(pxT[:, 2 * h:2 * h + 2, :], v3(b, 256), tl, T["h2"][15])
            mfree[bi] = [t]
            T["pxT"].append(t)
    hook("xv", 3, xa_turn)
    T["oxT"] = {}

    def xa_out():
        for h2 in range(0, 4, 2):
            bi, b, fr = bank()
            for j in range(2):
                for mc in range(2):
                    tl = mm(b[:, 256 * j:256 * j + 256], vx[:, mc, (h2 + j) * 128:(h2 + j + 1) * 128],
                            pxT[:, 2 * (h2 + j) + mc, :], mc == 0, mc == 1, fr, T["pxT"], T["vx"],
                            sig=(j == 1 and mc == 1))
                    fr = []
            th = act(oxh[:, h2:h2 + 2, :], v3(b, 256), ACT.Copy, tl)
            tl_ = tt(oxl[:, h2:h2 + 2, :], v3(b, 256), oxh[:, h2:h2 + 2, :].bitcast(F), ALU.subtract, th)
            mfree[bi] = [tl_]
            T["oxT"][h2] = T["oxT"][h2 + 1] = [th, tl_]
    hook("xo0", 0, xa_out)

    yM = at(M, [128, 2, D])
    part2 = small(8)
    for i in range(4):
        group("xo%d" % i, I["xa_wo"][0], 4, [(512 * i, 512)], "tok", oxh, oxl, reader("oxT"),
              tok_store(yM, part2, i, "sq2", lambda: T["pe:xv"], junk=junk_xo, junk_ok=lambda: T["pxT"]))

    def gb2_load():
        T["gb2"] = load("pool", gb, on_all(I["post_norm_xa"][0]), T["x1"])
    hook("xq", 0, gb2_load)

    HF = FF // 256
    ach = at(G, [128, HF, 256], R)
    acl = at(G + 22, [128, HF, 256], R)
    cvt = [at(B + 4 * s, [128, 1024]) for s in range(2)]
    cv = [[cvt[s][:, 256 * j:256 * j + 256] for j in range(4)] for s in range(2)]
    gate_up = [[cvt[s][:, 512 * j:512 * j + 512] for j in range(2)] for s in range(2)]

    def norm2():
        t = postnorm(yM, part2, xx, gb, "sq2", T["x1"], T["gb2"])
        T["x2"] = t
        prenorm(xx, yA2, junkB, gcols(60), "h3", t, [T["pe:xo3"]], [T["pe:xo0"]], dst_ok=T["pe:xq"])
    yA2 = at(A, [128, 2, D])
    T["acT"] = {}
    ngr = [0]

    def evac_up(half, i):
        def f(p, done):
            s = ngr[0] % 2
            ngr[0] += 1
            c = cv[s]
            cols = [half * HF + 2 * i, half * HF + 2 * i + 1, 44 + half * HF + 2 * i, 44 + half * HF + 2 * i + 1]
            ok = [T.get("cv%d" % s), T["h3"][15], t_vt2]
            r = []
            for b_ in range(2):
                for j in range(2):
                    q = 2 * b_ + j
                    t = act(c[q], p[b_][:, 256 * j:256 * j + 256], ACT.Identity, done, ok,
                            bias=VT[:, 128 + cols[q]:129 + cols[q]], scale=VT[:, 512 + cols[q]:513 + cols[q]])
                for j in range(2):
                    q = 2 * b_ + j
                    t1 = stt(c[q][:, 1:256], p[b_][:, 256 * j:256 * j + 255], VT[:, 384 + cols[q]:385 + cols[q]],
                             c[q][:, 1:256], ALU.mult, ALU.add, t)
                    t2 = stt(c[q][:, 2:256], p[b_][:, 256 * j:256 * j + 254], VT[:, 256 + cols[q]:257 + cols[q]],
                             c[q][:, 2:256], ALU.mult, ALU.add, t1)
                r.append(t2)
            cg = gate_up[s][0]
            cu = gate_up[s][1]
            t = act(cg, cg, ACT.Gelu_apprx_tanh, r[0])
            t = tt(cu, cg, cu, ALU.mult, t, r[1])
            k = slice(2 * i, 2 * i + 2)
            wok = [T["pe:xo3"], T["x2"]] if half == 0 else [T["pe:dn03"]]
            th = act(ach[:, k, :], v3(cu, 256), ACT.Copy, t, wok)
            tl_ = tt(acl[:, k, :], v3(cu, 256), ach[:, k, :].bitcast(F), ALU.subtract, th, wok)
            T["cv%d" % s] = tl_
            T["acT"][(half, 2 * i)] = T["acT"][(half, 2 * i + 1)] = [th, tl_]
            return r
        return f

    part3 = small(8)
    for half in range(2):
        for i in range(HF // 2):
            c0 = half * HF * 128 + 256 * i
            group("up%d_%d" % (half, i), I["ffn_w_up"][0], KC, [(c0, 256), (FF + c0, 256)], "feat", xth, xtl,
                  reader("h3"), evac_up(half, i))
        for i in range(4):
            group("dn%d%d" % (half, i), I["ffn_w_down"][0], HF, [(512 * i, 512)], "tok", ach, acl,
                  (lambda half: lambda k: T["acT"][(half, k)])(half),
                  tok_store(yA2, part3 if half else None, i, "sq3", lambda: T["h3"][15], add=bool(half),
                            junk=junk_dn, junk_ok=lambda: T["pe:xo3"]),
                  k_off=half * HF)
    hook("up0_0", 0, norm2)

    gb3 = at(B, [128, D])

    def gb3_load():
        T["gb3"] = load("pool", gb3, on_all(I["post_norm_ffn"][0]), T["cv0"], T["cv1"])
    hook("dn10", 1, gb3_load)

    w2 = I["w_in_2"][0]

    def norm3():
        t = postnorm(yA2, part3, xx, gb3, "sq3", T["x2"], T["gb3"])
        T["x3"] = t
        T["h4"] = {}
        to_features(xx, None, xth, xtl, T["h4"], KC, lambda k, tb: t[tb], T["pe:up1_10"])

    h4 = reader("h4")
    qi = at(A, [128, 2, 1024])
    qiT = at(A + 8, [128, 8, 256])
    kv = at(B, [128, 2, 512])
    kaT = at(B + 4, [128, 2, 256])
    score = at(B + 6, [128, 2, 256])
    amask = at(C + 16, [128, 2, 256])
    rt = [at(C + 18 + 0.5 * i, [128, 128]) for i in range(4)]
    ki2 = at(G, [128, 2, 128])
    kiT = at(G + 1, [128, 256])
    rl = [at(G + 2 + 2 * i, [128, 512]) for i in range(2)]
    top8 = at(G + 6, [128, 8])
    expa = at(G + 6.5, [128, 16])

    def rope(x3_, half, tb, col_c, col_s, n, ok):
        a, b = x3_[:, :, 0:half], x3_[:, :, half:2 * half]
        cs = bc(cst[:, col_c + tb * half:col_c + (tb + 1) * half].unsqueeze(1), [128, n, half])
        sn = bc(cst[:, col_s + tb * half:col_s + (tb + 1) * half].unsqueeze(1), [128, n, half])
        r_ = [v3(rt[i][:, 0:n * half], half) for i in range(4)]
        t0 = tt(r_[0], a, cs, ALU.mult, ok, T.get("rope"))
        t1 = tt(r_[1], b, sn, ALU.mult)
        t2 = tt(r_[2], b, cs, ALU.mult)
        t3 = tt(r_[3], a, sn, ALU.mult)
        t4 = tt(a, r_[0], r_[1], ALU.subtract, t1, t3)
        T["rope"] = tt(b, r_[2], r_[3], ALU.add, t3)
        return [t4, T["rope"]]

    def evac_small(p, done):
        r = []
        for tb in range(2):
            t0 = vcopy(ki2[:, tb, 0:64], p[tb][:, 0:64], done)
            t1 = ts(widx[:, 16 * tb:16 * tb + 16], p[tb][:, 64:80], 1.0 / 32.0, ALU.mult, None, None)
            t2 = rope(ki2[:, tb:tb + 1, 0:64], 8, tb, C_CI, C_SI, 1, t0)
            T["ki%d" % tb] = vcopy(ki2[:, tb, 64:128], ki2[:, tb, 0:64], t2)
            r.append(t1)
        T["wi"] = r
        return r

    def evac_dt(p, done):
        t = [tt(dt_[:, 16 * tb:16 * tb + 16], p[tb][:, 0:16], dtb, ALU.add, done, t_dtb) for tb in range(2)]
        T["dtr"] = t
        return t

    group("kiw", w2, KC, [(3584, 80)], "tok", xth, xtl, h4, evac_small, chunk=16)
    hook("kiw", 0, norm3)
    group("dt", w2, KC, [(6736, 16)], "tok", xth, xtl, h4, evac_dt, chunk=16)

    def softplus():
        t = act(dtmp, dt_, ACT.Abs, T["dtr"])
        z = act(dtmp, dtmp, ACT.Exp, t, scale=-1.0)
        s_, w_, q_ = dl1, do1, dtm2
        t = ts(s_, dtmp, 2.0, ALU.add, None, None, z)
        t = recip(s_, s_, t)
        t = tt(s_, s_, dtmp, ALU.mult, t)
        t = tt(w_, s_, s_, ALU.mult, t)
        t = ts(q_, w_, 1.0 / 17.0, ALU.mult, None, None, t)
        for n in range(15, 1, -2):
            t = stt(q_, q_, 1.0 / n, w_, ALU.add, ALU.mult, t)
        t = stt(q_, q_, 1.0, s_, ALU.add, ALU.mult, t)
        d1 = q_
        t = ts(q_, q_, 2.0, ALU.mult, None, None, t)
        T["dt"] = t = stt(dt_, dt_, 0.0, d1, ALU.max, ALU.add, t)
        ta = act(expa, alog, ACT.Exp, t_alog)
        t = tt(v3(adt, 16), v3(dt_, 16), bc(expa.unsqueeze(1), [128, 2, 16]), ALU.mult, t, ta)
        T["adt"] = ts(adt, adt, -1.0, ALU.mult, None, None, t)
    hook("qi0", 0, softplus)

    def evac_qi(i):
        def f(p, done):
            r = []
            for tb in range(2):
                o = qi[:, tb, 512 * i:512 * i + 512]
                t = vcopy(o, p[tb], done, T["h4"][15])
                r.append(t)
                T["qi%d%d" % (i, tb)] = rope(v3(o, 64), 8, tb, C_CI, C_SI, 8, t)
            return r
        return f

    for i in range(2):
        group("qi%d" % i, w2, KC, [(2560 + 512 * i, 512)], "tok", xth, xtl, h4, evac_qi(i))

    def turn_ki():
        bi, b, fr = bank()
        for tb in range(2):
            tl = tr(b[:, tb * 128:tb * 128 + 128], ki2[:, tb, :], fr, T["ki0"], T["ki1"], sig=(tb == 1))
            fr = []
        T["kiT"] = vcopy(kiT, b[:, 0:256], tl)
        mfree[bi] = [T["kiT"]]
    hook("qi0", 2, turn_ki)

    def turn_qi(i):
        def f():
            for p2 in range(4 * i, 4 * i + 4, 2):
                bi, b, fr = bank()
                for j in range(2):
                    for tb in range(2):
                        tl = tr(b[:, 256 * j + 128 * tb:256 * j + 128 * tb + 128], qi[:, tb, (p2 + j) * 128:(p2 + j + 1) * 128],
                                fr, T["qi%d0" % i], T["qi%d1" % i], sig=(j == 1 and tb == 1))
                        fr = []
                t = vcopy(qiT[:, p2:p2 + 2, :], v3(b, 256), tl)
                mfree[bi] = [t]
                T["qiT%d" % p2] = T["qiT%d" % (p2 + 1)] = t
        return f
    hook("qi1", 1, turn_qi(0))
    hook("kv", 1, turn_qi(1))

    def index_scores(qb, q4):
        def f():
            nk = 128 * (qb + 1)
            bs = [bank(), bank()]
            tls = []
            for par in range(2):
                bi, b, fr = bs[par]
                for j in range(2):
                    h = 4 * q4 + 2 * j + par
                    p0 = 64 * par
                    tl = mm(b[:, 256 * j:256 * j + nk], qiT[p0:p0 + 64, h // 2, 128 * qb:128 * qb + 128],
                            kiT[p0:p0 + 64, 0:nk], True, True, fr, T["qiT%d" % (h // 2)], T["kiT"], sig=(j == 1))
                    fr = []
                tls.append(tl)
            for par in range(2):
                bi, b, fr = bs[par]
                r3 = v3(rl[par], 256)
                t = act(r3[:, :, 0:nk], v3(b, 256)[:, :, 0:nk], ACT.Relu, tls[par], T.get("rl%d" % par))
                mfree[bi] = [t]
                for j in range(2):
                    h = 4 * q4 + 2 * j + par
                    w_ = widx[:, 16 * qb + h:16 * qb + h + 1]
                    o = score[:, qb, 0:nk]
                    if h == 0:
                        t = ts(o, r3[:, j, 0:nk], w_, ALU.mult, None, None, t, T["wi"], T["h4"][15], T["x3"])
                    else:
                        t = stt(o, r3[:, j, 0:nk], w_, o, ALU.mult, ALU.add, t, T["sc%d" % qb])
                    T["sc%d" % qb] = t
                T["rl%d" % par] = t
        return f

    for n, (qb, q4) in enumerate([(0, 0), (0, 1), (0, 2), (0, 3), (1, 0), (1, 1), (1, 2), (1, 3)]):
        hook("kv" if n < 2 else "xb0" if n < 6 else "xb1", (n + 2) % 4, index_scores(qb, q4))

    def choose(qb, part):
        def f():
            nk = 128 * (qb + 1)
            s_ = score[:, qb, 0:nk]
            if part == 0:
                own = score[:, qb, 128 * qb:128 * qb + 128]
                T["w%d" % qb] = tt(own, own, m64, ALU.add, T["sc%d" % qb])
            t = T["w%d" % qb]
            for _ in range(4):
                t = put("dve", lambda e: e.max(top8, s_), [t])
                t = put("dve", lambda e: e.match_replace(s_, top8, s_, GONE), [t])
            if part == 1:
                am = amask[:, qb, 0:nk]
                t = ts(am, s_, -2.0e38, ALU.is_gt, -BIG, ALU.mult, t, T["rope"], T["sqdone"])
            T["w%d" % qb] = t
        return f
    hook("xb1", 2, choose(0, 0))
    hook("xb1", 3, choose(0, 1))
    hook("xb2", 0, choose(1, 0))
    hook("xb2", 1, choose(1, 1))

    def sqd():
        T["sqdone"] = T["sq3"][-1]
    hook("xb0", 0, sqd)

    def evac_kv(p, done):
        r = []
        for tb in range(2):
            t = vcopy(kv[:, tb, :], p[tb], done, T["x3"])
            r.append(t)
            T["kv%d" % tb] = rope(v3(kv[:, tb, 0:256], 128), 16, tb, C_CA, C_SA, 2, t) + [t]
        return r
    group("kv", w2, KC, [(1024, 512)], "tok", xth, xtl, h4, evac_kv)

    def turn_k():
        bi, b, fr = bank()
        for g in range(2):
            for tb in range(2):
                tl = tr(b[:, 256 * g + 128 * tb:256 * g + 128 * tb + 128], kv[:, tb, 128 * g:128 * g + 128], fr,
                        T["kv0"], T["kv1"], sig=(g == 1 and tb == 1))
                fr = []
        T["kaT"] = vcopy(kaT, v3(b, 256), tl)
        mfree[bi] = [T["kaT"]]
    hook("xb0", 1, turn_k)

    xb = at(M, [128, 16, 256])

    def evac_xb(i):
        def f(p, done):
            r = []
            for b_ in range(2):
                for j in range(2):
                    c = 4 * i + 2 * b_ + j
                    t = act(xb[:, c, :], p[b_][:, 256 * j:256 * j + 256], ACT.Identity, done, T["pe:dn13"],
                            bias=VT[:, 84 + c:85 + c], scale=VT[:, 640 + 48 + c:640 + 49 + c])
                for j in range(2):
                    c = 4 * i + 2 * b_ + j
                    for tap in range(1, 4):
                        wc = VT[:, 640 + 16 * (3 - tap) + c:640 + 16 * (3 - tap) + c + 1]
                        t = stt(xb[:, c, tap:256], p[b_][:, 256 * j:256 * j + 256 - tap], wc, xb[:, c, tap:256],
                                ALU.mult, ALU.add, t)
                r.append(t)
                c = 4 * i + 2 * b_
                T["xb%d" % c] = T["xb%d" % (c + 1)] = act(xb[:, c:c + 2, :], xb[:, c:c + 2, :], ACT.Silu, t)
            return r
        return f

    for i in range(4):
        group("xb%d" % i, w2, KC, [(4688 + 512 * i, 512)], "feat", xth, xtl, h4, evac_xb(i))

    xs = at(DD, [128, 2, 1024])
    xdt = at(DD + 8, [128, 2, 1024])
    cbm = at(M, [128, 4, 384])
    sr = at(M + 8, [128, 4, 384])
    Wm = at(G + 8, [128, 4, 384])
    zs = at(G, [128, 2, 1024])

    def turn_xs(i):
        def f():
            for c2 in range(4 * i, 4 * i + 4, 2):
                bi, b, fr = bank()
                for j in range(2):
                    for tb in range(2):
                        tl = tr(b[:, 256 * tb + 128 * j:256 * tb + 128 * j + 128], xb[:, c2 + j, 128 * tb:128 * tb + 128], fr,
                                T["xb%d" % c2], T["xb%d" % (c2 + 1)], sig=(j == 1 and tb == 1))
                        fr = []
                t = vcopy(xs[:, :, c2 * 128:c2 * 128 + 256], v3(b, 256), tl, T["pe:dn13"])
                mfree[bi] = [t]
                T["xsT%d" % c2] = tl
                T["xs%d" % (c2 // 2)] = t
        return f
    hook("xb1", 1, turn_xs(0))
    hook("xb2", 2, turn_xs(1))

    def ssd_inputs():
        for tb in range(2):
            d3 = bc(dt_[:, 16 * tb:16 * tb + 16].unsqueeze(2), [128, 16, 64])
            T["xdt%d" % tb] = tt(v3(xdt[:, tb, :], 64), v3(xs[:, tb, :], 64), d3, ALU.mult,
                                 [T["xs%d" % j] for j in range(4)], T["dt"])
            k3 = bc(dsk.unsqueeze(2), [128, 16, 64])
            T["ys%d" % tb] = tt(v3(xs[:, tb, :], 64), v3(xs[:, tb, :], 64), k3, ALU.mult, T["xdt%d" % tb], t_dsk)
    hook("xb3", 2, ssd_inputs)

    def ssd_cb():
        for g in range(4):
            bi, b, fr = bank()
            bT_, cT_ = xb[:, 8 + g, :], xb[:, 12 + g, :]
            w_ = [T["xb%d" % (8 + g)], T["xb%d" % (12 + g)]]
            mm(b[:, 0:256], bT_[:, 0:128], cT_, True, True, fr, w_)
            tl = mm(b[:, 256:384], bT_[:, 128:256], cT_[:, 128:256], True, True, sig=True)
            t1 = tt(v3(b, 256)[:, :, 0:128].rearrange("p a b -> p a b"), v3(b, 256)[:, :, 0:128],
                    bc(triu.unsqueeze(1), [128, 2, 128]), ALU.mult, tl)
            t = vcopy(cbm[:, g, :], b[:, 0:384], t1, [T["xsT%d" % c] for c in (0, 2, 4, 6)])
            mfree[bi] = [t]
            T["cb%d" % g] = t
            T["cbpe"] = tl
    hook("q20", 1, ssd_cb)

    def ssd_group(g):
        def f():
            tr_ = []
            for j in range(4):
                h = 4 * g + j
                a0, a1 = adt[:, h:h + 1], adt[:, 16 + h:16 + h + 1]
                ok = [T["adt"], T["cbpe"], T.get("srpe")]
                tr_.append(ts(sr[:, j, 0:128], triu, a0, ALU.mult, None, None, ok))
                tr_.append(ts(sr[:, j, 128:256], ones, a0, ALU.mult, None, None, t_ones))
                tr_.append(ts(sr[:, j, 256:384], triu, a1, ALU.mult, None, None))
            tw = []
            for j2 in range(0, 4, 2):
                bi, b, fr = bank()
                for j in range(2):
                    mm(b[:, 256 * j:256 * j + 256], gt, sr[:, j2 + j, 0:256], True, False, fr, tr_)
                    fr = []
                    tl = mm(b[:, 256 * j + 128:256 * j + 256], ones, sr[:, j2 + j, 256:384], False, True, sig=(j == 1))
                t = act(Wm[:, j2:j2 + 2, 0:256], v3(b, 256), ACT.Exp, tl, T.get("wpe"))
                mfree[bi] = [t]
                tw.append(t)
            bi, b, fr = bank()
            for j in range(4):
                tl = mm(b[:, 128 * j:128 * j + 128], gt, sr[:, j, 256:384], True, True, fr, sig=(j == 3))
                fr = []
            t = act(Wm[:, :, 256:384], v3(b, 128), ACT.Exp, tl, T.get("wpe"))
            mfree[bi] = [t]
            tw.append(t)
            T["srpe"] = tl
            T["W"] = tt(Wm, Wm, bc(cbm[:, g:g + 1, :], [128, 4, 384]), ALU.mult, tw, T["cb%d" % g])
        return f

    def ssd_y(g):
        def f():
            bi, b, fr = bank()
            for j in range(4):
                h = 4 * g + j
                xd = lambda tb: xdt[:, tb, 64 * h:64 * h + 64]
                mm(b[:, 64 * j:64 * j + 64], Wm[:, j, 0:128], xd(0), True, True, fr, T["W"], T["xdt0"], T["xdt1"])
                fr = []
                mm(b[:, 256 + 64 * j:256 + 64 * j + 64], Wm[:, j, 128:256], xd(0), True, False)
                tl = mm(b[:, 256 + 64 * j:256 + 64 * j + 64], Wm[:, j, 256:384], xd(1), False, True, sig=(j == 3))
            T["wpe"] = tl
            y_ = xs[:, :, 256 * g:256 * g + 256]
            t = tt(y_, v3(b, 256), y_, ALU.add, tl, T["ys0"], T["ys1"])
            mfree[bi] = [t]
            T["y%d" % g] = t
        return f
    for g, (n_, u_) in enumerate([("q20", 3), ("q21", 1), ("q21", 3), ("zs0", 1)]):
        hook(n_, u_, ssd_group(g))
    for g, (n_, u_) in enumerate([("q21", 0), ("q21", 2), ("zs0", 0), ("zs0", 2)]):
        hook(n_, u_, ssd_y(g))

    qa = at(A, [128, 2, 1024])
    qaT = at(A + 8, [128, 8, 256])
    pa = at(M, [128, 8, 256])
    paT = at(M + 8, [128, 2, 1024])
    oaT = at(A, [128, 8, 256])

    def evac_q2(i):
        def f(p, done):
            r = []
            for tb in range(2):
                o = qa[:, tb, 512 * i:512 * i + 512]
                t = vcopy(o, p[tb], done)
                r.append(t)
                T["qa%d%d" % (i, tb)] = rope(v3(o, 128), 16, tb, C_CA, C_SA, 4, t)
            return r
        return f

    for i in range(2):
        group("q2%d" % i, w2, KC, [(512 * i, 512)], "tok", xth, xtl, h4, evac_q2(i))

    def turn_q(i):
        def f():
            for p2 in range(4 * i, 4 * i + 4, 2):
                bi, b, fr = bank()
                for j in range(2):
                    for tb in range(2):
                        tl = tr(b[:, 256 * j + 128 * tb:256 * j + 128 * tb + 128], qa[:, tb, (p2 + j) * 128:(p2 + j + 1) * 128],
                                fr, T["qa%d0" % i], T["qa%d1" % i], sig=(j == 1 and tb == 1))
                        fr = []
                t = vcopy(qaT[:, p2:p2 + 2, :], v3(b, 256), tl)
                mfree[bi] = [t]
                T["qaT%d" % p2] = T["qaT%d" % (p2 + 1)] = t
                T["qatr"] = tl
        return f
    hook("q21", 1, turn_q(0))
    hook("zs0", 1, turn_q(1))

    amx, anm, asm, arc = small(8), small(8), small(8), small(8)

    def at_scores(qb):
        def f():
            nk = 128 * (qb + 1)
            te = []
            for h2 in range(0, 8, 2):
                bi, b, fr = bank()
                for j in range(2):
                    h = h2 + j
                    tl = mm(b[:, 256 * j:256 * j + nk], qaT[:, h, 128 * qb:128 * qb + 128], kaT[:, h // 4, 0:nk], True, True,
                            fr, T["qaT%d" % h], T["kaT"], sig=(j == 1))
                    fr = []
                o = pa[:, h2:h2 + 2, 0:nk]
                t = tt(o, v3(b, 256)[:, :, 0:nk], bc(amask[:, qb:qb + 1, 0:nk], [128, 2, nk]), ALU.add, tl, T["w%d" % qb],
                       T["W"], T.get("paT"), T["wpe"])
                mfree[bi] = [t]
                t = reduce(amx[:, h2:h2 + 2], o, ALU.max, t, T.get("arc"))
                t = ts(anm[:, h2:h2 + 2], amx[:, h2:h2 + 2], -XS, ALU.mult, None, None, t)
                for j in range(2):
                    h = h2 + j
                    te.append(act(pa[:, h, 0:nk], pa[:, h, 0:nk], ACT.Exp, t, bias=anm[:, h:h + 1], scale=XS,
                                  accum=asm[:, h:h + 1]))
            T["arc"] = recip(arc, asm, te)
            T["pa"] = tt(pa[:, :, 0:nk], pa[:, :, 0:nk], bc(arc.unsqueeze(2), [128, 8, nk]), ALU.mult, T["arc"])
        return f

    def at_turn(qb):
        def f():
            for kb in range(qb + 1):
                for h4_ in (0, 4):
                    bi, b, fr = bank()
                    for j in range(4):
                        tl = tr(b[:, 128 * j:128 * j + 128], pa[:, h4_ + j, 128 * kb:128 * kb + 128], fr, T["pa"], sig=(j == 3))
                        fr = []
                    t = vcopy(paT[:, kb, 128 * h4_:128 * h4_ + 512], b, tl, T.get("opv"))
                    mfree[bi] = [t]
            T["paTd"] = t
            T["paT"] = tl
        return f

    def at_out(qb):
        def f():
            for h4_ in (0, 4):
                bi, b, fr = bank()
                for j in range(4):
                    h = h4_ + j
                    g = h // 4
                    for kb in range(qb + 1):
                        tl = mm(b[:, 128 * j:128 * j + 128], kv[:, kb, 256 + 128 * g:256 + 128 * g + 128],
                                paT[:, kb, 128 * h:128 * h + 128], kb == 0, kb == qb, fr, T["paTd"], T["kv0"], T["kv1"],
                                sig=(j == 3 and kb == qb))
                        fr = []
                t = vcopy(oaT[:, h4_:h4_ + 4, 128 * qb:128 * qb + 128], v3(b, 128), tl, T["qatr"])
                mfree[bi] = [t]
                T["oa%d%d" % (qb, h4_ // 4)] = t
            T["opv"] = tl
        return f
    for (n_, u_), fn in zip([("zs0", 3), ("zs1", 1), ("zs1", 2), ("zs1", 3), ("za0", 0), ("za0", 1)],
                            [at_scores(0), at_turn(0), at_out(0), at_scores(1), at_turn(1), at_out(1)]):
        hook(n_, u_, fn)

    def evac_zs(i):
        def f(p, done):
            r = []
            for tb in range(2):
                o = zs[:, tb, 512 * i:512 * i + 512]
                r.append(act(o, p[tb], ACT.Silu, done, T["sc1"], T["w1"], T["adt"]))
            T["zs%d" % i] = r
            return r
        return f

    for i in range(2):
        group("zs%d" % i, w2, KC, [(3664 + 512 * i, 512)], "tok", xth, xtl, h4, evac_zs(i))

    gssq = small(8)
    junk_g = at(G + 8, [128, 256])

    def ssd_gate(i):
        def f():
            for tb in range(2):
                y_ = xs[:, tb, 512 * i:512 * i + 512]
                t = tt(y_, y_, zs[:, tb, 512 * i:512 * i + 512], ALU.mult, T["zs%d" % i], [T["y%d" % g] for g in range(4)])
                for g in (2 * i, 2 * i + 1):
                    T["gs%d%d" % (tb, g)] = square(junk_g, xs[:, tb, 256 * g:256 * g + 256],
                                                   gssq[:, 4 * tb + g:4 * tb + g + 1], t, T["wpe"])
        return f
    hook("zs1", 0, ssd_gate(0))
    hook("za0", 2, ssd_gate(1))

    def ssd_norm():
        r, t = rstd_of(gssq, 256, LN_EPS, [T["gs%d%d" % (tb, g)] for tb in range(2) for g in range(4)])
        for tb in range(2):
            x4 = v3(xs[:, tb, :], 256)
            T["yn%d" % tb] = tt(x4, x4, bc(r[:, 4 * tb:4 * tb + 4].unsqueeze(2), [128, 4, 256]), ALU.mult, t)
    hook("za1", 0, ssd_norm)

    T["mix"] = {}
    zt = [at(G + 8 + 2 * i, [128, 512]) for i in range(2)]

    def evac_za(i):
        def f(p, done):
            r = []
            for b_ in range(2):
                c = slice(4 * i + 2 * b_, 4 * i + 2 * b_ + 2)
                t = act(zt[b_] if i else zk[b_], p[b_], ACT.Silu, done, T["gs13"] if i else T["wpe"], T["W"])
                r.append(t)
                T["za%d%d" % (i, b_)] = t
            return r
        return f
    zk = [at(G + 12 + 2 * i, [128, 512]) for i in range(2)]

    for i in range(2):
        group("za%d" % i, w2, KC, [(1536 + 512 * i, 512)], "feat", xth, xtl, h4, evac_za(i))

    def mix_attn():
        for i in range(2):
            for b_ in range(2):
                z = (zt if i else zk)[b_]
                c0 = 4 * i + 2 * b_
                c = slice(c0, c0 + 2)
                z3 = v3(z, 256)
                t = tt(z3, z3, oaT[:, c, :], ALU.mult, T["za%d%d" % (i, b_)], T["oa00"], T["oa01"], T["oa10"], T["oa11"])
                th = act(xth[:, c, :], z3, ACT.Copy, t, T["pe:za1"])
                tl_ = tt(xtl[:, c, :], z3, xth[:, c, :].bitcast(F), ALU.subtract, th, T["pe:za1"])
                T["mix"][c0] = T["mix"][c0 + 1] = [th, tl_]
        rr = {}
        to_features(xs, lambda k: VT[:, 76 + k:77 + k], xth[:, 8:16, :], xtl[:, 8:16, :], rr, 8,
                    lambda k, tb: T["yn%d" % tb], T["pe:za1"])
        for k in range(8):
            T["mix"][8 + k] = rr[k]
    hook("w20", 0, mix_attn)

    y5 = at(M, [128, 2, D])
    lg = at(DD, [128, D])
    lb = at(DD + 8, [128, D])
    bst = at(B, [128, 2, 24])

    def ln_loads():
        T["lg"] = load("pool", lg, on_all(I["ln_g_2"][0]), T["mix"][15])
        T["lb"] = load("pool", lb, on_all(I["ln_b_2"][0]), T["mix"][15])
    hook("w20", 1, ln_loads)

    def evac_w2(i):
        def f(p, done):
            r = []
            for tb in range(2):
                o = y5[:, tb, 512 * i:512 * i + 512]
                t = stt(o, xx[:, tb, 512 * i:512 * i + 512], ALPHA, p[tb], ALU.mult, ALU.add, done, T["x3"], T["opv"],
                        T["paT"])
                r.append(t)
                so = bst[:, tb, 6 * i:6 * i + 6]
                T["bs%d%d" % (tb, i)] = put("dve", lambda e, so=so, o=o: e.bn_stats(so, o), [t])
            return r
        return f

    for i in range(4):
        group("w2%d" % i, I["w_out_2"][0], KC, [(512 * i, 512)], "tok", xth, xtl, reader("mix"), evac_w2(i))

    run()

    o_dst = out_d[0].rearrange("(b p) d -> p b d", p=128)
    s_out = nc.alloc_semaphore("s_out")
    n_out = 0
    for tb in range(2):
        mv = small(2)
        s3 = bst[:, tb, :]
        t = put("dve", lambda e, mv=mv, s3=s3: e.bn_aggr(mv, s3), [T["bs%d%d" % (tb, i)] for i in range(4)])
        r, t = rstd_of(mv[:, 1:2], 1.0, LN_EPS, t)
        for hf in range(2):
            c = slice(1024 * hf, 1024 * hf + 1024)
            y_ = y5[:, tb, c]
            t1 = ts(y_, y_, mv[:, 0:1], ALU.subtract, r, ALU.mult, t)
            t1 = tt(y_, y_, lg[:, c], ALU.mult, t1, T["lg"])
            t1 = tt(y_, y_, lb[:, c], ALU.add, t1, T["lb"])
            d_ = o_dst[:, tb, c]
            put("sp", lambda e, d_=d_, y_=y_: e.dma_start(d_, y_).then_inc(s_out, 16), [t1], False)
            n_out += 16
    put("sp", None, [(s_out, n_out)], False)

    def play(name, e):
        for todo, fn, signal in queue[name]:
            for s, n in todo:
                e.wait_ge(s, n)
            if fn is None:
                continue
            ins = fn(e)
            if signal:
                ins.then_inc(sem[name], 1)

    with nc.Block() as block:
        @block.sync
        def _(e):
            play("sp", e)

        @block.scalar
        def _(e):
            play("act", e)

        @block.gpsimd
        def _(e):
            play("pool", e)

        @block.vector
        def _(e):
            play("dve", e)

        @block.tensor
        def _(e):
            play("pe", e)


_OUT = ((1, SEQ, D), "float32")


def kernel(**inputs):
    import concourse.bacc as bacc
    from concourse.bass_utils import run_bass_kernel_spmd

    nc = bacc.Bacc("TRN2", target_bir_lowering=False, num_devices=1)
    arrays, aps = {}, {}
    for name in inputs:
        a = np.ascontiguousarray(inputs[name])
        arrays[f"in_{name}"] = a
        aps[name] = nc.dram_tensor(f"in_{name}", a.shape, mybir.dt.from_np(a.dtype), kind="ExternalInput").ap()
    c = shape_constants()
    arrays["in_shape_constants"] = c
    cst = nc.dram_tensor("in_shape_constants", c.shape, F, kind="ExternalInput").ap()
    out = nc.dram_tensor("out_0", _OUT[0], mybir.dt.from_np(np.dtype(_OUT[1])), kind="ExternalOutput").ap()
    build(nc, aps, cst, out)
    r = run_bass_kernel_spmd(nc, [arrays], core_ids=[0])
    return r.results[0]["out_0"]
```

```python
import math

import numpy as np

import concourse.bass as bass
from concourse import mybir

F = mybir.dt.float32
R = mybir.dt.float32r
ALU = mybir.AluOpType
ACT = mybir.ActivationFunctionType
AX = mybir.AxisListType

SEQ = 256
D = 2048
KC = D // 128
FF = 5632
EPS = 1e-6
LN_EPS = 1e-5
ALPHA = 2.0 ** 0.25
BIG = 1.0e30
GONE = -3.0e38
TOPK = 64

KB = 1024
BASE = 16512

C_ID, C_TRIU, C_GT, C_M64, C_SCAN, C_CA, C_SA, C_CI, C_SI, C_END = 0, 128, 256, 384, 512, 768, 800, 832, 848, 864


def shape_constants():
    c = np.zeros((128, C_END), np.float32)
    i = np.arange(128)
    c[:, C_ID:C_ID + 128] = np.eye(128)
    c[:, C_TRIU:C_TRIU + 128] = i[None, :] >= i[:, None]
    c[:, C_GT:C_GT + 128] = i[:, None] > i[None, :]
    c[:64, C_M64 + 64:C_M64 + 128] = -BIG
    c[:, C_SCAN:C_SCAN + 256] = (np.arange(256) % 64 != 0)
    pos = np.arange(SEQ, dtype=np.float32)
    for rot, cc, cs in ((32, C_CA, C_SA), (16, C_CI, C_SI)):
        half = rot // 2
        inv = np.float32(500000.0) ** (-np.arange(half, dtype=np.float32) * np.float32(2.0) / np.float32(rot))
        ang = (pos[:, None] * inv.astype(np.float32)[None, :]).astype(np.float32)
        for tab, col in ((np.cos(ang), cc), (np.sin(ang), cs)):
            for tb in range(2):
                c[:, col + tb * half:col + (tb + 1) * half] = tab[tb * 128:(tb + 1) * 128]
    return c


def build(nc, I, cst_d, out_d):
    engines = ("pe", "dve", "act", "pool", "sp")
    queue = {e: [] for e in engines}
    sem = {e: nc.alloc_semaphore("s_" + e) for e in engines}
    count = dict.fromkeys(engines, 0)
    seen = {e: {} for e in engines}

    def tokens(w):
        if w is None:
            return []
        if isinstance(w, tuple) and len(w) == 2 and isinstance(w[1], int):
            return [w]
        return [p for x in w for p in tokens(x)]

    def put(e, fn, waits, signal=True):
        todo = []
        for s, n in tokens(waits):
            if seen[e].get(s.num, 0) < n:
                seen[e][s.num] = n
                todo.append((s, n))
        if signal:
            count[e] += 1
        queue[e].append((todo, fn, signal))
        return (sem[e], count[e]) if signal else None

    def tt(out, a, b, op, *w):
        return put("dve", lambda e: e.tensor_tensor(out, a, b, op), w)

    def ts(out, a, s1, op0, s2, op1, *w):
        if op1 is None:
            return put("dve", lambda e: e.tensor_scalar(out, a, s1, None, op0), w)
        return put("dve", lambda e: e.tensor_scalar(out, a, s1, s2, op0, op1), w)

    def stt(out, a, s, b, op0, op1, *w):
        return put("dve", lambda e: e.scalar_tensor_tensor(out=out, in0=a, scalar=s, in1=b, op0=op0, op1=op1), w)

    def vcopy(out, a, *w):
        return put("dve", lambda e: e.tensor_copy(out, a), w)

    def vset(out, v, *w):
        return put("dve", lambda e: e.memset(out, v), w)

    def recip(out, a, *w):
        return put("dve", lambda e: e.reciprocal(out, a), w)

    def reduce(out, a, op, *w):
        return put("dve", lambda e: e.tensor_reduce(out, a, AX.X, op), w)

    def act(out, a, func, *w, bias=0.0, scale=1.0, accum=None):
        if accum is None:
            return put("act", lambda e: e.activation(out, a, func, bias=bias, scale=scale), w)
        return put("act", lambda e: e.activation(out, a, func, bias=bias, scale=scale, accum_out=accum), w)

    last_junk = {}

    def square(junk, a, accum, *w):
        t = act(junk, a, ACT.Square, w, last_junk.get(junk.name), accum=accum)
        last_junk[junk.name] = t
        return t

    def mm(out, l, r, start, stop, *w, sig=False, share=False):
        return put("pe", lambda e: e.matmul(out, l, r, start=start, stop=stop, skip_group_check=share), w, sig)

    def tr(out, a, *w, sig=False):
        return put("pe", lambda e: e.transpose(out, a, ident), w, sig)

    def load(e, out, src, *w):
        nsem[0] += 1
        s = nc.alloc_semaphore(f"s_ld{nsem[0]}")
        put(e, lambda g: g.dma_start(out, src).then_inc(s, 16), w, False)
        return (s, 16)

    nsem = [0]

    nname = [0]

    def at(kb, shape, dt=F):
        nname[0] += 1
        t = nc.alloc_sbuf_tensor_at(f"b{nname[0]}", shape, dt, offset=BASE + int(kb * KB))
        return t[:, :] if len(shape) == 2 else t[:, :, :]

    RAW, SPL, XT, A, B, C, G, DD, M, K0 = 0, 24, 72, 104, 120, 128, 148, 164, 180, 196
    raw = [at(RAW + 8 * i, [128, 2048]) for i in range(3)]
    wh = [at(SPL + 16 * i, [128, 2048], R) for i in range(3)]
    wl = [at(SPL + 16 * i + 8, [128, 2048], R) for i in range(3)]
    xth = at(XT, [128, KC, 256], R)
    xtl = at(XT + 16, [128, KC, 256], R)
    cst = at(K0, [128, C_END])
    ident = cst[:, C_ID:C_ID + 128]
    triu = cst[:, C_TRIU:C_TRIU + 128]
    gt = cst[:, C_GT:C_GT + 128]
    m64 = cst[:, C_M64:C_M64 + 128]
    scan1 = cst[:, C_SCAN:C_SCAN + 256]
    ones = at(K0 + 3.5, [128, 128])
    VT = at(K0 + 4, [128, 6 * 128])
    st = at(K0 + 7, [128, 256])
    glr = at(K0 + 8, [128, 32])
    glrT = at(K0 + 8.125, [16, 256])
    sgb = at(K0 + 9.25, [1, 256])
    dtb = at(K0 + 10.25, [128, 16])
    alog = at(K0 + 10.3125, [128, 16])
    dsk = at(K0 + 10.375, [128, 16])
    dt_ = at(K0 + 10.5, [128, 32])
    adt = at(K0 + 10.625, [128, 32])
    dtmp = at(K0 + 10.75, [128, 32])
    dtm2 = at(K0 + 10.875, [128, 32])
    widx = at(K0 + 11, [128, 32])
    dl1 = at(K0 + 11.125, [128, 32])
    do1 = at(K0 + 11.25, [128, 32])

    used = [0]

    def small(n):
        used[0] += n
        assert used[0] <= 256
        return st[:, used[0] - n:used[0]]

    ps = [[nc.alloc_psum_tensor(f"ps{s}{b}", [128, 512], F)[:, :] for b in range(2)] for s in range(2)]
    ms = [nc.alloc_psum_tensor(f"pm{b}", [128, 512], F)[:, :] for b in range(4)]
    mfree = [[], [], [], []]
    mnext = [0]

    def bank():
        b = mnext[0] % 4
        mnext[0] += 1
        return b, ms[b], mfree[b]

    def v3(ap, n):
        return ap.rearrange("p (a b) -> p a b", b=n)

    def bc(ap, shape):
        return ap.to_broadcast(shape)

    groups = []

    def group(name, w, kcs, cols, kind, xh, xl, ready, evac, chunk=4, k_off=0):
        groups.append(dict(name=name, w=w, kcs=kcs, cols=cols, kind=kind, xh=xh, xl=xl, ready=ready,
                           evac=evac, chunk=chunk, k_off=k_off))

    T = {}
    hooks = {}

    def hook(name, unit, fn):
        hooks.setdefault((name, unit), []).append(fn)

    def run():
        units = []
        for gi, g in enumerate(groups):
            k = 0
            ui = 0
            while k < g["kcs"]:
                nk = min(g["chunk"], g["kcs"] - k)
                units.append((gi, ui, k, nk))
                k += nk
                ui += 1
        n_units = len(units)
        raw_sem = [nc.alloc_semaphore(f"s_raw{i}") for i in range(3)]
        raw_cnt = [0, 0, 0]
        landed, hi, lo, done = {}, {}, {}, {}
        set_free = [[], []]

        def dma(n):
            gi, ui, k, nk = units[n]
            g = groups[gi]
            s = n % 3
            nc_ = sum(c for _, c in g["cols"])
            dst = raw[s][:, 0:nk * nc_].rearrange("p (k c) -> p k c", c=nc_)
            w = [hi.get(n - 3), lo.get(n - 3)]
            o = 0
            k0 = g["k_off"] + k
            for c0, c in g["cols"]:
                src = g["w"][k0 * 128:(k0 + nk) * 128, c0:c0 + c].rearrange("(k p) c -> p k c", p=128)
                d = dst[:, :, o:o + c]
                put("sp", lambda e, d=d, src=src, s=s: e.dma_start(d, src).then_inc(raw_sem[s], 16), w, False)
                raw_cnt[s] += 16
                o += c
            landed[n] = (raw_sem[s], raw_cnt[s])

        def split_hi(n):
            gi, ui, k, nk = units[n]
            s = n % 3
            m = nk * sum(c for _, c in groups[gi]["cols"])
            hi[n] = act(wh[s][:, 0:m], raw[s][:, 0:m], ACT.Copy, landed[n], done.get(n - 3))

        def split_lo(n):
            gi, ui, k, nk = units[n]
            s = n % 3
            m = nk * sum(c for _, c in groups[gi]["cols"])
            lo[n] = tt(wl[s][:, 0:m], raw[s][:, 0:m], wh[s][:, 0:m].bitcast(F), ALU.subtract,
                       landed[n], hi[n], done.get(n - 3))

        def products(n):
            gi, ui, k, nk = units[n]
            g = groups[gi]
            s = n % 3
            pset = ps[gi % 2]
            nc_ = sum(c for _, c in g["cols"])
            h3 = wh[s][:, 0:nk * nc_].rearrange("p (k c) -> p k c", c=nc_)
            l3 = wl[s][:, 0:nk * nc_].rearrange("p (k c) -> p k c", c=nc_)
            w = [hi[n], lo[n]]
            if ui == 0:
                w += [set_free[gi % 2]]
            last_unit = k + nk == g["kcs"]
            for kk in range(nk):
                kg = k + kk
                w = w + [g["ready"](kg)]
                final = kk == nk - 1
                for b in range(2):
                    if g["kind"] == "tok":
                        xs_ = slice(b * 128, b * 128 + 128)
                        trio = [(g["xh"][:, kg, xs_], h3[:, kk, :]), (g["xh"][:, kg, xs_], l3[:, kk, :]),
                                (g["xl"][:, kg, xs_], h3[:, kk, :])]
                        for q, (l, r) in enumerate(trio):
                            tok = mm(pset[b][:, 0:nc_], l, r, kg == 0 and q == 0, kg == g["kcs"] - 1 and q == 2, w,
                                     sig=final and b == 1 and q == 2)
                            w = []
                    else:
                        for f in range(2):
                            cs = slice((2 * b + f) * 128, (2 * b + f + 1) * 128)
                            o = pset[b][:, f * 256:(f + 1) * 256]
                            trio = [(h3[:, kk, cs], g["xh"][:, kg, :]), (h3[:, kk, cs], g["xl"][:, kg, :]),
                                    (l3[:, kk, cs], g["xh"][:, kg, :])]
                            for q, (l, r) in enumerate(trio):
                                tok = mm(o, l, r, kg == 0 and q == 0 and f == 0, kg == g["kcs"] - 1 and q == 2, w,
                                         sig=final and b == 1 and f == 1 and q == 2, share=True)
                                w = []
            done[n] = tok
            T["pe:" + g["name"]] = tok
            if last_unit:
                r = g["evac"](pset, tok)
                set_free[gi % 2] = r

        for n in range(min(3, n_units)):
            dma(n)
        for n in range(min(2, n_units)):
            split_hi(n)
            split_lo(n)
            if n + 3 < n_units:
                dma(n + 3)
        for n in range(n_units):
            gi, ui, k, nk = units[n]
            if n + 2 < n_units:
                split_hi(n + 2)
            for fn in hooks.pop((groups[gi]["name"], ui), []):
                fn()
            if n + 2 < n_units:
                split_lo(n + 2)
                if n + 5 < n_units:
                    dma(n + 5)
            products(n)
        assert not hooks, hooks.keys()

    def rstd_of(ssq, n, eps, *w):
        k = ssq.shape[-1]
        a, b = small(k), small(k)
        t = ts(a, ssq, 1.0 / n, ALU.mult, eps, ALU.add, *w)
        t = act(b, a, ACT.Sqrt, t)
        c = small(k)
        t = recip(c, b, t)
        return c, t

    def to_features(src, gcol, dst_h, dst_l, ready, kcs, src_ok, dst_ok, k0=0):
        for k2 in range(k0, kcs, 2):
            bi, b, fr = bank()
            last = None
            for j in range(2):
                for tb in range(2):
                    last = tr(b[:, j * 256 + tb * 128:j * 256 + tb * 128 + 128],
                              src[:, tb, (k2 + j) * 128:(k2 + j + 1) * 128], fr, src_ok(k2 + j, tb),
                              sig=(j == 1 and tb == 1))
                    fr = []
            if gcol is None:
                th = act(dst_h[:, k2:k2 + 2, :], v3(b, 256), ACT.Copy, last, dst_ok)
                tl = tt(dst_l[:, k2:k2 + 2, :], v3(b, 256), dst_h[:, k2:k2 + 2, :].bitcast(F), ALU.subtract, th, dst_ok)
                ready[k2] = ready[k2 + 1] = [th, tl]
            else:
                t0 = act(dst_h[:, k2, :], b[:, 0:256], ACT.Copy, last, dst_ok, scale=gcol(k2))
                t1 = act(dst_h[:, k2 + 1, :], b[:, 256:512], ACT.Copy, scale=gcol(k2 + 1))
                l0 = stt(dst_l[:, k2, :], b[:, 0:256], gcol(k2), dst_h[:, k2, :].bitcast(F), ALU.mult, ALU.subtract,
                         t1, dst_ok)
                tl = stt(dst_l[:, k2 + 1, :], b[:, 256:512], gcol(k2 + 1), dst_h[:, k2 + 1, :].bitcast(F), ALU.mult,
                         ALU.subtract)
                ready[k2] = [t0, l0]
                ready[k2 + 1] = [t1, tl]
            mfree[bi] = [tl]

    def prenorm_sums(x, junk, ok, junk_ok):
        ssq = small(4)
        t = []
        for tb in range(2):
            for hf in range(2):
                j = 2 * tb + hf
                t.append(square(junk[:, 1024 * hf:1024 * hf + 1024], x[:, tb, 1024 * hf:1024 * hf + 1024],
                                ssq[:, j:j + 1], ok[tb][hf], junk_ok))
        T["junkB"] = t
        return ssq, t

    def prenorm_scale(x, h, ssq, t, h_ok):
        th = []
        for tb in range(2):
            s1 = small(1)
            t1 = tt(s1, ssq[:, 2 * tb:2 * tb + 1], ssq[:, 2 * tb + 1:2 * tb + 2], ALU.add, t[2 * tb:2 * tb + 2])
            r, t1 = rstd_of(s1, D, EPS, t1)
            th.append(ts(h[:, tb, :], x[:, tb, :], r, ALU.mult, None, None, t1, h_ok))
        return th

    def turn(h, gcol, key, th, dst_ok, dst_h=None, dst_l=None, k0=0, k1=KC):
        T.setdefault(key, {})
        to_features(h, gcol, xth if dst_h is None else dst_h, xtl if dst_l is None else dst_l, T[key], k1,
                    lambda k, tb: th[tb], dst_ok, k0)

    def tok_store(y, i, y_ok, part=None, tag=None, g=None, g_ok=None, add=False, junk=None, junk_ok=None):
        c = slice(i * 512, (i + 1) * 512)

        def evac(p, done):
            free, ready = [], []
            for tb in range(2):
                o = y[:, tb, c]
                if part is None:
                    t = T["dn0"] = vcopy(o, p[tb], done, y_ok())
                    free.append(t)
                    ready.append(t)
                    continue
                acc = part[:, tb * 4 + i:tb * 4 + i + 1]
                if add:
                    t = tt(o, p[tb], o, ALU.add, done, y_ok())
                    free.append(t)
                    t = square(junk, o, acc, t, junk_ok())
                    t2 = tt(o, o, g[:, c], ALU.mult, t, g_ok())
                else:
                    t = square(junk, p[tb], acc, done, junk_ok())
                    t2 = tt(o, p[tb], g[:, c], ALU.mult, t, g_ok(), y_ok())
                    free.append(t2)
                ready += [t, t2]
            T.setdefault(tag, []).extend(ready)
            return free
        return evac

    def postnorm(y, part, x, tag, x_ok):
        ssq = small(2)
        t = reduce(ssq, v3(part, 4), ALU.add, T[tag])
        r, t = rstd_of(ssq, D, EPS, t)
        return [[stt(x[:, tb, 1024 * hf:1024 * hf + 1024], y[:, tb, 1024 * hf:1024 * hf + 1024], r[:, tb:tb + 1],
                     x[:, tb, 1024 * hf:1024 * hf + 1024], ALU.mult, ALU.add, t, x_ok) for hf in range(2)]
                for tb in range(2)]

    def on_all(vec):
        return vec.partition_broadcast(128)

    t_cst = load("act", cst, cst_d)
    t_ones = vset(ones, 1.0)
    x_ap = at(DD, [128, 2, D])
    x_src = I["x"][0].rearrange("(b p) d -> p b d", p=128)
    t_x = [[load("sp", x_ap[:, tb, 1024 * hf:1024 * hf + 1024], x_src[:, tb, 1024 * hf:1024 * hf + 1024])
            for hf in range(2)] for tb in range(2)]

    vraw = at(B, [128, 6 * 128])
    tv = {}

    def vec_rows(e, tile, r0, src, n):
        t = load(e, vraw[r0:r0 + n, tile * 128:(tile + 1) * 128], src.rearrange("(r p) -> r p", p=128))
        tv.setdefault(tile, []).append(t)

    vec_rows("act", 0, 0, I["pre_norm_mix"][0], 16)
    vec_rows("act", 0, 16, I["gla_b_gate"][0], 8)
    vec_rows("act", 0, 24, I["gla_norm_g"][0], 4)
    vec_rows("act", 0, 28, I["pre_norm_xa"][0], 16)
    vec_rows("act", 0, 44, I["mem_norm_g"][0], 16)
    vec_rows("act", 0, 60, I["pre_norm_ffn"][0], 16)
    vec_rows("act", 0, 76, I["ssd_norm_w_2"][0], 8)
    vec_rows("act", 0, 84, I["conv_b_2"][0], 16)
    vec_rows("pool", 1, 0, I["ffn_conv_b"][0], 88)
    for j in range(3):
        vec_rows("pool", 2 + j, 0, I["ffn_conv_w"][0][j], 88)
    for j in range(4):
        vec_rows("pool", 5, 16 * j, I["conv_w_2"][0][j], 16)
    sgb8 = at(B + 4, [1, 1024])
    t_sgb = load("pool", sgb8, I["sg_b"][0].rearrange("(o g) t -> o (g t)", o=1))
    t_dtb = load("pool", dtb, on_all(I["dt_bias_2"][0]))
    t_alog = load("pool", alog, on_all(I["a_log_2"][0]))
    t_dsk = load("pool", dsk, on_all(I["d_skip_2"][0]))

    h_ap = at(G, [128, 2, D])
    junk0 = at(M, [128, D])
    bi, b, fr = bank()
    tl = put("pe", lambda e, b=b: e.transpose(b[:, 0:100], vraw[0:100, 0:128], ident[0:100, 0:100]), [tv[0], t_cst])
    t_vt = vcopy(VT[:, 0:100], b[:, 0:100], tl)
    mfree[bi] = [t_vt]

    def turn_vectors():
        bi, b, fr = bank()
        for i in range(4):
            tl = put("pe", lambda e, b=b, i=i: e.transpose(b[:, 128 * i:128 * i + 88],
                                                           vraw[0:88, 128 * (i + 1):128 * (i + 2)], ident[0:88, 0:88]),
                     [fr, tv[i + 1]])
        t = vcopy(v3(VT[:, 128:640], 128)[:, :, 0:88], v3(b, 128)[:, :, 0:88], tl)
        mfree[bi] = [t]
        bi, b, fr = bank()
        tl = put("pe", lambda e, b=b: e.transpose(b[:, 0:64], vraw[0:64, 640:768], ident[0:64, 0:64]), [fr, tv[5]])
        T["vt2"] = vcopy(VT[:, 640:704], b[:, 0:64], tl)
        mfree[bi] = [T["vt2"]]
    hook("vs0", 2, turn_vectors)

    def gcols(c0):
        return lambda k: VT[:, c0 + k:c0 + k + 1]

    ssq0, t0 = prenorm_sums(x_ap, junk0, t_x, None)
    th0 = prenorm_scale(x_ap, h_ap, ssq0, t0, None)
    turn(h_ap, gcols(0), "h1", th0, [t_vt])

    h1 = lambda k: T["h1"][k]
    w_in = I["w_in"][0]

    def reader(key):
        return lambda k: T[key][k]

    vs = at(A, [128, 2, 1024])
    uT = at(A + 8, [128, 8, 256])
    sgw = at(B, [128, 8, 128])
    sgr = at(C + 16, [128, 8, 128])
    swT = at(G + 8, [128, 8, 128])
    lng = at(G, [128, 1024])
    lnb = at(G + 4, [128, 1024])
    yaTh = at(C, [128, 8, 256], R)
    yaTl = at(C + 8, [128, 8, 256], R)
    yaf = [at(DD + 2 * i, [128, 512]) for i in range(2)]

    def evac_vs(i):
        def f(p, done):
            r = [act(vs[:, tb, i * 512:(i + 1) * 512], p[tb], ACT.Gelu, done) for tb in range(2)]
            T["vs%d" % i] = r
            return r
        return f

    def evac_u(i):
        def f(p, done):
            r = [act(uT[:, 4 * i + 2 * b_:4 * i + 2 * b_ + 2, :], v3(p[b_], 256), ACT.Gelu, done) for b_ in range(2)]
            T["u%d" % i] = r
            return r
        return f

    for i in range(2):
        group("vs%d" % i, w_in, KC, [(1024 + 512 * i, 512)], "tok", xth, xtl, h1, evac_vs(i))
    for i in range(2):
        group("u%d" % i, w_in, KC, [(512 * i, 512)], "feat", xth, xtl, h1, evac_u(i))

    def sg_loads():
        T["lng"] = load("pool", lng, on_all(I["sg_ln_g"][0]), T["pe:vs0"])
        T["lnb"] = load("pool", lnb, on_all(I["sg_ln_b"][0]), T["pe:vs0"])
        T["sgr"] = load("pool", sgr, I["sg_w"][0].rearrange("g t s -> t g s"))
    hook("vs1", 0, sg_loads)

    def sg_turn():
        for g0 in (0, 4):
            bi, b, fr = bank()
            for g in range(4):
                tl = tr(b[:, g * 128:(g + 1) * 128], sgr[:, g0 + g, :], fr, T["sgr"], sig=(g == 3))
                fr = []
            t = tt(swT[:, g0:g0 + 4, :], v3(b, 128), bc(triu.unsqueeze(1), [128, 4, 128]), ALU.mult, tl, T["pe:vs0"])
            mfree[bi] = [t]
            T["swT%d" % (g0 // 4)] = t
    hook("vs1", 3, sg_turn)

    stats = at(DD + 4, [128, 2, 12])

    def sg_norm(tb):
        def f():
            tt_ = []
            for i in range(2):
                o = stats[:, tb, 6 * i:6 * i + 6]
                a_ = vs[:, tb, i * 512:(i + 1) * 512]
                tt_.append(put("dve", lambda e, o=o, a_=a_: e.bn_stats(o, a_), [T["vs0"], T["vs1"]]))
            mv = small(2)
            s3 = stats[:, tb, :]
            t = put("dve", lambda e, mv=mv, s3=s3: e.bn_aggr(mv, s3), [tt_])
            r, t2 = rstd_of(mv[:, 1:2], 1.0, EPS, t)
            t3 = ts(vs[:, tb, :], vs[:, tb, :], mv[:, 0:1], ALU.subtract, r, ALU.mult, t2)
            t4 = tt(vs[:, tb, :], vs[:, tb, :], lng, ALU.mult, t3, T["lng"])
            T["vsn%d" % tb] = tt(vs[:, tb, :], vs[:, tb, :], lnb, ALU.add, t4, T["lnb"])
        return f
    hook("u0", 1, sg_norm(0))
    hook("u0", 3, sg_norm(1))

    def sg_mix():
        T["yaT"] = {}
        for g0 in range(0, 8, 2):
            bi, b, fr = bank()
            for j in range(2):
                for n in range(2):
                    o = b[:, j * 256 + n * 128:j * 256 + n * 128 + 128]
                    g = g0 + j
                    mm(o, vs[:, n, g * 128:(g + 1) * 128], swT[:, g, :], True, False, fr,
                       T["vsn0"], T["vsn1"], T["swT0"], T["swT1"])
                    fr = []
                    tl = mm(o, ones[0:1, :], sgb8[0:1, g * 128:(g + 1) * 128], False, True, t_ones, t_sgb,
                            sig=(j == 1 and n == 1))
            i = (g0 // 2) % 2
            t = tt(yaf[i], b, uT[:, g0:g0 + 2, :].rearrange("p a b -> p (a b)"), ALU.mult, tl, T["u0"], T["u1"],
                   T.get("yaf%d" % i))
            mfree[bi] = [t]
            th = act(yaTh[:, g0:g0 + 2, :], v3(yaf[i], 256), ACT.Copy, t)
            T["yaf%d" % i] = tl_ = tt(yaTl[:, g0:g0 + 2, :], v3(yaf[i], 256), yaTh[:, g0:g0 + 2, :].bitcast(F),
                                      ALU.subtract, th)
            T["yaT"][g0] = T["yaT"][g0 + 1] = [th, tl_]
    hook("ma0", 2, sg_mix)

    sig_a = at(M, [128, KC, 256])

    def evac_sig(dst, i, tag, ok):
        def f(p, done):
            r = [act(dst[:, 4 * i + 2 * b_:4 * i + 2 * b_ + 2, :], v3(p[b_], 256), ACT.Sigmoid, done, ok())
                 for b_ in range(2)]
            T[tag + str(i)] = r
            return r
        return f

    for i in range(4):
        group("ma%d" % i, w_in, KC, [(8208 + 512 * i, 512)], "feat", xth, xtl, h1,
              evac_sig(sig_a, i, "sa", lambda: None))

    def evac_pa(i):
        def f(p, done):
            r = []
            for b_ in range(2):
                o = sig_a[:, 4 * i + 2 * b_:4 * i + 2 * b_ + 2, :]
                r.append(tt(o, v3(p[b_], 256), o, ALU.mult, done, T["sa%d" % i]))
            T["ma_%d" % i] = r
            return r
        return f

    for i in range(4):
        group("pa%d" % i, I["w_proj_a"][0], 8, [(512 * i, 512)], "feat", yaTh, yaTl, reader("yaT"), evac_pa(i))

    qT = at(A, [128, 8, 256])
    kT = at(A + 8, [128, 8, 256])
    bT = at(B, [128, 8, 256])
    E = at(C, [128, 8, 640])
    tmpG = at(G, [128, 2048])
    wg2 = at(G + 8, [16, 1024])
    v_t = at(DD, [128, 2, D])
    og = at(G, [128, 2, D])
    AT = at(A + 8, [128, 4, 512])
    o_t = at(C, [128, 2, D])
    ybTh = at(A, [128, KC, 256], R)
    ybTl = at(G, [128, KC, 256], R)
    EO = [0, 64, 192, 384]

    def evac_glr(p, done):
        t = [vcopy(glr[:, 16 * tb:16 * tb + 16], p[tb][:, 0:16], done) for tb in range(2)]
        T["glr"] = t
        T["wg2"] = load("pool", wg2, I["gla_w_gate2"][0], T["swT0"], T["swT1"], T["pe:ma1"])
        return t

    group("glr", w_in, KC, [(8192, 128)], "tok", xth, xtl, h1, evac_glr, chunk=16)

    def gate1():
        bi, b, fr = bank()
        for tb in range(2):
            tl = tr(b[0:16, tb * 128:(tb + 1) * 128], glr[:, 16 * tb:16 * tb + 16], fr, T["glr"], sig=(tb == 1))
        T["glrT"] = vcopy(glrT, b[0:16, 0:256], tl)
        mfree[bi] = [T["glrT"]]
    hook("q0", 0, gate1)

    def gate2():
        T["y"] = []
        for d2 in range(0, 8, 2):
            bi, b, fr = bank()
            for j in range(2):
                tl = mm(b[:, 256 * j:256 * j + 256], wg2[0:16, (d2 + j) * 128:(d2 + j + 1) * 128], glrT, True, True,
                        fr, T["glrT"], T["wg2"], sig=(j == 1))
                fr = []
            for j in range(2):
                t = ts(bT[:, d2 + j, :], b[:, 256 * j:256 * j + 256], VT[:, 16 + d2 + j:17 + d2 + j], ALU.add, None,
                       None, tl, T["pe:ma1"], t_vt)
            T["y"].append(t)
            mfree[bi] = [t]
    hook("q0", 1, gate2)
    bT2 = bT.rearrange("p a b -> p (a b)")

    def gate_log():
        t = act(tmpG, bT2, ACT.Abs, T["y"], T["pe:pa0"])
        t = act(tmpG, tmpG, ACT.Exp, t, scale=-1.0)
        T["log"] = act(tmpG, tmpG, ACT.Ln, t, bias=1.0)
    hook("q0", 2, gate_log)

    def gate_la():
        t = stt(bT2, bT2, 0.0, tmpG, ALU.min, ALU.subtract, T["log"])
        T["la"] = ts(bT2, bT2, 1.0 / 16.0, ALU.mult, -1.0, ALU.max, t)
    hook("q1", 0, gate_la)

    def gate_scan():
        tb_ = []
        for d in range(8):
            o, i_ = tmpG[:, d * 256:(d + 1) * 256], bT[:, d, :]
            tb_.append(put("dve", lambda e, o=o, i_=i_: e.tensor_tensor_scan(o, scan1, i_, 0.0, ALU.mult, ALU.add),
                           [T["la"], t_cst]))
        T["b"] = tb_
    hook("q1", 1, gate_scan)

    def gate_spans():
        b3 = v3(tmpG, 256)
        tb_ = T["b"]
        prev = None
        for i in range(4):
            own = ts(E[:, :, EO[i] + 64 * i:EO[i] + 64 * i + 64], b3[:, :, 64 * i:64 * i + 64], -1.0, ALU.mult, None, None,
                     tb_, T["pe:pa3"])
            if i:
                last = b3[:, :, 64 * i - 1:64 * i]
                prev = tt(E[:, :, EO[i]:EO[i] + 64 * i], E[:, :, EO[i - 1]:EO[i - 1] + 64 * i],
                          bc(last, [128, 8, 64 * i]), ALU.add, prev)
                prev = [prev, own]
            else:
                prev = own
        T["spans"] = prev
    hook("q1", 2, gate_spans)

    def gate_exp():
        Ef = E.rearrange("p a b -> p (a b)")
        prev, tb_ = T["spans"], T["b"]
        T["E"] = act(Ef, Ef, ACT.Exp, prev)
        T["eb"] = act(bT.rearrange("p a b -> p (a b)"), tmpG, ACT.Exp, tb_, prev)
    hook("q1", 3, gate_exp)

    def evac_q(i):
        def f(p, done):
            r = [vcopy(qT[:, 4 * i + 2 * b_:4 * i + 2 * b_ + 2, :], v3(p[b_], 256), done, T["pe:pa3"])
                 for b_ in range(2)]
            T["q%d" % i] = r
            return r
        return f

    def evac_k(i):
        def f(p, done):
            r = [vcopy(kT[:, 4 * i + 2 * b_:4 * i + 2 * b_ + 2, :], v3(p[b_], 256), done) for b_ in range(2)]
            T["k%d" % i] = r
            return r
        return f

    for i in range(2):
        group("q%d" % i, w_in, KC, [(2048 + 512 * i, 512)], "feat", xth, xtl, h1, evac_q(i))
    for i in range(2):
        group("k%d" % i, w_in, KC, [(3072 + 512 * i, 512)], "feat", xth, xtl, h1, evac_k(i))

    def gate_q():
        q2 = qT.rearrange("p a b -> p (a b)")
        T["qs"] = stt(q2, q2, 1.0 / 16.0, bT.rearrange("p a b -> p (a b)"), ALU.mult, ALU.mult, T["eb"], T["q0"], T["q1"])
    hook("k0", 1, gate_q)

    def gate_k(part):
        def f():
            T.setdefault("ks", []).extend(
                tt(E[:, :, EO[i]:EO[i] + 64 * (i + 1)], E[:, :, EO[i]:EO[i] + 64 * (i + 1)],
                   kT[:, :, 0:64 * (i + 1)], ALU.mult, T["E"], T["k0"], T["k1"]) for i in part)
            if 3 in part:
                z = AT.rearrange("p h (a b) -> p (h a) b", b=256)[64:128, :, 0:64]
                T["ATz"] = vset(z, 0.0, T["ks"])
        return f
    hook("v0", 1, gate_k([0, 1, 2]))
    hook("v0", 3, gate_k([3]))

    def gla_scores(hs):
        def f():
            for h in hs:
                bi, b, fr = bank()
                tl = None
                for i in range(4):
                    for sb in range((i // 2) + 1):
                        rows_ = min(64 * (i + 1) - 128 * sb, 128)
                        o = b[0:rows_, 256 * sb + 64 * (i - 2 * sb):256 * sb + 64 * (i - 2 * sb) + 64]
                        for d in range(2):
                            e0 = EO[i] + 128 * sb
                            tl = mm(o, E[:, 2 * h + d, e0:e0 + rows_], qT[:, 2 * h + d, 64 * i:64 * i + 64], d == 0, d == 1,
                                    fr, T["ks"], T["qs"], sig=(i == 3 and sb == 1 and d == 1))
                            fr = []
                bv, av = v3(b, 256), v3(AT[:, h, :], 256)
                t1 = tt(av[0:64, :, 0:64], bv[0:64, :, 0:64], bc(triu[0:64, 0:64].unsqueeze(1), [64, 2, 64]), ALU.mult,
                        tl, T["ATz"])
                t2 = tt(av[:, :, 64:128], bv[:, :, 64:128], bc(triu[:, 64:128].unsqueeze(1), [128, 2, 64]), ALU.mult)
                t3 = vcopy(AT[:, h, 128:256], b[:, 128:256])
                mfree[bi] = [t3]
                T["AT%d" % h] = [t1, t2, t3]
        return f
    hook("v1", 2, gla_scores([0, 1]))
    hook("v2", 0, gla_scores([2, 3]))

    def evac_v(i):
        def f(p, done):
            r = [vcopy(v_t[:, tb, 512 * i:512 * i + 512], p[tb], done, T["yaT"][6]) for tb in range(2)]
            T["v%d" % i] = r
            return r
        return f

    for i in range(4):
        group("v%d" % i, w_in, KC, [(4096 + 512 * i, 512)], "tok", xth, xtl, h1, evac_v(i))

    ossq = small(8)

    def gla_out(h):
        def f():
            for cb in range(2):
                bi, b, fr = bank()
                mm(b, AT[:, h, 128 * cb:128 * cb + 128], v_t[:, 0, 512 * h:512 * h + 512], True, cb == 0, fr,
                   T["AT%d" % h], T["v%d" % h], sig=False)
                if cb == 1:
                    tl = mm(b, AT[:, h, 256:384], v_t[:, 1, 512 * h:512 * h + 512], False, True, sig=True)
                else:
                    queue["pe"][-1] = (queue["pe"][-1][0], queue["pe"][-1][1], True)
                    count["pe"] += 1
                    tl = (sem["pe"], count["pe"])
                o = o_t[:, cb, 512 * h:512 * h + 512]
                allks = [T["AT%d" % j] for j in range(4)]
                t = vcopy(o, b, tl, *allks)
                mfree[bi] = [t]
                j = cb * 4 + h
                T["o%d%d" % (cb, h)] = square(junk_o, o, ossq[:, j:j + 1], t, T["junk_ok"])
            T["go%d" % h] = tl
        return f
    junk_o = at(B + 4, [128, 512])

    def set_junk():
        T["junk_ok"] = T["qs"]
    hook("og0", 0, set_junk)
    for h in range(4):
        hook("og0", h, gla_out(h))

    def evac_og(i):
        def f(p, done):
            r = [act(og[:, tb, 512 * i:512 * i + 512], p[tb], ACT.Silu, done, T["b"], T["E"], T["eb"], T["y"]) for tb in range(2)]
            T["og%d" % i] = r
            return r
        return f

    for i in range(4):
        group("og%d" % i, w_in, KC, [(6144 + 512 * i, 512)], "tok", xth, xtl, h1, evac_og(i))

    def gla_rstd():
        T["or"], T["orok"] = rstd_of(ossq, 512, EPS, [T["o%d%d" % (c, h)] for c in range(2) for h in range(4)])
    hook("og1", 0, gla_rstd)

    def gla_gate(h):
        def f():
            for cb in range(2):
                j = cb * 4 + h
                o = o_t[:, cb, 512 * h:512 * h + 512]
                T["yb%d%d" % (cb, h)] = stt(o, o, T["or"][:, j:j + 1], og[:, cb, 512 * h:512 * h + 512], ALU.mult,
                                            ALU.mult, T["orok"], T["og%d" % h])
        return f
    hook("og1", 2, gla_gate(0))
    hook("og2", 2, gla_gate(1))
    hook("og3", 2, gla_gate(2))
    hook("mb0", 1, gla_gate(3))

    def gla_turn(k0):
        def f():
            to_features(o_t, lambda k: VT[:, 24 + k % 4:25 + k % 4], ybTh, ybTl, T.setdefault("ybT", {}), k0 + 4,
                        lambda k, tb: T["yb%d%d" % (tb, k // 4)],
                        [T["yb%d3" % cb] for cb in range(2)] + [T["go3"]], k0)
        return f
    for u in range(4):
        hook("mb1", u, gla_turn(4 * u))

    sig_b = at(DD, [128, KC, 256])
    for i in range(4):
        group("mb%d" % i, w_in, KC, [(10256 + 512 * i, 512)], "feat", xth, xtl, h1,
              evac_sig(sig_b, i, "sb", lambda: T["go3"]))

    mt = [at(B + 2 * i, [128, 512]) for i in range(2)]
    T["mg"] = {}

    def evac_pb(i):
        def f(p, done):
            r = []
            for b_ in range(2):
                c = slice(4 * i + 2 * b_, 4 * i + 2 * b_ + 2)
                m_ = v3(mt[b_], 256)
                t = tt(m_, v3(p[b_], 256), sig_b[:, c, :], ALU.mult, done, T["sb%d" % i], T.get("mt%d" % b_), T["qs"])
                r.append(t)
                t = tt(m_, m_, sig_a[:, c, :], ALU.add, t, T["ma_%d" % i])
                th = act(xth[:, c, :], m_, ACT.Copy, t, T["pe:mb3"])
                tl_ = tt(xtl[:, c, :], m_, xth[:, c, :].bitcast(F), ALU.subtract, th, T["pe:mb3"])
                T["mt%d" % b_] = tl_
                T["mg"][4 * i + 2 * b_] = T["mg"][4 * i + 2 * b_ + 1] = [th, tl_]
            return r
        return f

    for i in range(4):
        group("pb%d" % i, I["w_proj_b"][0], KC, [(512 * i, 512)], "feat", ybTh, ybTl, reader("ybT"), evac_pb(i))

    xx = at(C, [128, 2, D])
    memTh = at(M, [128, KC, 256], R)
    memTl = at(DD, [128, KC, 256], R)
    junkB = at(B, [128, D])
    junk_wo = at(B + 4, [128, 512])
    junk_xo = at(A + 4, [128, 512])
    junk_dn = at(C + 16, [128, 512])

    def mem_load():
        s = I["mem"][0].rearrange("(b p) d -> p b d", p=128)
        ok = [T["pe:pb0"], T["ybT"][15]]
        T["mem"] = [[t, t] for t in [load("pool", xx[:, tb, :], s[:, tb, :], *ok) for tb in range(2)]]
    hook("pb1", 0, mem_load)

    def mem_sums():
        T["gb1"] = load("pool", gb, on_all(I["post_norm_mix"][0]), T["pe:pb3"])
        T["mems"] = prenorm_sums(xx, junkB, T["mem"], [T["mt0"], T["mt1"]])

    def mem_scale():
        T["memh"] = prenorm_scale(xx, xx, *T["mems"], None)
    hook("wo0", 0, mem_sums)
    hook("wo0", 2, mem_scale)

    def mem_turn(k0):
        def f():
            turn(xx, gcols(44), "memT", T["memh"], [T["mt0"], T["mt1"]], memTh, memTl, k0, k0 + 4)
            if k0 == 12:
                s = I["x"][0].rearrange("(b p) d -> p b d", p=128)
                T["x"] = [load("pool", xx[:, tb, :], s[:, tb, :], T["memT"][15]) for tb in range(2)]
        return f
    for u in range(4):
        hook("wo1", u, mem_turn(4 * u))

    gb = at(G, [128, D])
    yA = at(A, [128, 2, D])
    part1 = small(8)
    for i in range(4):
        group("wo%d" % i, I["w_out"][0], KC, [(512 * i, 512)], "tok", xth, xtl, reader("mg"),
              tok_store(yA, i, lambda: T["pe:pb3"], part1, "sq1", gb, lambda: T["gb1"], junk=junk_wo,
                        junk_ok=lambda: T["junkB"]))

    kxT = at(G + 8, [128, 4, 256])
    vx = at(G + 12, [128, 2, 512])
    qxT = at(A, [128, 4, 256])
    px = at(A + 4, [128, 8, 256])
    pxT = at(B, [128, 8, 256])
    oxh = at(A + 12, [128, 4, 256], R)
    oxl = at(C + 16, [128, 4, 256], R)

    def norm1a():
        T["x1"] = postnorm(yA, part1, xx, "sq1", T["x"])
        T["x1s"] = prenorm_sums(xx, junkB, T["x1"], T["sq1"])

    def norm1b():
        T["x1h"] = prenorm_scale(xx, yA, *T["x1s"], T["x1"])

    def evac_kx(p, done):
        r = [vcopy(kxT[:, 2 * b_:2 * b_ + 2, :], v3(p[b_], 256), done, T["pe:pb3"]) for b_ in range(2)]
        T["kx"] = r
        return r

    def evac_vx(p, done):
        r = [vcopy(vx[:, tb, :], p[tb], done, T["pe:pb3"]) for tb in range(2)]
        T["vx"] = r
        return r

    def evac_qx(p, done):
        r = [vcopy(qxT[:, 2 * b_:2 * b_ + 2, :], v3(p[b_], 256), done, T["h2"][15]) for b_ in range(2)]
        T["qx"] = r
        return r

    group("xk", I["xa_wk"][0], KC, [(0, 512)], "feat", memTh, memTl, reader("memT"), evac_kx)
    hook("xk", 0, norm1a)
    hook("xk", 1, norm1b)
    hook("xk", 3, lambda: turn(yA, gcols(28), "h2", T["x1h"], T["pe:wo3"], k1=8))
    hook("xq", 0, lambda: turn(yA, gcols(28), "h2", T["x1h"], T["pe:wo3"], k0=8))
    group("xq", I["xa_wq"][0], KC, [(0, 512)], "feat", xth, xtl, reader("h2"), evac_qx)
    group("xv", I["xa_wv"][0], KC, [(0, 512)], "tok", memTh, memTl, reader("memT"), evac_vx)

    XS = 128.0 ** -0.5
    mxx, nmx, sx, rx = small(8), small(8), small(8), small(8)

    def xa_scores():
        tx = []
        for h in range(4):
            bi, b, fr = bank()
            for tb in range(2):
                tl = mm(b[:, 256 * tb:256 * tb + 256], qxT[:, h, 128 * tb:128 * tb + 128], kxT[:, h, :], True, True,
                        fr, T["qx"], T["kx"], sig=(tb == 1))
                fr = []
            t = reduce(mxx[:, 2 * h:2 * h + 2], v3(b, 256), ALU.max, tl)
            t = ts(nmx[:, 2 * h:2 * h + 2], mxx[:, 2 * h:2 * h + 2], -XS, ALU.mult, None, None, t)
            for tb in range(2):
                j = 2 * h + tb
                t2 = act(px[:, j, :], b[:, 256 * tb:256 * tb + 256], ACT.Exp, t, T["h2"][15], bias=nmx[:, j:j + 1],
                         scale=XS, accum=sx[:, j:j + 1])
            mfree[bi] = [t2]
            tx.append(t2)
        t = recip(rx, sx, tx)
        T["px"] = tt(px, px, bc(rx.unsqueeze(2), [128, 8, 256]), ALU.mult, t)
    hook("xv", 1, xa_scores)

    def xa_turn():
        T["pxT"] = []
        for h in range(4):
            bi, b, fr = bank()
            for mc in range(2):
                for tb in range(2):
                    tl = tr(b[:, 256 * mc + 128 * tb:256 * mc + 128 * tb + 128], px[:, 2 * h + tb, 128 * mc:128 * mc + 128],
                            fr, T["px"], sig=(mc == 1 and tb == 1))
                    fr = []
            t = vcopy(pxT[:, 2 * h:2 * h + 2, :], v3(b, 256), tl, T["h2"][15])
            mfree[bi] = [t]
            T["pxT"].append(t)
    hook("xv", 3, xa_turn)
    T["oxT"] = {}

    def xa_out():
        for h2 in range(0, 4, 2):
            bi, b, fr = bank()
            for j in range(2):
                for mc in range(2):
                    tl = mm(b[:, 256 * j:256 * j + 256], vx[:, mc, (h2 + j) * 128:(h2 + j + 1) * 128],
                            pxT[:, 2 * (h2 + j) + mc, :], mc == 0, mc == 1, fr, T["pxT"], T["vx"],
                            sig=(j == 1 and mc == 1))
                    fr = []
            th = act(oxh[:, h2:h2 + 2, :], v3(b, 256), ACT.Copy, tl)
            tl_ = tt(oxl[:, h2:h2 + 2, :], v3(b, 256), oxh[:, h2:h2 + 2, :].bitcast(F), ALU.subtract, th)
            mfree[bi] = [tl_]
            T["oxT"][h2] = T["oxT"][h2 + 1] = [th, tl_]
    hook("xo0", 0, xa_out)

    yM = at(M, [128, 2, D])
    part2 = small(8)
    for i in range(4):
        group("xo%d" % i, I["xa_wo"][0], 4, [(512 * i, 512)], "tok", oxh, oxl, reader("oxT"),
              tok_store(yM, i, lambda: T["pe:xv"], part2, "sq2", gb, lambda: T["gb2"], junk=junk_xo,
                        junk_ok=lambda: T["pxT"]))

    def gb2_load():
        T["gb2"] = load("pool", gb, on_all(I["post_norm_xa"][0]), T["x1"])
    hook("xq", 0, gb2_load)

    HF = FF // 256
    ach = at(G, [128, HF, 256], R)
    acl = at(G + 22, [128, HF, 256], R)
    cvt = [at(B + 4 * s, [128, 1024]) for s in range(2)]
    cv = [[cvt[s][:, 256 * j:256 * j + 256] for j in range(4)] for s in range(2)]
    gate_up = [[cvt[s][:, 512 * j:512 * j + 512] for j in range(2)] for s in range(2)]

    def norm2():
        T["x2"] = postnorm(yM, part2, xx, "sq2", T["x1"])
        sums = prenorm_sums(xx, junkB, T["x2"], [T["pe:xo0"]])
        th = prenorm_scale(xx, yA2, *sums, T["pe:xo3"])
        turn(yA2, gcols(60), "h3", th, T["pe:xq"])
    yA2 = at(A, [128, 2, D])
    T["acT"] = {}
    ngr = [0]

    def evac_up(half, i):
        def f(p, done):
            s = ngr[0] % 2
            ngr[0] += 1
            c = cv[s]
            cols = [half * HF + 2 * i, half * HF + 2 * i + 1, 44 + half * HF + 2 * i, 44 + half * HF + 2 * i + 1]
            ok = [T.get("cv%d" % s), T["h3"][15], T["vt2"]]
            r = []
            for b_ in range(2):
                for j in range(2):
                    q = 2 * b_ + j
                    t = act(c[q], p[b_][:, 256 * j:256 * j + 256], ACT.Identity, done, ok,
                            bias=VT[:, 128 + cols[q]:129 + cols[q]], scale=VT[:, 512 + cols[q]:513 + cols[q]])
                for j in range(2):
                    q = 2 * b_ + j
                    t1 = stt(c[q][:, 1:256], p[b_][:, 256 * j:256 * j + 255], VT[:, 384 + cols[q]:385 + cols[q]],
                             c[q][:, 1:256], ALU.mult, ALU.add, t)
                    t2 = stt(c[q][:, 2:256], p[b_][:, 256 * j:256 * j + 254], VT[:, 256 + cols[q]:257 + cols[q]],
                             c[q][:, 2:256], ALU.mult, ALU.add, t1)
                r.append(t2)
            cg = gate_up[s][0]
            cu = gate_up[s][1]
            t = act(cg, cg, ACT.Gelu_apprx_tanh, r[0])
            t = tt(cu, cg, cu, ALU.mult, t, r[1])
            k = slice(2 * i, 2 * i + 2)
            wok = [T["pe:xo3"], T["x2"]] if half == 0 else [T["pe:dn03"]]
            th = act(ach[:, k, :], v3(cu, 256), ACT.Copy, t, wok)
            tl_ = tt(acl[:, k, :], v3(cu, 256), ach[:, k, :].bitcast(F), ALU.subtract, th, wok)
            T["cv%d" % s] = tl_
            T["acT"][(half, 2 * i)] = T["acT"][(half, 2 * i + 1)] = [th, tl_]
            return r
        return f

    part3 = small(8)
    gb3 = at(B, [128, D])
    for half in range(2):
        for i in range(HF // 2):
            c0 = half * HF * 128 + 256 * i
            group("up%d_%d" % (half, i), I["ffn_w_up"][0], KC, [(c0, 256), (FF + c0, 256)], "feat", xth, xtl,
                  reader("h3"), evac_up(half, i))
        for i in range(4):
            group("dn%d%d" % (half, i), I["ffn_w_down"][0], HF, [(512 * i, 512)], "tok", ach, acl,
                  (lambda half: lambda k: T["acT"][(half, k)])(half),
                  tok_store(yA2, i, lambda: T["yA2"], part3, "sq3", gb3, lambda: T["gb3"], True, junk_dn,
                            lambda: T["pe:xo3"]) if half else tok_store(yA2, i, lambda: T["h3"][15]),
                  k_off=half * HF)
    hook("up0_0", 0, norm2)

    def load_sqrt():
        act(small(1), ones[:, 0:1], ACT.Sqrt, t_ones)
    hook("xo1", 0, load_sqrt)
    hook("dn13", 1, load_sqrt)
    hook("w22", 1, load_sqrt)


    def gb3_load():
        T["yA2"] = T["dn0"]
        T["gb3"] = load("pool", gb3, on_all(I["post_norm_ffn"][0]), T["cv0"], T["cv1"])
    hook("dn10", 1, gb3_load)

    w2 = I["w_in_2"][0]

    def norm3():
        T["x3"] = t = postnorm(yA2, part3, xx, "sq3", T["x2"])
        T["h4"] = {}
        to_features(xx, None, xth, xtl, T["h4"], KC, lambda k, tb: t[tb], T["pe:up1_10"])

    h4 = reader("h4")
    qi = at(A, [128, 2, 1024])
    qiT = at(A + 8, [128, 8, 256])
    kv = at(B, [128, 2, 512])
    kaT = at(B + 4, [128, 2, 256])
    score = at(B + 6, [128, 2, 256])
    amask = at(C + 16, [128, 2, 256])
    rt = [at(C + 18 + 0.5 * i, [128, 128]) for i in range(4)]
    ki2 = at(G, [128, 2, 128])
    kiT = at(G + 1, [128, 256])
    rl = [at(G + 2 + 2 * i, [128, 512]) for i in range(2)]
    top8 = at(G + 6, [128, 8])
    expa = at(G + 6.5, [128, 16])

    def rope(x3_, half, tb, col_c, col_s, n, ok):
        a, b = x3_[:, :, 0:half], x3_[:, :, half:2 * half]
        cs = bc(cst[:, col_c + tb * half:col_c + (tb + 1) * half].unsqueeze(1), [128, n, half])
        sn = bc(cst[:, col_s + tb * half:col_s + (tb + 1) * half].unsqueeze(1), [128, n, half])
        r_ = [v3(rt[i][:, 0:n * half], half) for i in range(4)]
        t0 = tt(r_[0], a, cs, ALU.mult, ok, T.get("rope"))
        t1 = tt(r_[1], b, sn, ALU.mult)
        t2 = tt(r_[2], b, cs, ALU.mult)
        t3 = tt(r_[3], a, sn, ALU.mult)
        t4 = tt(a, r_[0], r_[1], ALU.subtract, t1, t3)
        T["rope"] = tt(b, r_[2], r_[3], ALU.add, t3)
        return [t4, T["rope"]]

    def evac_small(p, done):
        r = []
        T["dtr"] = [tt(dt_[:, 16 * tb:16 * tb + 16], p[tb][:, 112:128], dtb, ALU.add, done, t_dtb) for tb in range(2)]
        for tb in range(2):
            t0 = vcopy(ki2[:, tb, 0:64], p[tb][:, 0:64], done)
            t1 = ts(widx[:, 16 * tb:16 * tb + 16], p[tb][:, 64:80], 1.0 / 32.0, ALU.mult, None, None)
            t2 = rope(ki2[:, tb:tb + 1, 0:64], 8, tb, C_CI, C_SI, 1, t0)
            T["ki%d" % tb] = vcopy(ki2[:, tb, 64:128], ki2[:, tb, 0:64], t2)
            r.append(t1)
        T["wi"] = r
        return r

    group("kiw", w2, KC, [(3584, 80), (6704, 48)], "tok", xth, xtl, h4, evac_small, chunk=16)
    hook("kiw", 0, norm3)

    def softplus():
        t = act(dtmp, dt_, ACT.Abs, T["dtr"])
        z = act(dtmp, dtmp, ACT.Exp, t, scale=-1.0)
        s_, w_, q_ = dl1, do1, dtm2
        t = ts(s_, dtmp, 2.0, ALU.add, None, None, z)
        t = recip(s_, s_, t)
        t = tt(s_, s_, dtmp, ALU.mult, t)
        t = tt(w_, s_, s_, ALU.mult, t)
        t = ts(q_, w_, 1.0 / 17.0, ALU.mult, None, None, t)
        for n in range(15, 1, -2):
            t = stt(q_, q_, 1.0 / n, w_, ALU.add, ALU.mult, t)
        t = stt(q_, q_, 1.0, s_, ALU.add, ALU.mult, t)
        d1 = q_
        t = ts(q_, q_, 2.0, ALU.mult, None, None, t)
        T["dt"] = t = stt(dt_, dt_, 0.0, d1, ALU.max, ALU.add, t)
        ta = act(expa, alog, ACT.Exp, t_alog)
        t = tt(v3(adt, 16), v3(dt_, 16), bc(expa.unsqueeze(1), [128, 2, 16]), ALU.mult, t, ta)
        T["adt"] = ts(adt, adt, -1.0, ALU.mult, None, None, t)
    hook("qi0", 0, softplus)

    def evac_qi(i):
        def f(p, done):
            r = []
            for tb in range(2):
                o = qi[:, tb, 512 * i:512 * i + 512]
                t = vcopy(o, p[tb], done, T["h4"][15])
                r.append(t)
                T["qi%d%d" % (i, tb)] = rope(v3(o, 64), 8, tb, C_CI, C_SI, 8, t)
            return r
        return f

    for i in range(2):
        group("qi%d" % i, w2, KC, [(2560 + 512 * i, 512)], "tok", xth, xtl, h4, evac_qi(i))

    def turn_ki():
        bi, b, fr = bank()
        for tb in range(2):
            tl = tr(b[:, tb * 128:tb * 128 + 128], ki2[:, tb, :], fr, T["ki0"], T["ki1"], sig=(tb == 1))
            fr = []
        T["kiT"] = vcopy(kiT, b[:, 0:256], tl)
        mfree[bi] = [T["kiT"]]
    hook("qi0", 2, turn_ki)

    def turn_qi(i):
        def f():
            for p2 in range(4 * i, 4 * i + 4, 2):
                bi, b, fr = bank()
                for j in range(2):
                    for tb in range(2):
                        tl = tr(b[:, 256 * j + 128 * tb:256 * j + 128 * tb + 128], qi[:, tb, (p2 + j) * 128:(p2 + j + 1) * 128],
                                fr, T["qi%d0" % i], T["qi%d1" % i], sig=(j == 1 and tb == 1))
                        fr = []
                t = vcopy(qiT[:, p2:p2 + 2, :], v3(b, 256), tl)
                mfree[bi] = [t]
                T["qiT%d" % p2] = T["qiT%d" % (p2 + 1)] = t
        return f
    hook("qi1", 1, turn_qi(0))
    hook("kv", 1, turn_qi(1))

    def index_scores(qb, q4):
        def f():
            nk = 128 * (qb + 1)
            bs = [bank(), bank()]
            tls = []
            for par in range(2):
                bi, b, fr = bs[par]
                for j in range(2):
                    h = 4 * q4 + 2 * j + par
                    p0 = 64 * par
                    tl = mm(b[:, 256 * j:256 * j + nk], qiT[p0:p0 + 64, h // 2, 128 * qb:128 * qb + 128],
                            kiT[p0:p0 + 64, 0:nk], True, True, fr, T["qiT%d" % (h // 2)], T["kiT"], sig=(j == 1))
                    fr = []
                tls.append(tl)
            for par in range(2):
                bi, b, fr = bs[par]
                r3 = v3(rl[par], 256)
                t = act(r3[:, :, 0:nk], v3(b, 256)[:, :, 0:nk], ACT.Relu, tls[par], T.get("rl%d" % par))
                mfree[bi] = [t]
                for j in range(2):
                    h = 4 * q4 + 2 * j + par
                    w_ = widx[:, 16 * qb + h:16 * qb + h + 1]
                    o = score[:, qb, 0:nk]
                    if h == 0:
                        t = ts(o, r3[:, j, 0:nk], w_, ALU.mult, None, None, t, T["wi"], T["h4"][15], T["x3"])
                    else:
                        t = stt(o, r3[:, j, 0:nk], w_, o, ALU.mult, ALU.add, t, T["sc%d" % qb])
                    T["sc%d" % qb] = t
                T["rl%d" % par] = t
        return f

    for n, (qb, q4) in enumerate([(0, 0), (0, 1), (0, 2), (0, 3), (1, 0), (1, 1), (1, 2), (1, 3)]):
        hook("kv" if n < 2 else "xb0" if n < 6 else "xb1", (n + 2) % 4, index_scores(qb, q4))

    def choose(qb, part):
        def f():
            nk = 128 * (qb + 1)
            s_ = score[:, qb, 0:nk]
            if part == 0:
                own = score[:, qb, 128 * qb:128 * qb + 128]
                T["w%d" % qb] = tt(own, own, m64, ALU.add, T["sc%d" % qb])
            t = T["w%d" % qb]
            for _ in range(4):
                t = put("dve", lambda e: e.max(top8, s_), [t])
                t = put("dve", lambda e: e.match_replace(s_, top8, s_, GONE), [t])
            if part == 1:
                am = amask[:, qb, 0:nk]
                t = ts(am, s_, -2.0e38, ALU.is_gt, -BIG, ALU.mult, t, T["rope"], T["sqdone"])
            T["w%d" % qb] = t
        return f
    hook("xb1", 2, choose(0, 0))
    hook("xb2", 2, choose(0, 1))
    hook("xb3", 2, choose(1, 0))
    hook("zs1", 0, choose(1, 1))

    def sqd():
        T["sqdone"] = T["sq3"][-1]
    hook("xb0", 0, sqd)

    def evac_kv(p, done):
        r = []
        for tb in range(2):
            t = vcopy(kv[:, tb, :], p[tb], done, T["x3"])
            r.append(t)
            T["kv%d" % tb] = rope(v3(kv[:, tb, 0:256], 128), 16, tb, C_CA, C_SA, 2, t) + [t]
        return r
    group("kv", w2, KC, [(1024, 512)], "tok", xth, xtl, h4, evac_kv)

    def turn_k():
        bi, b, fr = bank()
        for g in range(2):
            for tb in range(2):
                tl = tr(b[:, 256 * g + 128 * tb:256 * g + 128 * tb + 128], kv[:, tb, 128 * g:128 * g + 128], fr,
                        T["kv0"], T["kv1"], sig=(g == 1 and tb == 1))
                fr = []
        T["kaT"] = vcopy(kaT, v3(b, 256), tl)
        mfree[bi] = [T["kaT"]]
    hook("xb0", 1, turn_k)

    xb = at(M, [128, 16, 256])

    def evac_xb(i):
        def f(p, done):
            r = []
            for b_ in range(2):
                for j in range(2):
                    c = 4 * i + 2 * b_ + j
                    t = act(xb[:, c, :], p[b_][:, 256 * j:256 * j + 256], ACT.Identity, done, T["pe:dn13"],
                            bias=VT[:, 84 + c:85 + c], scale=VT[:, 640 + 48 + c:640 + 49 + c])
                for j in range(2):
                    c = 4 * i + 2 * b_ + j
                    for tap in range(1, 4):
                        wc = VT[:, 640 + 16 * (3 - tap) + c:640 + 16 * (3 - tap) + c + 1]
                        t = stt(xb[:, c, tap:256], p[b_][:, 256 * j:256 * j + 256 - tap], wc, xb[:, c, tap:256],
                                ALU.mult, ALU.add, t)
                r.append(t)
                c = 4 * i + 2 * b_
                T["xb%d" % c] = T["xb%d" % (c + 1)] = act(xb[:, c:c + 2, :], xb[:, c:c + 2, :], ACT.Silu, t)
            return r
        return f

    for i in range(4):
        group("xb%d" % i, w2, KC, [(4688 + 512 * i, 512)], "feat", xth, xtl, h4, evac_xb(i))

    xs = at(DD, [128, 2, 1024])
    xdt = at(DD + 8, [128, 2, 1024])
    cbm = at(M, [128, 4, 384])
    sr = at(M + 8, [128, 4, 384])
    Wm = at(G + 8, [128, 4, 384])
    zs = at(G, [128, 2, 1024])

    def turn_xs(i):
        def f():
            for c2 in range(4 * i, 4 * i + 4, 2):
                bi, b, fr = bank()
                for j in range(2):
                    for tb in range(2):
                        tl = tr(b[:, 256 * tb + 128 * j:256 * tb + 128 * j + 128], xb[:, c2 + j, 128 * tb:128 * tb + 128], fr,
                                T["xb%d" % c2], T["xb%d" % (c2 + 1)], sig=(j == 1 and tb == 1))
                        fr = []
                t = vcopy(xs[:, :, c2 * 128:c2 * 128 + 256], v3(b, 256), tl, T["pe:dn13"])
                mfree[bi] = [t]
                T["xsT%d" % c2] = tl
                T["xs%d" % (c2 // 2)] = t
        return f
    hook("xb1", 3, turn_xs(0))
    hook("xb2", 3, turn_xs(1))

    def ssd_inputs(tb):
        def f():
            d3 = bc(dt_[:, 16 * tb:16 * tb + 16].unsqueeze(2), [128, 16, 64])
            T["xdt%d" % tb] = tt(v3(xdt[:, tb, :], 64), v3(xs[:, tb, :], 64), d3, ALU.mult,
                                 [T["xs%d" % j] for j in range(4)], T["dt"])
            k3 = bc(dsk.unsqueeze(2), [128, 16, 64])
            T["ys%d" % tb] = tt(v3(xs[:, tb, :], 64), v3(xs[:, tb, :], 64), k3, ALU.mult, T["xdt%d" % tb], t_dsk)
        return f
    hook("xb3", 3, ssd_inputs(0))
    hook("q20", 1, ssd_inputs(1))

    def ssd_cb(gs):
        for g in gs:
            bi, b, fr = bank()
            bT_, cT_ = xb[:, 8 + g, :], xb[:, 12 + g, :]
            w_ = [T["xb%d" % (8 + g)], T["xb%d" % (12 + g)]]
            mm(b[:, 0:256], bT_[:, 0:128], cT_, True, True, fr, w_)
            tl = mm(b[:, 256:384], bT_[:, 128:256], cT_[:, 128:256], True, True, sig=True)
            t1 = tt(v3(b, 256)[:, :, 0:128].rearrange("p a b -> p a b"), v3(b, 256)[:, :, 0:128],
                    bc(triu.unsqueeze(1), [128, 2, 128]), ALU.mult, tl)
            t = vcopy(cbm[:, g, :], b[:, 0:384], t1, [T["xsT%d" % c] for c in (0, 2, 4, 6)])
            mfree[bi] = [t]
            T["cb%d" % g] = t
            T["cbpe"] = tl
    hook("q20", 2, lambda: ssd_cb((0, 1)))
    hook("q20", 3, lambda: ssd_cb((2, 3)))

    def ssd_steps(g):
        def f():
            r = []
            for j in range(4):
                h = 4 * g + j
                a0, a1 = adt[:, h:h + 1], adt[:, 16 + h:16 + h + 1]
                ok = [T["adt"], T["cbpe"], T.get("srpe")]
                r.append(ts(sr[:, j, 0:128], triu, a0, ALU.mult, None, None, ok))
                r.append(ts(sr[:, j, 128:256], ones, a0, ALU.mult, None, None, t_ones))
                r.append(ts(sr[:, j, 256:384], triu, a1, ALU.mult, None, None))
            T["sr"] = r
        return f

    def ssd_decays(g):
        def f():
            tw = []
            for j2 in range(0, 4, 2):
                bi, b, fr = bank()
                for j in range(2):
                    mm(b[:, 256 * j:256 * j + 256], gt, sr[:, j2 + j, 0:256], True, False, fr, T["sr"])
                    fr = []
                    tl = mm(b[:, 256 * j + 128:256 * j + 256], ones, sr[:, j2 + j, 256:384], False, True, sig=(j == 1))
                t = act(Wm[:, j2:j2 + 2, 0:256], v3(b, 256), ACT.Exp, tl, T.get("wpe"))
                mfree[bi] = [t]
                tw.append(t)
            bi, b, fr = bank()
            for j in range(4):
                tl = mm(b[:, 128 * j:128 * j + 128], gt, sr[:, j, 256:384], True, True, fr, sig=(j == 3))
                fr = []
            t = act(Wm[:, :, 256:384], v3(b, 128), ACT.Exp, tl, T.get("wpe"))
            mfree[bi] = [t]
            T["srpe"] = tl
            T["dec"] = tw + [t]
        return f

    def ssd_weigh(g):
        def f():
            T["W"] = tt(Wm, Wm, bc(cbm[:, g:g + 1, :], [128, 4, 384]), ALU.mult, T["dec"], T["cb%d" % g])
        return f

    def ssd_y(g):
        def f():
            bi, b, fr = bank()
            for j in range(4):
                h = 4 * g + j
                xd = lambda tb: xdt[:, tb, 64 * h:64 * h + 64]
                mm(b[:, 64 * j:64 * j + 64], Wm[:, j, 0:128], xd(0), True, True, fr, T["W"], T["xdt0"], T["xdt1"])
                fr = []
                mm(b[:, 256 + 64 * j:256 + 64 * j + 64], Wm[:, j, 128:256], xd(0), True, False)
                tl = mm(b[:, 256 + 64 * j:256 + 64 * j + 64], Wm[:, j, 256:384], xd(1), False, True, sig=(j == 3))
            T["wpe"] = tl
            y_ = xs[:, :, 256 * g:256 * g + 256]
            t = tt(y_, v3(b, 256), y_, ALU.add, tl, T["ys0"], T["ys1"])
            mfree[bi] = [t]
            T["y%d" % g] = t
        return f
    for n_, u_, fn in [
            ("q21", 0, ssd_steps(0)), ("q21", 1, ssd_decays(0)),
            ("q21", 2, ssd_weigh(0)), ("q21", 2, ssd_steps(1)), ("q21", 3, ssd_y(0)), ("q21", 3, ssd_decays(1)),
            ("zs0", 0, ssd_weigh(1)), ("zs0", 0, ssd_steps(2)), ("zs0", 1, ssd_y(1)), ("zs0", 1, ssd_decays(2)),
            ("zs0", 2, ssd_weigh(2)), ("zs0", 2, ssd_steps(3)), ("zs0", 3, ssd_y(2)), ("zs0", 3, ssd_decays(3)),
            ("zs1", 0, ssd_weigh(3)), ("zs1", 1, ssd_y(3))]:
        hook(n_, u_, fn)

    qa = at(A, [128, 2, 1024])
    qaT = at(A + 8, [128, 8, 256])
    pa = at(M, [128, 8, 256])
    paT = at(M + 8, [128, 2, 1024])
    oaT = at(A, [128, 8, 256])

    def evac_q2(i):
        def f(p, done):
            r = []
            for tb in range(2):
                o = qa[:, tb, 512 * i:512 * i + 512]
                t = vcopy(o, p[tb], done)
                r.append(t)
                T["qa%d%d" % (i, tb)] = rope(v3(o, 128), 16, tb, C_CA, C_SA, 4, t)
            return r
        return f

    for i in range(2):
        group("q2%d" % i, w2, KC, [(512 * i, 512)], "tok", xth, xtl, h4, evac_q2(i))

    def turn_q(i):
        def f():
            for p2 in range(4 * i, 4 * i + 4, 2):
                bi, b, fr = bank()
                for j in range(2):
                    for tb in range(2):
                        tl = tr(b[:, 256 * j + 128 * tb:256 * j + 128 * tb + 128], qa[:, tb, (p2 + j) * 128:(p2 + j + 1) * 128],
                                fr, T["qa%d0" % i], T["qa%d1" % i], sig=(j == 1 and tb == 1))
                        fr = []
                t = vcopy(qaT[:, p2:p2 + 2, :], v3(b, 256), tl)
                mfree[bi] = [t]
                T["qaT%d" % p2] = T["qaT%d" % (p2 + 1)] = t
                T["qatr"] = tl
        return f
    hook("q21", 1, turn_q(0))
    hook("zs0", 1, turn_q(1))

    amx, anm, asm, arc = small(8), small(8), small(8), small(8)

    def at_scores(qb):
        def f():
            nk = 128 * (qb + 1)
            te = []
            for h2 in range(0, 8, 2):
                bi, b, fr = bank()
                for j in range(2):
                    h = h2 + j
                    tl = mm(b[:, 256 * j:256 * j + nk], qaT[:, h, 128 * qb:128 * qb + 128], kaT[:, h // 4, 0:nk], True, True,
                            fr, T["qaT%d" % h], T["kaT"], sig=(j == 1))
                    fr = []
                o = pa[:, h2:h2 + 2, 0:nk]
                t = tt(o, v3(b, 256)[:, :, 0:nk], bc(amask[:, qb:qb + 1, 0:nk], [128, 2, nk]), ALU.add, tl, T["w%d" % qb],
                       T["W"], T.get("paT"), T["wpe"])
                mfree[bi] = [t]
                t = reduce(amx[:, h2:h2 + 2], o, ALU.max, t, T.get("arc"))
                t = ts(anm[:, h2:h2 + 2], amx[:, h2:h2 + 2], -XS, ALU.mult, None, None, t)
                for j in range(2):
                    h = h2 + j
                    te.append(act(pa[:, h, 0:nk], pa[:, h, 0:nk], ACT.Exp, t, bias=anm[:, h:h + 1], scale=XS,
                                  accum=asm[:, h:h + 1]))
            T["arc"] = recip(arc, asm, te)
            T["pa"] = tt(pa[:, :, 0:nk], pa[:, :, 0:nk], bc(arc.unsqueeze(2), [128, 8, nk]), ALU.mult, T["arc"])
        return f

    def at_turn(qb):
        def f():
            for kb in range(qb + 1):
                for h4_ in (0, 4):
                    bi, b, fr = bank()
                    for j in range(4):
                        tl = tr(b[:, 128 * j:128 * j + 128], pa[:, h4_ + j, 128 * kb:128 * kb + 128], fr, T["pa"], sig=(j == 3))
                        fr = []
                    t = vcopy(paT[:, kb, 128 * h4_:128 * h4_ + 512], b, tl, T.get("opv"))
                    mfree[bi] = [t]
            T["paTd"] = t
            T["paT"] = tl
        return f

    def at_out(qb):
        def f():
            for h4_ in (0, 4):
                bi, b, fr = bank()
                for j in range(4):
                    h = h4_ + j
                    g = h // 4
                    for kb in range(qb + 1):
                        tl = mm(b[:, 128 * j:128 * j + 128], kv[:, kb, 256 + 128 * g:256 + 128 * g + 128],
                                paT[:, kb, 128 * h:128 * h + 128], kb == 0, kb == qb, fr, T["paTd"], T["kv0"], T["kv1"],
                                sig=(j == 3 and kb == qb))
                        fr = []
                t = vcopy(oaT[:, h4_:h4_ + 4, 128 * qb:128 * qb + 128], v3(b, 128), tl, T["qatr"])
                mfree[bi] = [t]
                T["oa%d%d" % (qb, h4_ // 4)] = t
            T["opv"] = tl
        return f
    for (n_, u_), fn in zip([("zs1", 1), ("zs1", 3), ("za0", 0), ("za0", 1), ("za0", 3), ("za1", 0)],
                            [at_scores(0), at_turn(0), at_out(0), at_scores(1), at_turn(1), at_out(1)]):
        hook(n_, u_, fn)

    def evac_zs(i):
        def f(p, done):
            r = []
            for tb in range(2):
                o = zs[:, tb, 512 * i:512 * i + 512]
                r.append(act(o, p[tb], ACT.Silu, done, T["sc1"], T["w1"], T["adt"]))
            T["zs%d" % i] = r
            return r
        return f

    for i in range(2):
        group("zs%d" % i, w2, KC, [(3664 + 512 * i, 512)], "tok", xth, xtl, h4, evac_zs(i))

    gssq = small(8)
    junk_g = at(G + 8, [128, 256])

    def ssd_gate(i):
        def f():
            for tb in range(2):
                y_ = xs[:, tb, 512 * i:512 * i + 512]
                t = tt(y_, y_, zs[:, tb, 512 * i:512 * i + 512], ALU.mult, T["zs%d" % i], [T["y%d" % g] for g in range(4)])
                for g in (2 * i, 2 * i + 1):
                    T["gs%d%d" % (tb, g)] = square(junk_g, xs[:, tb, 256 * g:256 * g + 256],
                                                   gssq[:, 4 * tb + g:4 * tb + g + 1], t, T["wpe"])
        return f
    hook("za0", 0, ssd_gate(0))
    hook("za0", 2, ssd_gate(1))

    def ssd_norm():
        r, t = rstd_of(gssq, 256, LN_EPS, [T["gs%d%d" % (tb, g)] for tb in range(2) for g in range(4)])
        for tb in range(2):
            x4 = v3(xs[:, tb, :], 256)
            T["yn%d" % tb] = tt(x4, x4, bc(r[:, 4 * tb:4 * tb + 4].unsqueeze(2), [128, 4, 256]), ALU.mult, t)
    hook("za1", 1, ssd_norm)

    T["mix"] = {}
    zt = [at(G + 8 + 2 * i, [128, 512]) for i in range(2)]

    def evac_za(i):
        def f(p, done):
            r = []
            for b_ in range(2):
                c = slice(4 * i + 2 * b_, 4 * i + 2 * b_ + 2)
                t = act(zt[b_] if i else zk[b_], p[b_], ACT.Silu, done, T["gs13"] if i else T["wpe"], T["W"])
                r.append(t)
                T["za%d%d" % (i, b_)] = t
            return r
        return f
    zk = [at(G + 12 + 2 * i, [128, 512]) for i in range(2)]

    for i in range(2):
        group("za%d" % i, w2, KC, [(1536 + 512 * i, 512)], "feat", xth, xtl, h4, evac_za(i))

    def mix_attn():
        for i in range(2):
            for b_ in range(2):
                z = (zt if i else zk)[b_]
                c0 = 4 * i + 2 * b_
                c = slice(c0, c0 + 2)
                z3 = v3(z, 256)
                t = tt(z3, z3, oaT[:, c, :], ALU.mult, T["za%d%d" % (i, b_)], T["oa00"], T["oa01"], T["oa10"], T["oa11"])
                th = act(xth[:, c, :], z3, ACT.Copy, t, T["pe:za1"])
                tl_ = tt(xtl[:, c, :], z3, xth[:, c, :].bitcast(F), ALU.subtract, th, T["pe:za1"])
                T["mix"][c0] = T["mix"][c0 + 1] = [th, tl_]
        rr = {}
        to_features(xs, lambda k: VT[:, 76 + k:77 + k], xth[:, 8:16, :], xtl[:, 8:16, :], rr, 8,
                    lambda k, tb: T["yn%d" % tb], T["pe:za1"])
        for k in range(8):
            T["mix"][8 + k] = rr[k]
    hook("w20", 0, mix_attn)

    y5 = at(M, [128, 2, D])
    lg = at(DD, [128, D])
    lb = at(DD + 8, [128, D])
    bst = at(B, [128, 2, 24])

    def ln_loads():
        T["lg"] = load("pool", lg, on_all(I["ln_g_2"][0]), T["mix"][15])
        T["lb"] = load("pool", lb, on_all(I["ln_b_2"][0]), T["mix"][15])
    hook("w20", 1, ln_loads)

    def evac_w2(i):
        def f(p, done):
            r = []
            for tb in range(2):
                o = y5[:, tb, 512 * i:512 * i + 512]
                t = stt(o, xx[:, tb, 512 * i:512 * i + 512], ALPHA, p[tb], ALU.mult, ALU.add, done, T["x3"], T["opv"],
                        T["paT"])
                r.append(t)
                so = bst[:, tb, 6 * i:6 * i + 6]
                T["bs%d%d" % (tb, i)] = put("dve", lambda e, so=so, o=o: e.bn_stats(so, o), [t])
            return r
        return f

    for i in range(4):
        group("w2%d" % i, I["w_out_2"][0], KC, [(512 * i, 512)], "tok", xth, xtl, reader("mix"), evac_w2(i))

    run()

    o_dst = out_d[0].rearrange("(b p) d -> p b d", p=128)
    s_out = nc.alloc_semaphore("s_out")
    n_out = 0
    for tb in range(2):
        mv = small(2)
        s3 = bst[:, tb, :]
        t = put("dve", lambda e, mv=mv, s3=s3: e.bn_aggr(mv, s3), [T["bs%d%d" % (tb, i)] for i in range(4)])
        r, t = rstd_of(mv[:, 1:2], 1.0, LN_EPS, t)
        for hf in range(2):
            c = slice(1024 * hf, 1024 * hf + 1024)
            y_ = y5[:, tb, c]
            t1 = ts(y_, y_, mv[:, 0:1], ALU.subtract, r, ALU.mult, t)
            t1 = tt(y_, y_, lg[:, c], ALU.mult, t1, T["lg"])
            t1 = tt(y_, y_, lb[:, c], ALU.add, t1, T["lb"])
            d_ = o_dst[:, tb, c]
            put("sp", lambda e, d_=d_, y_=y_: e.dma_start(d_, y_).then_inc(s_out, 16), [t1], False)
            n_out += 16
    put("sp", None, [(s_out, n_out)], False)

    def play(name, e):
        for todo, fn, signal in queue[name]:
            for s, n in todo:
                e.wait_ge(s, n)
            if fn is None:
                continue
            ins = fn(e)
            if signal:
                ins.then_inc(sem[name], 1)

    with nc.Block() as block:
        @block.sync
        def _(e):
            play("sp", e)

        @block.scalar
        def _(e):
            play("act", e)

        @block.gpsimd
        def _(e):
            play("pool", e)

        @block.vector
        def _(e):
            play("dve", e)

        @block.tensor
        def _(e):
            play("pe", e)


_OUT = ((1, SEQ, D), "float32")


def kernel(**inputs):
    import concourse.bacc as bacc
    from concourse.bass_utils import run_bass_kernel_spmd

    nc = bacc.Bacc("TRN2", target_bir_lowering=False, num_devices=1)
    arrays, aps = {}, {}
    for name in inputs:
        a = np.ascontiguousarray(inputs[name])
        arrays[f"in_{name}"] = a
        aps[name] = nc.dram_tensor(f"in_{name}", a.shape, mybir.dt.from_np(a.dtype), kind="ExternalInput").ap()
    c = shape_constants()
    arrays["in_shape_constants"] = c
    cst = nc.dram_tensor("in_shape_constants", c.shape, F, kind="ExternalInput").ap()
    out = nc.dram_tensor("out_0", _OUT[0], mybir.dt.from_np(np.dtype(_OUT[1])), kind="ExternalOutput").ap()
    build(nc, aps, cst, out)
    r = run_bass_kernel_spmd(nc, [arrays], core_ids=[0])
    return r.results[0]["out_0"]
```

```python
import math

import numpy as np

import concourse.bass as bass
from concourse import mybir

F = mybir.dt.float32
R = mybir.dt.float32r
ALU = mybir.AluOpType
ACT = mybir.ActivationFunctionType
AX = mybir.AxisListType

SEQ = 256
D = 2048
KC = D // 128
FF = 5632
EPS = 1e-6
LN_EPS = 1e-5
ALPHA = 2.0 ** 0.25
BIG = 1.0e30
GONE = -3.0e38
TOPK = 64

KB = 1024
BASE = 16512

C_ID, C_TRIU, C_GT, C_M64, C_SCAN, C_CA, C_SA, C_CI, C_SI, C_END = 0, 128, 256, 384, 512, 768, 800, 832, 848, 864


def shape_constants():
    c = np.zeros((128, C_END), np.float32)
    i = np.arange(128)
    c[:, C_ID:C_ID + 128] = np.eye(128)
    c[:, C_TRIU:C_TRIU + 128] = i[None, :] >= i[:, None]
    c[:, C_GT:C_GT + 128] = i[:, None] > i[None, :]
    c[:64, C_M64 + 64:C_M64 + 128] = -BIG
    c[:, C_SCAN:C_SCAN + 256] = (np.arange(256) % 64 != 0)
    pos = np.arange(SEQ, dtype=np.float32)
    for rot, cc, cs in ((32, C_CA, C_SA), (16, C_CI, C_SI)):
        half = rot // 2
        inv = np.float32(500000.0) ** (-np.arange(half, dtype=np.float32) * np.float32(2.0) / np.float32(rot))
        ang = (pos[:, None] * inv.astype(np.float32)[None, :]).astype(np.float32)
        for tab, col in ((np.cos(ang), cc), (np.sin(ang), cs)):
            for tb in range(2):
                c[:, col + tb * half:col + (tb + 1) * half] = tab[tb * 128:(tb + 1) * 128]
    return c


def build(nc, I, cst_d, out_d):
    engines = ("pe", "dve", "act", "pool", "sp")
    queue = {e: [] for e in engines}
    sem = {e: nc.alloc_semaphore("s_" + e) for e in engines}
    count = dict.fromkeys(engines, 0)
    seen = {e: {} for e in engines}

    def tokens(w):
        if w is None:
            return []
        if isinstance(w, tuple) and len(w) == 2 and isinstance(w[1], int):
            return [w]
        return [p for x in w for p in tokens(x)]

    def put(e, fn, waits, signal=True):
        todo = []
        for s, n in tokens(waits):
            if seen[e].get(s.num, 0) < n:
                seen[e][s.num] = n
                todo.append((s, n))
        if signal:
            count[e] += 1
        queue[e].append((todo, fn, signal))
        return (sem[e], count[e]) if signal else None

    def tt(out, a, b, op, *w):
        return put("dve", lambda e: e.tensor_tensor(out, a, b, op), w)

    def ts(out, a, s1, op0, s2, op1, *w):
        if op1 is None:
            return put("dve", lambda e: e.tensor_scalar(out, a, s1, None, op0), w)
        return put("dve", lambda e: e.tensor_scalar(out, a, s1, s2, op0, op1), w)

    def stt(out, a, s, b, op0, op1, *w):
        return put("dve", lambda e: e.scalar_tensor_tensor(out=out, in0=a, scalar=s, in1=b, op0=op0, op1=op1), w)

    def vcopy(out, a, *w):
        return put("dve", lambda e: e.tensor_copy(out, a), w)

    def vset(out, v, *w):
        return put("dve", lambda e: e.memset(out, v), w)

    def recip(out, a, *w):
        return put("dve", lambda e: e.reciprocal(out, a), w)

    def reduce(out, a, op, *w):
        return put("dve", lambda e: e.tensor_reduce(out, a, AX.X, op), w)

    def act(out, a, func, *w, bias=0.0, scale=1.0, accum=None):
        if accum is None:
            return put("act", lambda e: e.activation(out, a, func, bias=bias, scale=scale), w)
        return put("act", lambda e: e.activation(out, a, func, bias=bias, scale=scale, accum_out=accum), w)

    last_junk = {}

    def square(junk, a, accum, *w):
        t = act(junk, a, ACT.Square, w, last_junk.get(junk.name), accum=accum)
        last_junk[junk.name] = t
        return t

    def mm(out, l, r, start, stop, *w, sig=False, share=False):
        return put("pe", lambda e: e.matmul(out, l, r, start=start, stop=stop, skip_group_check=share), w, sig)

    def tr(out, a, *w, sig=False):
        return put("pe", lambda e: e.transpose(out, a, ident), w, sig)

    def load(e, out, src, *w):
        nsem[0] += 1
        s = nc.alloc_semaphore(f"s_ld{nsem[0]}")
        put(e, lambda g: g.dma_start(out, src).then_inc(s, 16), w, False)
        return (s, 16)

    nsem = [0]

    nname = [0]

    def at(kb, shape, dt=F):
        nname[0] += 1
        t = nc.alloc_sbuf_tensor_at(f"b{nname[0]}", shape, dt, offset=BASE + int(kb * KB))
        return t[:, :] if len(shape) == 2 else t[:, :, :]

    RAW, SPL, XT, A, B, C, G, DD, M, K0 = 0, 24, 72, 104, 120, 128, 148, 164, 180, 196
    raw = [at(RAW + 8 * i, [128, 2048]) for i in range(3)]
    wh = [at(SPL + 16 * i, [128, 2048], R) for i in range(3)]
    wl = [at(SPL + 16 * i + 8, [128, 2048], R) for i in range(3)]
    xth = at(XT, [128, KC, 256], R)
    xtl = at(XT + 16, [128, KC, 256], R)
    cst = at(K0, [128, C_END])
    ident = cst[:, C_ID:C_ID + 128]
    triu = cst[:, C_TRIU:C_TRIU + 128]
    gt = cst[:, C_GT:C_GT + 128]
    m64 = cst[:, C_M64:C_M64 + 128]
    scan1 = cst[:, C_SCAN:C_SCAN + 256]
    ones = at(K0 + 3.5, [128, 128])
    VT = at(K0 + 4, [128, 6 * 128])
    st = at(K0 + 7, [128, 256])
    glrT = at(K0 + 8.125, [16, 256])
    dg = at(K0 + 9.25, [128, 256])
    dtb = at(K0 + 10.25, [128, 16])
    alog = at(K0 + 10.3125, [128, 16])
    dsk = at(K0 + 10.375, [128, 16])
    dt_ = at(K0 + 10.5, [128, 32])
    adt = at(K0 + 10.625, [128, 32])
    dtmp = at(K0 + 10.75, [128, 32])
    dtm2 = at(K0 + 10.875, [128, 32])
    widx = at(K0 + 11, [128, 32])
    dl1 = at(K0 + 11.125, [128, 32])
    do1 = at(K0 + 11.25, [128, 32])

    used = [0]

    def small(n):
        used[0] += n
        assert used[0] <= 256
        return st[:, used[0] - n:used[0]]

    ps = [[nc.alloc_psum_tensor(f"ps{s}{b}", [128, 512], F)[:, :] for b in range(2)] for s in range(2)]
    ms = [nc.alloc_psum_tensor(f"pm{b}", [128, 512], F)[:, :] for b in range(4)]
    mfree = [[], [], [], []]
    mnext = [0]

    def bank():
        b = mnext[0] % 4
        mnext[0] += 1
        return b, ms[b], mfree[b]

    def v3(ap, n):
        return ap.rearrange("p (a b) -> p a b", b=n)

    def bc(ap, shape):
        return ap.to_broadcast(shape)

    def keep_warm(n, *w):
        bi, b, fr = bank()
        for i in range(n):
            mm(b[:, 0:128], ident, ident, True, True, fr, w)

    groups = []

    def group(name, w, kcs, cols, kind, xh, xl, ready, evac, chunk=4, k_off=0, late=0):
        groups.append(dict(name=name, w=w, kcs=kcs, cols=cols, kind=kind, xh=xh, xl=xl, ready=ready,
                           evac=evac, chunk=chunk, k_off=k_off, late=late))

    T = {}
    hooks = {}

    def hook(name, unit, fn):
        hooks.setdefault((name, unit), []).append(fn)

    def run():
        units = []
        for gi, g in enumerate(groups):
            k = 0
            ui = 0
            while k < g["kcs"]:
                nk = min(g["chunk"], g["kcs"] - k)
                units.append((gi, ui, k, nk))
                k += nk
                ui += 1
        n_units = len(units)
        raw_sem = [nc.alloc_semaphore(f"s_raw{i}") for i in range(3)]
        raw_cnt = [0, 0, 0]
        landed, hi, lo, done = {}, {}, {}, {}
        set_free = [[], []]

        def dma(n):
            gi, ui, k, nk = units[n]
            g = groups[gi]
            s = n % 3
            nc_ = sum(c for _, c in g["cols"])
            dst = raw[s][:, 0:nk * nc_].rearrange("p (k c) -> p k c", c=nc_)
            w = [hi.get(n - 3), lo.get(n - 3)]
            o = 0
            k0 = g["k_off"] + k
            if n == 0:
                c0, c = g["cols"][0]
                landed[0] = [load("sp", dst[:, j, :], g["w"][j * 128:(j + 1) * 128, c0:c0 + c]) for j in range(nk)]
                return
            for c0, c in g["cols"]:
                src = g["w"][k0 * 128:(k0 + nk) * 128, c0:c0 + c].rearrange("(k p) c -> p k c", p=128)
                d = dst[:, :, o:o + c]
                put("sp", lambda e, d=d, src=src, s=s: e.dma_start(d, src).then_inc(raw_sem[s], 16), w, False)
                raw_cnt[s] += 16
                o += c
            landed[n] = (raw_sem[s], raw_cnt[s])

        def split_hi(n):
            gi, ui, k, nk = units[n]
            s = n % 3
            m = nk * sum(c for _, c in groups[gi]["cols"])
            hi[n] = act(wh[s][:, 0:m], raw[s][:, 0:m], ACT.Copy, landed[n], done.get(n - 3))

        def split_lo(n):
            gi, ui, k, nk = units[n]
            s = n % 3
            m = nk * sum(c for _, c in groups[gi]["cols"])
            lo[n] = tt(wl[s][:, 0:m], raw[s][:, 0:m], wh[s][:, 0:m].bitcast(F), ALU.subtract,
                       landed[n], hi[n], done.get(n - 3))

        def some_products(n, order, toks):
            gi, ui, k, nk = units[n]
            g = groups[gi]
            s = n % 3
            pset = ps[gi % 2]
            nc_ = sum(c for _, c in g["cols"])
            h3 = wh[s][:, 0:nk * nc_].rearrange("p (k c) -> p k c", c=nc_)
            l3 = wl[s][:, 0:nk * nc_].rearrange("p (k c) -> p k c", c=nc_)
            w = [hi[n], lo[n]] if n else []
            if ui == 0:
                w += [set_free[gi % 2]]
            for b, kk in order:
                if kk == nk // 2 and b == 0:
                    for fn in hooks.pop((g["name"], ui + 0.5), []):
                        fn()
                kg = k + kk
                w = w + [g["ready"](kg)]
                if n == 0:
                    w += [hi[0][kk], lo[0][kk]]
                final = kk == nk - 1
                if g["kind"] == "tok":
                    xs_ = slice(b * 128, b * 128 + 128)
                    trio = [(g["xh"][:, kg, xs_], h3[:, kk, :]), (g["xh"][:, kg, xs_], l3[:, kk, :]),
                            (g["xl"][:, kg, xs_], h3[:, kk, :])]
                    for q, (l, r) in enumerate(trio):
                        tok = mm(pset[b][:, 0:nc_], l, r, kg == 0 and q == 0, kg == g["kcs"] - 1 and q == 2, w,
                                 sig=final and q == 2)
                        w = []
                elif g["kind"] == "thin":
                    trio = [(h3[:, kk, :], g["xh"][:, kg, :]), (h3[:, kk, :], g["xl"][:, kg, :]),
                            (l3[:, kk, :], g["xh"][:, kg, :])]
                    for q, (l, r) in enumerate(trio):
                        tok = mm(pset[0][0:nc_, 0:256], l, r, kg == 0 and q == 0, kg == g["kcs"] - 1 and q == 2, w,
                                 sig=final and q == 2)
                        w = []
                else:
                    for f in range(2):
                        cs = slice((2 * b + f) * 128, (2 * b + f + 1) * 128)
                        o = pset[b][:, f * 256:(f + 1) * 256]
                        trio = [(h3[:, kk, cs], g["xh"][:, kg, :]), (h3[:, kk, cs], g["xl"][:, kg, :]),
                                (l3[:, kk, cs], g["xh"][:, kg, :])]
                        for q, (l, r) in enumerate(trio):
                            tok = mm(o, l, r, kg == 0 and q == 0 and f == 0, kg == g["kcs"] - 1 and q == 2, w,
                                     sig=final and f == 1 and q == 2, share=True)
                            w = []
                if final:
                    toks[b] = tok

        def products(n):
            gi, ui, k, nk = units[n]
            g = groups[gi]
            last_unit = k + nk == g["kcs"]
            banks[n] = {}
            first_, second = [(0, kk) for kk in range(nk)], [(1, kk) for kk in range(nk)]
            if n in held:
                some_products(n, first_, banks[n])
                if last_unit:
                    set_free[gi % 2] = g["evac"](ps[gi % 2], banks[n], (0,))
                return
            if g["kind"] == "thin":
                some_products(n, first_, banks[n])
            elif last_unit:
                some_products(n, first_, banks[n])
                if n - 1 in held:
                    cross = units[n - 1][0] != gi
                    if cross:
                        r0 = g["evac"](ps[gi % 2], banks[n], (0,))
                    some_products(n - 1, held[n - 1], banks[n - 1])
                    finish(n - 1)
                    if cross:
                        pi = units[n - 1][0]
                        set_free[pi % 2] += groups[pi]["evac"](ps[pi % 2], banks[n - 1], (1,))
                some_products(n, second, banks[n])
            else:
                some_products(n, [(b, kk) for kk in range(nk) for b in range(2)], banks[n])
            finish(n)
            if last_unit:
                if n - 1 in held and units[n - 1][0] != gi:
                    set_free[gi % 2] = r0 + g["evac"](ps[gi % 2], banks[n], (1,))
                else:
                    set_free[gi % 2] = g["evac"](ps[gi % 2], banks[n])

        def finish(n):
            tok = banks[n].get(1, banks[n][0])
            done[n] = tok
            T["pe:" + groups[units[n][0]]["name"]] = tok

        banks, held = {}, {}
        for n, (gi, ui, k, nk) in enumerate(units):
            if (groups[gi]["name"], ui) in (("xo2", 0), ("dn13", 4), ("w23", 2)):
                held[n] = [(1, kk) for kk in range(nk)]
        for n in range(min(3, n_units)):
            dma(n)
        def piece(j):
            return slice(512 * j, 512 * j + 512)

        def lo_piece(j):
            return tt(wl[0][:, piece(j)], raw[0][:, piece(j)], wh[0][:, piece(j)].bitcast(F), ALU.subtract,
                      landed[0][j], hi[0][j])

        hi[0] = [act(wh[0][:, piece(j)], raw[0][:, piece(j)], ACT.Copy, landed[0][j]) for j in range(4)]
        lo[0] = [lo_piece(0)]
        first[0]()
        lo[0] += [lo_piece(j) for j in range(1, 4)]
        first[1]()
        split_hi(1)
        split_lo(1)
        dma(3)
        dma(4)
        owed = None
        for n in range(n_units):
            gi, ui, k, nk = units[n]
            for fn in hooks.pop((groups[gi]["name"], "first" if ui == 0 else None), []):
                fn()
            if owed is not None:
                if owed not in hi:
                    split_hi(owed)
                split_lo(owed)
                if owed + 3 < n_units:
                    dma(owed + 3)
                owed = None
            late = k + nk == groups[gi]["kcs"] and groups[gi]["late"]
            if n + 2 < n_units and not late:
                split_hi(n + 2)
            for fn in hooks.pop((groups[gi]["name"], ui), []):
                fn()
            if late:
                products(n)
                if late < 3:
                    split_hi(n + 2)
            if late >= 2:
                owed = n + 2
            elif n + 2 < n_units:
                split_lo(n + 2)
                if n + 5 < n_units:
                    dma(n + 5)
            if not late:
                products(n)
        assert not hooks, hooks.keys()

    def rstd_of(ssq, n, eps, *w):
        k = ssq.shape[-1]
        a, b = small(k), small(k)
        t = ts(a, ssq, 1.0 / n, ALU.mult, eps, ALU.add, *w)
        t = act(b, a, ACT.Sqrt, t)
        c = small(k)
        t = recip(c, b, t)
        return c, t

    def to_features(src, gcol, dst_h, dst_l, ready, kcs, src_ok, dst_ok, k0=0, early=False):
        turned = {}

        def turn_chunks(k2, tbs):
            if k2 not in turned:
                turned[k2] = [bank(), None]
            bi, b, fr = turned[k2][0]
            for j in range(2):
                for tb in tbs:
                    o = b[:, j * 256 + tb * 128:j * 256 + tb * 128 + 128]
                    i_ = src[:, tb, (k2 + j) * 128:(k2 + j + 1) * 128]
                    sig = j == 1 and tb == 1
                    t = tr(o, i_, fr, src_ok(k2 + j, tb), sig=sig)
                    fr = []
                    if sig:
                        turned[k2][1] = t

        if early:
            for tb in range(2):
                for k2 in range(k0, kcs, 2):
                    turn_chunks(k2, [tb])
        for k2 in range(k0, kcs, 2):
            if not early:
                turn_chunks(k2, [0, 1])
            (bi, b, fr), last = turned[k2]
            if gcol is None:
                th = act(dst_h[:, k2:k2 + 2, :], v3(b, 256), ACT.Copy, last, dst_ok)
                tl = tt(dst_l[:, k2:k2 + 2, :], v3(b, 256), dst_h[:, k2:k2 + 2, :].bitcast(F), ALU.subtract, th, dst_ok)
                ready[k2] = ready[k2 + 1] = [th, tl]
            else:
                t0 = act(dst_h[:, k2, :], b[:, 0:256], ACT.Copy, last, dst_ok, scale=gcol(k2))
                t1 = act(dst_h[:, k2 + 1, :], b[:, 256:512], ACT.Copy, scale=gcol(k2 + 1))
                l0 = stt(dst_l[:, k2, :], b[:, 0:256], gcol(k2), dst_h[:, k2, :].bitcast(F), ALU.mult, ALU.subtract,
                         t1, dst_ok)
                tl = stt(dst_l[:, k2 + 1, :], b[:, 256:512], gcol(k2 + 1), dst_h[:, k2 + 1, :].bitcast(F), ALU.mult,
                         ALU.subtract)
                ready[k2] = [t0, l0]
                ready[k2 + 1] = [t1, tl]
            mfree[bi] = [tl]

    def half_sums(x, tb, hf, junk, ssq, ok, junk_ok):
        j = 2 * tb + hf
        c = slice(1024 * hf, 1024 * hf + 1024)
        return square(junk[:, c], x[:, tb, c], ssq[:, j:j + 1], ok, junk_ok)

    def scale_first(x, h, tb, r, t, h_ok):
        T["rstd%d" % tb] = r, t
        q = 2 if tb == 0 else 1
        th = []
        for c in range(0, 1024, 512 * q):
            th += [ts(h[:, tb, c:c + 512 * q], x[:, tb, c:c + 512 * q], r, ALU.mult, None, None, t, h_ok)] * q
        return th

    def scale_second(x, h, x_ok, th, h_ok):
        c = slice(1024, 2048)
        for tb in range(2):
            r, t = T["rstd%d" % tb]
            th[tb] += [ts(h[:, tb, c], x[:, tb, c], r, ALU.mult, None, None, t, x_ok[tb][1], h_ok)] * 2

    def sum_halves(ssq, tb, *w):
        s = small(1)
        return s, tt(s, ssq[:, 2 * tb:2 * tb + 1], ssq[:, 2 * tb + 1:2 * tb + 2], ALU.add, w)

    def prenorm_sums(x, junk, ok, junk_ok):
        ssq = small(4)
        t = [half_sums(x, tb, hf, junk, ssq, ok[tb][hf], junk_ok) for tb in range(2) for hf in range(2)]
        T["junkB"] = t
        return ssq, t

    def prenorm_tokens(x, h, ssq, t, h_ok):
        th = []
        for tb in range(2):
            s, t1 = sum_halves(ssq, tb, t[2 * tb:2 * tb + 2])
            r, t1 = rstd_of(s, D, EPS, t1)
            th.append([ts(h[:, tb, :], x[:, tb, :], r, ALU.mult, None, None, t1, h_ok)] * 4)
        return th

    def turn(h, gcol, key, ok, dst_ok, dst_h=None, dst_l=None, k0=0, k1=KC, early=False):
        T.setdefault(key, {})
        to_features(h, gcol, xth if dst_h is None else dst_h, xtl if dst_l is None else dst_l, T[key], k1,
                    lambda k, tb: ok[tb][k // 4], dst_ok, k0, early)

    def tok_store(y, i, y_ok, part=None, tag=None, g=None, g_ok=None, add=False, junk=None, junk_ok=None,
                  tail=None):
        c = slice(i * 512, (i + 1) * 512)

        def evac(p, done, blocks=(0, 1)):
            free, ready = [], []
            for tb in blocks:
                o = y[:, tb, c]
                if tail is not None:
                    tail(tb, None)
                if part is None:
                    t = T["dn0"] = vcopy(o, p[tb], done[tb], y_ok())
                    free.append(t)
                    ready.append(t)
                    continue
                acc = part[:, tb * 4 + i:tb * 4 + i + 1]
                if add:
                    t = tt(o, p[tb], o, ALU.add, done[tb], y_ok())
                    free.append(t)
                    t = square(junk, o, acc, t, junk_ok())
                    t2 = tt(o, o, g[:, c], ALU.mult, t, g_ok())
                else:
                    t = square(junk, p[tb], acc, done[tb], junk_ok())
                    t2 = tt(o, p[tb], g[:, c], ALU.mult, t, g_ok(), y_ok())
                    free.append(t2)
                if tail is not None:
                    tail(tb, [t, t2])
                ready += [t, t2]
            T.setdefault(tag, []).extend(ready)
            return free
        return evac

    def postnorm(y, part, x, tag, x_ok):
        ssq = small(2)
        t = reduce(ssq, v3(part, 4), ALU.add, T[tag])
        r, t = rstd_of(ssq, D, EPS, t)
        return [[stt(x[:, tb, 1024 * hf:1024 * hf + 1024], y[:, tb, 1024 * hf:1024 * hf + 1024], r[:, tb:tb + 1],
                     x[:, tb, 1024 * hf:1024 * hf + 1024], ALU.mult, ALU.add, t, x_ok) for hf in range(2)]
                for tb in range(2)]

    def entrance(y, part, x, tag, h):
        ok = T[tag] = [[None, None], [None, None]]
        ssq = small(4)
        sq, rs = {}, {}

        def half(tb, hf):
            c = slice(1024 * hf, 1024 * hf + 1024)
            ok[tb][hf] = stt(x[:, tb, c], y[:, tb, c], rs[tb][0], x[:, tb, c], ALU.mult, ALU.add, rs[tb][1])

        def square_half(tb, hf):
            sq[tb, hf] = half_sums(x, tb, hf, junkB, ssq, ok[tb][hf], T["pe:xv"])

        def root(s, *w):
            a, b = small(1), small(1)
            t = ts(a, s, 1.0 / D, ALU.mult, EPS, ALU.add, *w)
            return b, act(b, a, ACT.Sqrt, t)

        def inverse(b, t):
            c = small(1)
            return c, recip(c, b, t)

        def norm_root(tb):
            return root(*sum_halves(ssq, tb, sq[tb, 0], sq[tb, 1]))

        def scale(tb, r):
            T[tag + "h"][tb] = scale_first(x, h, tb, *inverse(*r), T["pe:xo3"])

        T[tag + "h"] = [None, None]

        def tail(tb, w):
            if w is None:
                if tb == 1:
                    square_half(0, 0)
                    half(0, 1)
                return
            s = small(1)
            r = root(s, reduce(s, part[:, 4 * tb:4 * tb + 4], ALU.add, w))
            if tb == 1:
                square_half(0, 1)
            rs[tb] = inverse(*r)
            half(tb, 0)
            if tb == 1:
                r0 = norm_root(0)
                square_half(1, 0)
                half(1, 1)
                square_half(1, 1)
                scale(0, r0)
                scale(1, norm_root(1))
                keep_warm(8)
                keep_warm(5, ok[1][0])
                keep_warm(3, ok[1][1])
        return tail

    def on_all(vec):
        return vec.partition_broadcast(128)

    vraw = at(B, [128, 6 * 128])
    t_id = load("act", ident, cst_d[:, 0:128])
    t_pn = load("act", vraw[0:16, 0:128], I["pre_norm_mix"][0].rearrange("(r p) -> r p", p=128))
    act(small(1), ident[:, 0:1], ACT.Sqrt, t_id)
    t_ones = vset(ones, 1.0)
    x_ap = at(DD, [128, 2, D])
    x_src = I["x"][0].rearrange("(b p) d -> p b d", p=128)
    t_x = [[load("sp", x_ap[:, tb, 1024 * hf:1024 * hf + 1024], x_src[:, tb, 1024 * hf:1024 * hf + 1024])
            for hf in range(2)] for tb in range(2)]

    tv = {}

    def vec_rows(e, tile, r0, src, n):
        t = load(e, vraw[r0:r0 + n, tile * 128:(tile + 1) * 128], src.rearrange("(r p) -> r p", p=128))
        tv.setdefault(tile, []).append(t)

    vec_rows("pool", 0, 16, I["gla_b_gate"][0], 8)
    vec_rows("pool", 0, 24, I["gla_norm_g"][0], 4)
    vec_rows("pool", 0, 28, I["pre_norm_xa"][0], 16)
    vec_rows("pool", 0, 44, I["mem_norm_g"][0], 16)
    vec_rows("pool", 0, 60, I["pre_norm_ffn"][0], 16)
    vec_rows("pool", 0, 76, I["ssd_norm_w_2"][0], 8)
    vec_rows("pool", 0, 84, I["conv_b_2"][0], 16)
    t_cst = load("pool", cst[:, 128:C_END], cst_d[:, 128:C_END])
    vec_rows("pool", 1, 0, I["ffn_conv_b"][0], 88)
    for j in range(3):
        vec_rows("pool", 2 + j, 0, I["ffn_conv_w"][0][j], 88)
    for j in range(4):
        vec_rows("pool", 5, 16 * j, I["conv_w_2"][0][j], 16)
    sgb8 = at(B + 4, [1, 1024])
    t_sgb = load("pool", sgb8, I["sg_b"][0].rearrange("(o g) t -> o (g t)", o=1))
    t_dtb = load("pool", dtb, on_all(I["dt_bias_2"][0]))
    t_alog = load("pool", alog, on_all(I["a_log_2"][0]))
    t_dsk = load("pool", dsk, on_all(I["d_skip_2"][0]))

    junk0 = at(M, [128, D])

    def first_vectors():
        bi, b, fr = bank()
        tl = put("pe", lambda e, b=b: e.transpose(b[:, 0:16], vraw[0:16, 0:128], ident[0:16, 0:16]), [t_pn, t_id])
        T["vt0"] = vcopy(VT[:, 0:16], b[:, 0:16], tl)
        mfree[bi] = [T["vt0"]]

    first_vectors()
    keep_warm(6)
    ssq0, t0 = prenorm_sums(x_ap, junk0, t_x, None)
    h_ap = at(G, [128, 2, D])
    th0 = []
    for tb in range(2):
        s_, t_ = sum_halves(ssq0, tb, t0[2 * tb:2 * tb + 2])
        th0.append(scale_first(x_ap, h_ap, tb, *rstd_of(s_, D, EPS, t_), t_id))

    def turn_vectors():
        bi, b, fr = bank()
        tl = put("pe", lambda e, b=b: e.transpose(b[:, 0:100], vraw[0:100, 0:128], ident[0:100, 0:100]), [fr, tv[0], t_pn])
        T["vt"] = vcopy(VT[:, 16:100], b[:, 16:100], tl)
        mfree[bi] = [T["vt"]]
        bi, b, fr = bank()
        for i in range(4):
            tl = put("pe", lambda e, b=b, i=i: e.transpose(b[:, 128 * i:128 * i + 88],
                                                           vraw[0:88, 128 * (i + 1):128 * (i + 2)], ident[0:88, 0:88]),
                     [fr, tv[i + 1]])
        t = vcopy(v3(VT[:, 128:640], 128)[:, :, 0:88], v3(b, 128)[:, :, 0:88], tl)
        mfree[bi] = [t]
        bi, b, fr = bank()
        tl = put("pe", lambda e, b=b: e.transpose(b[:, 0:64], vraw[0:64, 640:768], ident[0:64, 0:64]),
                 [fr, tv[5], t_cst])
        T["vt2"] = vcopy(VT[:, 640:704], b[:, 0:64], tl)
        mfree[bi] = [T["vt2"]]
    hook("vs0", 2, turn_vectors)

    def gcols(c0):
        return lambda k: VT[:, c0 + k:c0 + k + 1]

    def first_turn():
        turn(h_ap, gcols(0), "h1", th0, T["vt0"], k1=4, early=True)

    def second_turn():
        turn(h_ap, gcols(0), "h1", th0, T["vt0"], k0=4, k1=8, early=True)
        scale_second(x_ap, h_ap, t_x, th0, None)
    first = [first_turn, second_turn]
    hook("vs0", 1, lambda: turn(h_ap, gcols(0), "h1", th0, T["vt0"], k0=8))

    h1 = lambda k: T["h1"][k]
    w_in = I["w_in"][0]

    def reader(key):
        return lambda k: T[key][k]

    vs = at(A, [128, 2, 1024])
    uT = at(A + 8, [128, 8, 256])
    sgr = at(C + 16, [128, 8, 128])
    swT = at(G + 8, [128, 8, 128])
    lng = at(G, [128, 1024])
    lnb = at(G + 4, [128, 1024])
    yaTh = at(C, [128, 8, 256], R)
    yaTl = at(C + 8, [128, 8, 256], R)
    yaf = [at(DD + 2 * i, [128, 512]) for i in range(2)]

    def evac_vs(i):
        def f(p, done):
            r = [act(vs[:, tb, i * 512:(i + 1) * 512], p[tb], ACT.Gelu, done[tb]) for tb in range(2)]
            T["vs%d" % i] = r
            return r
        return f

    def evac_u(i):
        def f(p, done):
            r = [act(uT[:, 4 * i + 2 * b_:4 * i + 2 * b_ + 2, :], v3(p[b_], 256), ACT.Gelu, done[b_]) for b_ in range(2)]
            T["u%d" % i] = r
            return r
        return f

    for i in range(2):
        group("vs%d" % i, w_in, KC, [(1024 + 512 * i, 512)], "tok", xth, xtl, h1, evac_vs(i))
    for i in range(2):
        group("u%d" % i, w_in, KC, [(512 * i, 512)], "feat", xth, xtl, h1, evac_u(i))

    def sg_loads():
        T["lng"] = load("pool", lng, on_all(I["sg_ln_g"][0]), T["pe:vs0"])
        T["lnb"] = load("pool", lnb, on_all(I["sg_ln_b"][0]), T["pe:vs0"])
        T["sgr"] = load("pool", sgr, I["sg_w"][0].rearrange("g t s -> t g s"))
    hook("vs1", 0, sg_loads)

    def sg_turn():
        for g0 in (0, 4):
            bi, b, fr = bank()
            for g in range(4):
                tl = tr(b[:, g * 128:(g + 1) * 128], sgr[:, g0 + g, :], fr, T["sgr"], sig=(g == 3))
                fr = []
            t = tt(swT[:, g0:g0 + 4, :], v3(b, 128), bc(triu.unsqueeze(1), [128, 4, 128]), ALU.mult, tl, T["pe:vs0"])
            mfree[bi] = [t]
            T["swT%d" % (g0 // 4)] = t
    hook("vs1", 3, sg_turn)

    stats = at(DD + 4, [128, 2, 12])

    def sg_norm(tb):
        def f():
            tt_ = []
            for i in range(2):
                o = stats[:, tb, 6 * i:6 * i + 6]
                a_ = vs[:, tb, i * 512:(i + 1) * 512]
                tt_.append(put("dve", lambda e, o=o, a_=a_: e.bn_stats(o, a_), [T["vs0"], T["vs1"]]))
            mv = small(2)
            s3 = stats[:, tb, :]
            t = put("dve", lambda e, mv=mv, s3=s3: e.bn_aggr(mv, s3), [tt_])
            r, t2 = rstd_of(mv[:, 1:2], 1.0, EPS, t)
            t3 = ts(vs[:, tb, :], vs[:, tb, :], mv[:, 0:1], ALU.subtract, r, ALU.mult, t2)
            t4 = tt(vs[:, tb, :], vs[:, tb, :], lng, ALU.mult, t3, T["lng"])
            T["vsn%d" % tb] = tt(vs[:, tb, :], vs[:, tb, :], lnb, ALU.add, t4, T["lnb"])
        return f
    hook("u0", 1, sg_norm(0))
    hook("u0", 3, sg_norm(1))

    def sg_mix():
        T["yaT"] = {}
        for g0 in range(0, 8, 2):
            bi, b, fr = bank()
            for j in range(2):
                for n in range(2):
                    o = b[:, j * 256 + n * 128:j * 256 + n * 128 + 128]
                    g = g0 + j
                    mm(o, vs[:, n, g * 128:(g + 1) * 128], swT[:, g, :], True, False, fr,
                       T["vsn0"], T["vsn1"], T["swT0"], T["swT1"])
                    fr = []
                    tl = mm(o, ones[0:1, :], sgb8[0:1, g * 128:(g + 1) * 128], False, True, t_ones, t_sgb,
                            sig=(j == 1 and n == 1))
            i = (g0 // 2) % 2
            t = tt(yaf[i], b, uT[:, g0:g0 + 2, :].rearrange("p a b -> p (a b)"), ALU.mult, tl, T["u0"], T["u1"],
                   T.get("yaf%d" % i))
            mfree[bi] = [t]
            th = act(yaTh[:, g0:g0 + 2, :], v3(yaf[i], 256), ACT.Copy, t)
            T["yaf%d" % i] = tl_ = tt(yaTl[:, g0:g0 + 2, :], v3(yaf[i], 256), yaTh[:, g0:g0 + 2, :].bitcast(F),
                                      ALU.subtract, th)
            T["yaT"][g0] = T["yaT"][g0 + 1] = [th, tl_]
    hook("ma0", 2, sg_mix)

    sig_a = at(M, [128, KC, 256])

    def evac_sig(dst, i, tag, ok):
        def f(p, done):
            r = [act(dst[:, 4 * i + 2 * b_:4 * i + 2 * b_ + 2, :], v3(p[b_], 256), ACT.Sigmoid, done[b_], ok())
                 for b_ in range(2)]
            T[tag + str(i)] = r
            return r
        return f

    for i in range(4):
        group("ma%d" % i, w_in, KC, [(8208 + 512 * i, 512)], "feat", xth, xtl, h1,
              evac_sig(sig_a, i, "sa", lambda: None))

    def evac_pa(i):
        def f(p, done):
            r = []
            for b_ in range(2):
                o = sig_a[:, 4 * i + 2 * b_:4 * i + 2 * b_ + 2, :]
                r.append(tt(o, v3(p[b_], 256), o, ALU.mult, done[b_], T["sa%d" % i]))
            T["ma_%d" % i] = r
            return r
        return f

    for i in range(4):
        group("pa%d" % i, I["w_proj_a"][0], 8, [(512 * i, 512)], "feat", yaTh, yaTl, reader("yaT"), evac_pa(i))

    qT = at(A, [128, 8, 256])
    kT = at(A + 8, [128, 8, 256])
    bT = at(B, [128, 8, 256])
    E = at(C, [128, 8, 640])
    tmpG = at(G, [128, 2048])
    wg2 = at(G + 8, [16, 1024])
    v_t = at(DD, [128, 2, D])
    og = at(G, [128, 2, D])
    AT = at(A + 8, [128, 4, 512])
    o_t = at(C, [128, 2, D])
    ybTh = at(A, [128, KC, 256], R)
    ybTl = at(G, [128, KC, 256], R)
    EO = [0, 64, 192, 384]

    def evac_glr(p, done):
        t = T["glrT"] = vcopy(glrT, p[0][0:16, 0:256], done[0])
        T["wg2"] = load("pool", wg2, I["gla_w_gate2"][0], T["swT0"], T["swT1"], T["pe:ma1"])
        return t

    group("glr", w_in, KC, [(8192, 16)], "thin", xth, xtl, h1, evac_glr, chunk=16)

    def gate2(d2):
        def f():
            bi, b, fr = bank()
            for j in range(2):
                tl = mm(b[:, 256 * j:256 * j + 256], wg2[0:16, (d2 + j) * 128:(d2 + j + 1) * 128], glrT, True, True,
                        fr, T["glrT"], T["wg2"], sig=(j == 1))
                fr = []
            for j in range(2):
                t = ts(bT[:, d2 + j, :], b[:, 256 * j:256 * j + 256], VT[:, 16 + d2 + j:17 + d2 + j], ALU.add, None,
                       None, tl, T["pe:ma1"], T["vt"])
            T.setdefault("y", []).append(t)
            mfree[bi] = [t]
        return f
    for i, u in enumerate((0.5, 1, 1.5, 2)):
        hook("q0", u, gate2(2 * i))
    bT2 = bT.rearrange("p a b -> p (a b)")

    def gate_log():
        t = act(tmpG, bT2, ACT.Abs, T["y"], T["pe:pa0"])
        t = act(tmpG, tmpG, ACT.Exp, t, scale=-1.0)
        T["log"] = act(tmpG, tmpG, ACT.Ln, t, bias=1.0)
    hook("q0", 2, gate_log)

    def gate_la():
        t = stt(bT2, bT2, 0.0, tmpG, ALU.min, ALU.subtract, T["log"])
        T["la"] = ts(bT2, bT2, 1.0 / 16.0, ALU.mult, -1.0, ALU.max, t)
    hook("q1", 0, gate_la)

    def gate_scan():
        tb_ = []
        for d in range(8):
            o, i_ = tmpG[:, d * 256:(d + 1) * 256], bT[:, d, :]
            tb_.append(put("dve", lambda e, o=o, i_=i_: e.tensor_tensor_scan(o, scan1, i_, 0.0, ALU.mult, ALU.add),
                           [T["la"], t_cst]))
        T["b"] = tb_
    hook("q1", 1, gate_scan)

    def gate_spans():
        b3 = v3(tmpG, 256)
        tb_ = T["b"]
        prev = None
        for i in range(4):
            own = ts(E[:, :, EO[i] + 64 * i:EO[i] + 64 * i + 64], b3[:, :, 64 * i:64 * i + 64], -1.0, ALU.mult, None, None,
                     tb_, T["pe:pa3"])
            if i:
                last = b3[:, :, 64 * i - 1:64 * i]
                prev = tt(E[:, :, EO[i]:EO[i] + 64 * i], E[:, :, EO[i - 1]:EO[i - 1] + 64 * i],
                          bc(last, [128, 8, 64 * i]), ALU.add, prev)
                prev = [prev, own]
            else:
                prev = own
        T["spans"] = prev
    hook("q1", 2, gate_spans)

    def gate_exp():
        T["eb"] = act(bT.rearrange("p a b -> p (a b)"), tmpG, ACT.Exp, T["b"], T["spans"])

    def gate_exp_spans(d):
        def f():
            T["E"] = act(E[:, d:d + 4, :], E[:, d:d + 4, :], ACT.Exp, T["spans"])
        return f
    hook("k0", 0, gate_exp_spans(0))
    hook("k0", 2, gate_exp_spans(4))
    hook("q1", 3, gate_exp)

    def evac_q(i):
        def f(p, done):
            r = [vcopy(qT[:, 4 * i + 2 * b_:4 * i + 2 * b_ + 2, :], v3(p[b_], 256), done[b_], T["pe:pa3"])
                 for b_ in range(2)]
            T["q%d" % i] = r
            return r
        return f

    def evac_k(i):
        def f(p, done):
            r = [vcopy(kT[:, 4 * i + 2 * b_:4 * i + 2 * b_ + 2, :], v3(p[b_], 256), done[b_]) for b_ in range(2)]
            T["k%d" % i] = r
            return r
        return f

    for i in range(2):
        group("q%d" % i, w_in, KC, [(2048 + 512 * i, 512)], "feat", xth, xtl, h1, evac_q(i))
    for i in range(2):
        group("k%d" % i, w_in, KC, [(3072 + 512 * i, 512)], "feat", xth, xtl, h1, evac_k(i))

    def gate_q():
        q2 = qT.rearrange("p a b -> p (a b)")
        T["qs"] = stt(q2, q2, 1.0 / 16.0, bT.rearrange("p a b -> p (a b)"), ALU.mult, ALU.mult, T["eb"], T["q0"], T["q1"])
    hook("k0", 1, gate_q)

    def gate_k(part):
        def f():
            T.setdefault("ks", []).extend(
                tt(E[:, :, EO[i]:EO[i] + 64 * (i + 1)], E[:, :, EO[i]:EO[i] + 64 * (i + 1)],
                   kT[:, :, 0:64 * (i + 1)], ALU.mult, T["E"], T["k0"], T["k1"]) for i in part)
            if 3 in part:
                z = AT.rearrange("p h (a b) -> p (h a) b", b=256)[64:128, :, 0:64]
                T["ATz"] = vset(z, 0.0, T["ks"])
        return f
    hook("v0", 1, gate_k([0, 1, 2]))
    hook("v0", 3, gate_k([3]))

    def gla_scores(hs):
        def f():
            for h in hs:
                bi, b, fr = bank()
                tl = None
                for i in range(4):
                    for sb in range((i // 2) + 1):
                        rows_ = min(64 * (i + 1) - 128 * sb, 128)
                        o = b[0:rows_, 256 * sb + 64 * (i - 2 * sb):256 * sb + 64 * (i - 2 * sb) + 64]
                        for d in range(2):
                            e0 = EO[i] + 128 * sb
                            tl = mm(o, E[:, 2 * h + d, e0:e0 + rows_], qT[:, 2 * h + d, 64 * i:64 * i + 64], d == 0, d == 1,
                                    fr, T["ks"], T["qs"], sig=(i == 3 and sb == 1 and d == 1))
                            fr = []
                bv, av = v3(b, 256), v3(AT[:, h, :], 256)
                t1 = tt(av[0:64, :, 0:64], bv[0:64, :, 0:64], bc(triu[0:64, 0:64].unsqueeze(1), [64, 2, 64]), ALU.mult,
                        tl, T["ATz"])
                t2 = tt(av[:, :, 64:128], bv[:, :, 64:128], bc(triu[:, 64:128].unsqueeze(1), [128, 2, 64]), ALU.mult)
                t3 = vcopy(AT[:, h, 128:256], b[:, 128:256])
                mfree[bi] = [t3]
                T["AT%d" % h] = [t1, t2, t3]
        return f
    hook("v1", 2, gla_scores([0, 1]))
    hook("v2", 0, gla_scores([2, 3]))

    def evac_v(i):
        def f(p, done):
            r = [vcopy(v_t[:, tb, 512 * i:512 * i + 512], p[tb], done[tb], T["yaT"][6]) for tb in range(2)]
            T["v%d" % i] = r
            return r
        return f

    for i in range(4):
        group("v%d" % i, w_in, KC, [(4096 + 512 * i, 512)], "tok", xth, xtl, h1, evac_v(i))

    ossq = small(8)

    def gla_out(h):
        def f():
            for cb in range(2):
                bi, b, fr = bank()
                tl = mm(b, AT[:, h, 128 * cb:128 * cb + 128], v_t[:, 0, 512 * h:512 * h + 512], True, cb == 0, fr,
                        T["AT%d" % h], T["v%d" % h], sig=(cb == 0))
                if cb == 1:
                    tl = mm(b, AT[:, h, 256:384], v_t[:, 1, 512 * h:512 * h + 512], False, True, sig=True)
                o = o_t[:, cb, 512 * h:512 * h + 512]
                allks = [T["AT%d" % j] for j in range(4)]
                t = vcopy(o, b, tl, *allks)
                mfree[bi] = [t]
                j = cb * 4 + h
                T["o%d%d" % (cb, h)] = square(junk_o, o, ossq[:, j:j + 1], t, T["qs"])
            T["go%d" % h] = tl
        return f
    junk_o = at(B + 4, [128, 512])

    for h in range(4):
        hook("og0", h, gla_out(h))

    def evac_og(i):
        def f(p, done):
            r = [act(og[:, tb, 512 * i:512 * i + 512], p[tb], ACT.Silu, done[tb], T["b"], T["E"], T["eb"], T["y"]) for tb in range(2)]
            T["og%d" % i] = r
            return r
        return f

    for i in range(4):
        group("og%d" % i, w_in, KC, [(6144 + 512 * i, 512)], "tok", xth, xtl, h1, evac_og(i))

    def gla_rstd():
        T["or"], T["orok"] = rstd_of(ossq, 512, EPS, [T["o%d%d" % (c, h)] for c in range(2) for h in range(4)])
    hook("og1", 0, gla_rstd)

    def gla_gate(h):
        def f():
            for cb in range(2):
                j = cb * 4 + h
                o = o_t[:, cb, 512 * h:512 * h + 512]
                T["yb%d%d" % (cb, h)] = stt(o, o, T["or"][:, j:j + 1], og[:, cb, 512 * h:512 * h + 512], ALU.mult,
                                            ALU.mult, T["orok"], T["og%d" % h])
        return f
    hook("og1", 2, gla_gate(0))
    hook("og2", 2, gla_gate(1))
    hook("og3", 2, gla_gate(2))
    hook("mb0", 1, gla_gate(3))

    def gla_turn(k0):
        def f():
            to_features(o_t, lambda k: VT[:, 24 + k % 4:25 + k % 4], ybTh, ybTl, T.setdefault("ybT", {}), k0 + 4,
                        lambda k, tb: T["yb%d%d" % (tb, k // 4)],
                        [T["yb%d3" % cb] for cb in range(2)] + [T["go3"]], k0)
        return f
    for u in range(4):
        hook("mb1", u, gla_turn(4 * u))

    sig_b = at(DD, [128, KC, 256])
    for i in range(4):
        group("mb%d" % i, w_in, KC, [(10256 + 512 * i, 512)], "feat", xth, xtl, h1,
              evac_sig(sig_b, i, "sb", lambda: T["go3"]))

    mt = [at(B + 2 * i, [128, 512]) for i in range(2)]
    T["mg"] = {}

    def evac_pb(i):
        def f(p, done):
            r = []
            for b_ in range(2):
                c = slice(4 * i + 2 * b_, 4 * i + 2 * b_ + 2)
                m_ = v3(mt[b_], 256)
                t = tt(m_, v3(p[b_], 256), sig_b[:, c, :], ALU.mult, done[b_], T["sb%d" % i], T.get("mt%d" % b_), T["qs"])
                r.append(t)
                t = tt(m_, m_, sig_a[:, c, :], ALU.add, t, T["ma_%d" % i])
                th = act(xth[:, c, :], m_, ACT.Copy, t, T["pe:mb3"])
                tl_ = tt(xtl[:, c, :], m_, xth[:, c, :].bitcast(F), ALU.subtract, th, T["pe:mb3"])
                T["mt%d" % b_] = tl_
                T["mg"][4 * i + 2 * b_] = T["mg"][4 * i + 2 * b_ + 1] = [th, tl_]
            return r
        return f

    for i in range(4):
        group("pb%d" % i, I["w_proj_b"][0], KC, [(512 * i, 512)], "feat", ybTh, ybTl, reader("ybT"), evac_pb(i))

    xx = at(C, [128, 2, D])
    memTh = at(M, [128, KC, 256], R)
    memTl = at(DD, [128, KC, 256], R)
    junkB = at(B, [128, D])
    junk_wo = at(B + 4, [128, 512])
    junk_xo = at(A + 4, [128, 512])
    junk_dn = at(C + 16, [128, 512])

    def mem_load():
        s = I["mem"][0].rearrange("(b p) d -> p b d", p=128)
        ok = [T["pe:pb0"], T["ybT"][15]]
        T["mem"] = [[t, t] for t in [load("pool", xx[:, tb, :], s[:, tb, :], *ok) for tb in range(2)]]
    hook("pb1", 0, mem_load)

    def mem_sums():
        T["gb1"] = load("pool", gb, on_all(I["post_norm_mix"][0]), T["pe:pb3"])
        T["mems"] = prenorm_sums(xx, junkB, T["mem"], [T["mt0"], T["mt1"]])

    def mem_scale():
        T["memh"] = prenorm_tokens(xx, xx, *T["mems"], None)
    hook("wo0", 0, mem_sums)
    hook("wo0", 2, mem_scale)

    def mem_turn(k0):
        def f():
            turn(xx, gcols(44), "memT", T["memh"], [T["mt0"], T["mt1"]], memTh, memTl, k0, k0 + 4)
            if k0 == 12:
                s = I["x"][0].rearrange("(b p) d -> p b d", p=128)
                T["x"] = [load("pool", xx[:, tb, :], s[:, tb, :], T["memT"][15]) for tb in range(2)]
        return f
    for u in range(4):
        hook("wo1", u, mem_turn(4 * u))

    gb = at(G, [128, D])
    yA = at(A, [128, 2, D])
    part1 = small(8)
    for i in range(4):
        group("wo%d" % i, I["w_out"][0], KC, [(512 * i, 512)], "tok", xth, xtl, reader("mg"),
              tok_store(yA, i, lambda: T["pe:pb3"], part1, "sq1", gb, lambda: T["gb1"], junk=junk_wo,
                        junk_ok=lambda: T["junkB"]))

    kxT = at(G + 8, [128, 4, 256])
    vx = at(G + 12, [128, 2, 512])
    qxT = at(A, [128, 4, 256])
    px = at(A + 4, [128, 8, 256])
    pxT = at(B, [128, 8, 256])
    oxh = at(A + 12, [128, 4, 256], R)
    oxl = at(C + 16, [128, 4, 256], R)

    def norm1a():
        T["x1"] = postnorm(yA, part1, xx, "sq1", T["x"])
        T["x1s"] = prenorm_sums(xx, junkB, T["x1"], T["sq1"])

    def norm1b():
        T["x1h"] = prenorm_tokens(xx, yA, *T["x1s"], T["x1"])

    def evac_kx(p, done):
        r = [vcopy(kxT[:, 2 * b_:2 * b_ + 2, :], v3(p[b_], 256), done[b_], T["pe:pb3"]) for b_ in range(2)]
        T["kx"] = r
        return r

    def evac_vx(p, done):
        r = [vcopy(vx[:, tb, :], p[tb], done[tb], T["pe:pb3"]) for tb in range(2)]
        T["vx"] = r
        return r

    def evac_qx(p, done):
        r = [vcopy(qxT[:, 2 * b_:2 * b_ + 2, :], v3(p[b_], 256), done[b_], T["h2"][15]) for b_ in range(2)]
        T["qx"] = r
        return r

    group("xk", I["xa_wk"][0], KC, [(0, 512)], "feat", memTh, memTl, reader("memT"), evac_kx)
    hook("xk", 0, norm1a)
    hook("xk", 1, norm1b)
    hook("xk", 3, lambda: turn(yA, gcols(28), "h2", T["x1h"], T["pe:wo3"], k1=8))
    hook("xq", 0, lambda: turn(yA, gcols(28), "h2", T["x1h"], T["pe:wo3"], k0=8))
    group("xq", I["xa_wq"][0], KC, [(0, 512)], "feat", xth, xtl, reader("h2"), evac_qx)
    group("xv", I["xa_wv"][0], KC, [(0, 512)], "tok", memTh, memTl, reader("memT"), evac_vx)

    XS = 128.0 ** -0.5
    mxx, nmx, sx, rx = small(8), small(8), small(8), small(8)

    def xa_scores():
        tx = []
        for h in range(4):
            bi, b, fr = bank()
            for tb in range(2):
                tl = mm(b[:, 256 * tb:256 * tb + 256], qxT[:, h, 128 * tb:128 * tb + 128], kxT[:, h, :], True, True,
                        fr, T["qx"], T["kx"], sig=(tb == 1))
                fr = []
            t = reduce(mxx[:, 2 * h:2 * h + 2], v3(b, 256), ALU.max, tl)
            t = ts(nmx[:, 2 * h:2 * h + 2], mxx[:, 2 * h:2 * h + 2], -XS, ALU.mult, None, None, t)
            for tb in range(2):
                j = 2 * h + tb
                t2 = act(px[:, j, :], b[:, 256 * tb:256 * tb + 256], ACT.Exp, t, T["h2"][15], bias=nmx[:, j:j + 1],
                         scale=XS, accum=sx[:, j:j + 1])
            mfree[bi] = [t2]
            tx.append(t2)
        t = recip(rx, sx, tx)
        T["px"] = tt(px, px, bc(rx.unsqueeze(2), [128, 8, 256]), ALU.mult, t)
    hook("xv", 1, xa_scores)

    def xa_turn():
        T["pxT"] = []
        for h in range(4):
            bi, b, fr = bank()
            for mc in range(2):
                for tb in range(2):
                    tl = tr(b[:, 256 * mc + 128 * tb:256 * mc + 128 * tb + 128], px[:, 2 * h + tb, 128 * mc:128 * mc + 128],
                            fr, T["px"], sig=(mc == 1 and tb == 1))
                    fr = []
            t = vcopy(pxT[:, 2 * h:2 * h + 2, :], v3(b, 256), tl, T["h2"][15])
            mfree[bi] = [t]
            T["pxT"].append(t)
    hook("xv", 3, xa_turn)
    T["oxT"] = {}

    def xa_out():
        for h2 in range(0, 4, 2):
            bi, b, fr = bank()
            for j in range(2):
                for mc in range(2):
                    tl = mm(b[:, 256 * j:256 * j + 256], vx[:, mc, (h2 + j) * 128:(h2 + j + 1) * 128],
                            pxT[:, 2 * (h2 + j) + mc, :], mc == 0, mc == 1, fr, T["pxT"], T["vx"],
                            sig=(j == 1 and mc == 1))
                    fr = []
            th = act(oxh[:, h2:h2 + 2, :], v3(b, 256), ACT.Copy, tl)
            tl_ = tt(oxl[:, h2:h2 + 2, :], v3(b, 256), oxh[:, h2:h2 + 2, :].bitcast(F), ALU.subtract, th)
            mfree[bi] = [tl_]
            T["oxT"][h2] = T["oxT"][h2 + 1] = [th, tl_]
    hook("xo0", 0, xa_out)

    yM = at(M, [128, 2, D])
    part2 = small(8)
    yA2 = at(A, [128, 2, D])
    for i in range(4):
        group("xo%d" % i, I["xa_wo"][0], 4, [(512 * i, 512)], "tok", oxh, oxl, reader("oxT"),
              tok_store(yM, i, lambda: T["pe:xv"], part2, "sq2", gb, lambda: T["gb2"], junk=junk_xo,
                        junk_ok=lambda: T["pxT"], tail=entrance(yM, part2, xx, "x2", yA2) if i == 3 else None), late=3 * (i == 3))

    def gb2_load():
        T["gb2"] = load("pool", gb, on_all(I["post_norm_xa"][0]), T["x1"])
    hook("xq", 0, gb2_load)

    HF = FF // 256
    ach = at(G, [128, HF, 256], R)
    acl = at(G + 22, [128, HF, 256], R)
    cvt = [at(B + 4 * s, [128, 1024]) for s in range(2)]
    cv = [[cvt[s][:, 256 * j:256 * j + 256] for j in range(4)] for s in range(2)]
    gate_up = [[cvt[s][:, 512 * j:512 * j + 512] for j in range(2)] for s in range(2)]

    def norm2():
        turn(yA2, gcols(60), "h3", T["x2h"], T["pe:xq"], k1=8, early=True)
        scale_second(xx, yA2, T["x2"], T["x2h"], T["pe:xo3"])

    def norm2b():
        turn(yA2, gcols(60), "h3", T["x2h"], T["pe:xq"], k0=8)
    T["acT"] = {}
    ngr = [0]

    def evac_up(half, i):
        def f(p, done):
            s = ngr[0] % 2
            ngr[0] += 1
            c = cv[s]
            cols = [half * HF + 2 * i, half * HF + 2 * i + 1, 44 + half * HF + 2 * i, 44 + half * HF + 2 * i + 1]
            ok = [T.get("cv%d" % s), T["h3"][15], T["vt2"]]
            r = []
            for b_ in range(2):
                for j in range(2):
                    q = 2 * b_ + j
                    t = act(c[q], p[b_][:, 256 * j:256 * j + 256], ACT.Identity, done[b_], ok,
                            bias=VT[:, 128 + cols[q]:129 + cols[q]], scale=VT[:, 512 + cols[q]:513 + cols[q]])
                for j in range(2):
                    q = 2 * b_ + j
                    t1 = stt(c[q][:, 1:256], p[b_][:, 256 * j:256 * j + 255], VT[:, 384 + cols[q]:385 + cols[q]],
                             c[q][:, 1:256], ALU.mult, ALU.add, t)
                    t2 = stt(c[q][:, 2:256], p[b_][:, 256 * j:256 * j + 254], VT[:, 256 + cols[q]:257 + cols[q]],
                             c[q][:, 2:256], ALU.mult, ALU.add, t1)
                r.append(t2)
            cg = gate_up[s][0]
            cu = gate_up[s][1]
            t = act(cg, cg, ACT.Gelu_apprx_tanh, r[0])
            t = tt(cu, cg, cu, ALU.mult, t, r[1])
            k = slice(2 * i, 2 * i + 2)
            wok = [T["pe:xo3"], T["x2"]] if half == 0 else [T["pe:dn03"]]
            th = act(ach[:, k, :], v3(cu, 256), ACT.Copy, t, wok)
            tl_ = tt(acl[:, k, :], v3(cu, 256), ach[:, k, :].bitcast(F), ALU.subtract, th, wok)
            T["cv%d" % s] = tl_
            T["acT"][(half, 2 * i)] = T["acT"][(half, 2 * i + 1)] = [th, tl_]
            return r
        return f

    part3 = small(8)

    def evac_last(p, done):
        c = slice(1536, 2048)
        add, sq = [], []
        T["r3"], T["x3d"] = [], []
        for tb in range(2):
            o = yA2[:, tb, c]
            add.append(tt(o, p[tb], o, ALU.add, done[tb]))
            sq.append(square(junk_dn, o, part3[:, 4 * tb + 3:4 * tb + 4], add[tb], T["pe:xo3"]))
            s = small(1)
            r, t = rstd_of(s, D, EPS, reduce(s, part3[:, 4 * tb:4 * tb + 4], ALU.add, sq[tb]))
            T["r3"].append((r, t))
            T["x3d"].append(ts(dg[:, 128 * tb:128 * tb + 128], ident, r, ALU.mult, None, None, t))
        T["sq3"] += sq
        T["y3"] = [tt(yA2[:, tb, c], yA2[:, tb, c], gb3[:, c], ALU.mult, sq[tb], T["gb3"]) for tb in range(2)]
        return add
    gb3 = at(B, [128, D])
    for half in range(2):
        for i in range(HF // 2):
            c0 = half * HF * 128 + 256 * i
            group("up%d_%d" % (half, i), I["ffn_w_up"][0], KC, [(c0, 256), (FF + c0, 256)], "feat", xth, xtl,
                  reader("h3"), evac_up(half, i))
        for i in range(4):
            group("dn%d%d" % (half, i), I["ffn_w_down"][0], HF, [(512 * i, 512)], "tok", ach, acl,
                  (lambda half: lambda k: T["acT"][(half, k)])(half),
                  evac_last if half and i == 3 else
                  tok_store(yA2, i, lambda: T["yA2"], part3, "sq3", gb3, lambda: T["gb3"], True, junk_dn,
                            lambda: T["pe:xo3"]) if half else tok_store(yA2, i, lambda: T["h3"][15]),
                  k_off=half * HF, late=2 if half == 1 and i == 3 else 0)
    hook("up0_0", "first", norm2)
    hook("up0_0", 1, norm2b)

    def load_sqrt():
        act(small(1), ones[:, 0:1], ACT.Sqrt, t_ones)
    hook("xo1", 0, load_sqrt)
    hook("dn13", 1, load_sqrt)
    hook("w22", 1, load_sqrt)


    def gb3_load():
        T["yA2"] = T["dn0"]
        T["gb3"] = load("pool", gb3, on_all(I["post_norm_ffn"][0]), T["cv0"], T["cv1"])
    hook("dn10", 1, gb3_load)

    w2 = I["w_in_2"][0]

    x3b = {}

    def x2_turn(tb):
        def f():
            for k2 in range(0, 8, 2):
                if tb == 0:
                    x3b[k2] = bank()
                bi, b, fr = x3b[k2]
                for j in range(2):
                    T["x2pe"] = mm(b[:, j * 256 + tb * 128:j * 256 + tb * 128 + 128],
                                   xx[:, tb, (k2 + j) * 128:(k2 + j + 1) * 128], ident, tb == 0 and j == 0, False,
                                   fr, T["x2"], sig=(tb == 1 and j == 1 and k2 == 6), share=True)
        return f

    def norm3a():
        x2_turn(1)()
        T["h4"] = {}
        last = {}
        for tb in range(2):
            for k2 in range(0, 8, 2):
                b = x3b[k2][1]
                for j in range(2):
                    last[k2] = mm(b[:, j * 256 + tb * 128:j * 256 + tb * 128 + 128],
                                  yA2[:, tb, (k2 + j) * 128:(k2 + j + 1) * 128], dg[:, 128 * tb:128 * tb + 128],
                                  False, True, T["x3d"][tb], T["sq3"], sig=(tb == 1 and j == 1), share=True)
        for k2 in range(0, 8, 2):
            bi, b, fr = x3b[k2]
            th = act(xth[:, k2:k2 + 2, :], v3(b, 256), ACT.Copy, last[k2], T["pe:up1_10"])
            tl = tt(xtl[:, k2:k2 + 2, :], v3(b, 256), xth[:, k2:k2 + 2, :].bitcast(F), ALU.subtract, th)
            T["h4"][k2] = T["h4"][k2 + 1] = [th, tl]
            mfree[bi] = [tl]
        T["x3p"] = last[6]

    def x3_half(hf):
        c = slice(1024 * hf, 1024 * hf + 1024)
        return [stt(xx[:, tb, c], yA2[:, tb, c], T["r3"][tb][0], xx[:, tb, c], ALU.mult, ALU.add, T["r3"][tb][1],
                    T["y3"], T["x2pe"]) for tb in range(2)]

    def norm3b():
        T["x3h"] = x3_half(1)
        T["x3"] = [x3_half(0), T["x3h"]]

    def norm3c():
        to_features(xx, None, xth, xtl, T["h4"], KC, lambda k, tb: T["x3h"][tb], T["pe:up1_10"], 8)

    h4 = reader("h4")
    qi = at(A, [128, 2, 1024])
    qiT = at(A + 8, [128, 8, 256])
    kv = at(B, [128, 2, 512])
    kaT = at(B + 4, [128, 2, 256])
    score = at(B + 6, [128, 2, 256])
    amask = at(C + 16, [128, 2, 256])
    rt = [at(C + 18 + 0.5 * i, [128, 128]) for i in range(4)]
    ki2 = at(G, [128, 2, 128])
    kwT = at(G + 7, [128, 256])
    kiT = at(G + 1, [128, 256])
    rl = [at(G + 2 + 2 * i, [128, 512]) for i in range(2)]
    top8 = at(G + 6, [128, 8])
    expa = at(G + 6.5, [128, 16])

    def rope(x3_, half, tb, col_c, col_s, n, ok):
        a, b = x3_[:, :, 0:half], x3_[:, :, half:2 * half]
        cs = bc(cst[:, col_c + tb * half:col_c + (tb + 1) * half].unsqueeze(1), [128, n, half])
        sn = bc(cst[:, col_s + tb * half:col_s + (tb + 1) * half].unsqueeze(1), [128, n, half])
        r_ = [v3(rt[i][:, 0:n * half], half) for i in range(4)]
        t0 = tt(r_[0], a, cs, ALU.mult, ok, T.get("rope"))
        t1 = tt(r_[1], b, sn, ALU.mult)
        t2 = tt(r_[2], b, cs, ALU.mult)
        t3 = tt(r_[3], a, sn, ALU.mult)
        t4 = tt(a, r_[0], r_[1], ALU.subtract, t1, t3)
        T["rope"] = tt(b, r_[2], r_[3], ALU.add, t3)
        return [t4, T["rope"]]

    def evac_kiw(p, done):
        T["kwT"] = vcopy(kwT, p[0][:, 0:256], done[0], T["h4"][15])
        return T["kwT"]

    def part_kiw():
        bi, b, fr = bank()
        for tb in range(2):
            tl = tr(b[:, 128 * tb:128 * tb + 128], kwT[:, 128 * tb:128 * tb + 128], fr, T["kwT"], sig=(tb == 1))
        p = v3(b[:, 0:256], 128)
        T["dtr"] = tt(v3(dt_, 16), p[:, :, 112:128], bc(dtb.unsqueeze(1), [128, 2, 16]), ALU.add, tl, t_dtb)
        T["wi"] = ts(v3(widx, 16), p[:, :, 64:80], 1.0 / 32.0, ALU.mult, None, None)
        t0 = vcopy(ki2[:, :, 0:64], p[:, :, 0:64])
        mfree[bi] = [t0]
        for tb in range(2):
            t2 = rope(ki2[:, tb:tb + 1, 0:64], 8, tb, C_CI, C_SI, 1, t0)
            T["ki%d" % tb] = vcopy(ki2[:, tb, 64:128], ki2[:, tb, 0:64], t2)
    hook("qi1", 0.5, part_kiw)

    def softplus():
        t = act(dtmp, dt_, ACT.Abs, T["dtr"])
        z = act(dtmp, dtmp, ACT.Exp, t, scale=-1.0)
        s_, w_, q_ = dl1, do1, dtm2
        t = ts(s_, dtmp, 2.0, ALU.add, None, None, z)
        t = recip(s_, s_, t)
        t = tt(s_, s_, dtmp, ALU.mult, t)
        t = tt(w_, s_, s_, ALU.mult, t)
        t = ts(q_, w_, 1.0 / 17.0, ALU.mult, None, None, t)
        for n in range(15, 1, -2):
            t = stt(q_, q_, 1.0 / n, w_, ALU.add, ALU.mult, t)
        t = stt(q_, q_, 1.0, s_, ALU.add, ALU.mult, t)
        d1 = q_
        t = ts(q_, q_, 2.0, ALU.mult, None, None, t)
        T["dt"] = t = stt(dt_, dt_, 0.0, d1, ALU.max, ALU.add, t)
        ta = act(expa, alog, ACT.Exp, t_alog)
        t = tt(v3(adt, 16), v3(dt_, 16), bc(expa.unsqueeze(1), [128, 2, 16]), ALU.mult, t, ta)
        T["adt"] = ts(adt, adt, -1.0, ALU.mult, None, None, t)
    hook("qi1", 1, softplus)

    def evac_qi(i):
        def f(p, done):
            r = []
            for tb in range(2):
                o = qi[:, tb, 512 * i:512 * i + 512]
                t = vcopy(o, p[tb], done[tb], T["h4"][15])
                r.append(t)
                T["qi%d%d" % (i, tb)] = rope(v3(o, 64), 8, tb, C_CI, C_SI, 8, t)
            return r
        return f

    group("qi0", w2, KC, [(2560, 512)], "tok", xth, xtl, h4, evac_qi(0))
    hook("dn13", 5, x2_turn(0))
    hook("qi0", "first", norm3a)
    hook("qi0", 0, norm3b)
    hook("qi0", 1, norm3c)
    group("kiw", w2, KC, [(3584, 80), (6704, 48)], "thin", xth, xtl, h4, evac_kiw, chunk=16)
    group("qi1", w2, KC, [(3072, 512)], "tok", xth, xtl, h4, evac_qi(1))

    def turn_ki():
        bi, b, fr = bank()
        for tb in range(2):
            tl = tr(b[:, tb * 128:tb * 128 + 128], ki2[:, tb, :], fr, T["ki0"], T["ki1"], sig=(tb == 1))
            fr = []
        T["kiT"] = vcopy(kiT, b[:, 0:256], tl)
        mfree[bi] = [T["kiT"]]
    hook("qi1", 2, turn_ki)

    def turn_qi(i):
        def f():
            for p2 in range(4 * i, 4 * i + 4, 2):
                bi, b, fr = bank()
                for j in range(2):
                    for tb in range(2):
                        tl = tr(b[:, 256 * j + 128 * tb:256 * j + 128 * tb + 128], qi[:, tb, (p2 + j) * 128:(p2 + j + 1) * 128],
                                fr, T["qi%d0" % i], T["qi%d1" % i], sig=(j == 1 and tb == 1))
                        fr = []
                t = vcopy(qiT[:, p2:p2 + 2, :], v3(b, 256), tl)
                mfree[bi] = [t]
                T["qiT%d" % p2] = T["qiT%d" % (p2 + 1)] = t
        return f
    hook("qi1", 1, turn_qi(0))
    hook("kv", 1, turn_qi(1))

    def index_scores(qb, q4):
        def f():
            nk = 128 * (qb + 1)
            bs = [bank(), bank()]
            tls = []
            for par in range(2):
                bi, b, fr = bs[par]
                for j in range(2):
                    h = 4 * q4 + 2 * j + par
                    p0 = 64 * par
                    tl = mm(b[:, 256 * j:256 * j + nk], qiT[p0:p0 + 64, h // 2, 128 * qb:128 * qb + 128],
                            kiT[p0:p0 + 64, 0:nk], True, True, fr, T["qiT%d" % (h // 2)], T["kiT"], sig=(j == 1))
                    fr = []
                tls.append(tl)
            for par in range(2):
                bi, b, fr = bs[par]
                r3 = v3(rl[par], 256)
                t = act(r3[:, :, 0:nk], v3(b, 256)[:, :, 0:nk], ACT.Relu, tls[par], T.get("rl%d" % par))
                mfree[bi] = [t]
                for j in range(2):
                    h = 4 * q4 + 2 * j + par
                    w_ = widx[:, 16 * qb + h:16 * qb + h + 1]
                    o = score[:, qb, 0:nk]
                    if h == 0:
                        t = ts(o, r3[:, j, 0:nk], w_, ALU.mult, None, None, t, T["wi"], T["h4"][15], T["x3"])
                    else:
                        t = stt(o, r3[:, j, 0:nk], w_, o, ALU.mult, ALU.add, t, T["sc%d" % qb])
                    T["sc%d" % qb] = t
                T["rl%d" % par] = t
        return f

    for n, (qb, q4) in enumerate([(0, 0), (0, 1), (0, 2), (0, 3), (1, 0), (1, 1), (1, 2), (1, 3)]):
        hook("kv" if n < 2 else "xb0" if n < 6 else "xb1", (n + 2) % 4, index_scores(qb, q4))

    def choose(qb, part):
        def f():
            nk = 128 * (qb + 1)
            s_ = score[:, qb, 0:nk]
            if part == 0:
                own = score[:, qb, 128 * qb:128 * qb + 128]
                T["w%d" % qb] = tt(own, own, m64, ALU.add, T["sc%d" % qb])
            t = T["w%d" % qb]
            for _ in range(TOPK // 16):
                t = put("dve", lambda e: e.max(top8, s_), [t])
                t = put("dve", lambda e: e.match_replace(s_, top8, s_, GONE), [t])
            if part == 1:
                am = amask[:, qb, 0:nk]
                t = ts(am, s_, -2.0e38, ALU.is_gt, -BIG, ALU.mult, t, T["rope"], T["sq3"][-1])
            T["w%d" % qb] = t
        return f
    hook("xb1", 2, choose(0, 0))
    hook("xb2", 2, choose(0, 1))
    hook("xb3", 2, choose(1, 0))
    hook("zs1", 0, choose(1, 1))


    def evac_kv(p, done):
        r = []
        for tb in range(2):
            t = vcopy(kv[:, tb, :], p[tb], done[tb], T["x3"])
            r.append(t)
            T["kv%d" % tb] = rope(v3(kv[:, tb, 0:256], 128), 16, tb, C_CA, C_SA, 2, t) + [t]
        return r
    group("kv", w2, KC, [(1024, 512)], "tok", xth, xtl, h4, evac_kv)

    def turn_k():
        bi, b, fr = bank()
        for g in range(2):
            for tb in range(2):
                tl = tr(b[:, 256 * g + 128 * tb:256 * g + 128 * tb + 128], kv[:, tb, 128 * g:128 * g + 128], fr,
                        T["kv0"], T["kv1"], sig=(g == 1 and tb == 1))
                fr = []
        T["kaT"] = vcopy(kaT, v3(b, 256), tl)
        mfree[bi] = [T["kaT"]]
    hook("xb0", 1, turn_k)

    xb = at(M, [128, 16, 256])

    def evac_xb(i):
        def f(p, done):
            r, taps = [], []
            for b_ in range(2):
                for j in range(2):
                    c = 4 * i + 2 * b_ + j
                    t = act(xb[:, c, :], p[b_][:, 256 * j:256 * j + 256], ACT.Identity, done[b_], T["pe:dn13"],
                            bias=VT[:, 84 + c:85 + c], scale=VT[:, 640 + 48 + c:640 + 49 + c])
                taps.append(t)
            for b_ in range(2):
                ts_ = [taps[b_], taps[b_]]
                for tap in range(1, 4):
                    for j in range(2):
                        c = 4 * i + 2 * b_ + j
                        wc = VT[:, 640 + 16 * (3 - tap) + c:640 + 16 * (3 - tap) + c + 1]
                        ts_[j] = stt(xb[:, c, tap:256], p[b_][:, 256 * j:256 * j + 256 - tap], wc, xb[:, c, tap:256],
                                     ALU.mult, ALU.add, ts_[j])
                r.append(ts_)
            T["xbc%d" % i] = r
            return r
        return f

    def silu_xb(i):
        def f():
            for b_ in range(2):
                c = 4 * i + 2 * b_
                T["xb%d" % c] = T["xb%d" % (c + 1)] = act(xb[:, c:c + 2, :], xb[:, c:c + 2, :], ACT.Silu,
                                                          T["xbc%d" % i][b_])
        return f
    for i in range(4):
        hook("xb%d" % (i + 1) if i < 3 else "q20", 0, silu_xb(i))

    for i in range(4):
        group("xb%d" % i, w2, KC, [(4688 + 512 * i, 512)], "feat", xth, xtl, h4, evac_xb(i))

    xs = at(DD, [128, 2, 1024])
    xdt = at(DD + 8, [128, 2, 1024])
    cbm = at(M, [128, 4, 384])
    Wm = at(G + 8, [128, 4, 384])
    zs = at(G, [128, 2, 1024])

    def turn_xs(i):
        def f():
            for c2 in range(4 * i, 4 * i + 4, 2):
                bi, b, fr = bank()
                for j in range(2):
                    for tb in range(2):
                        tl = tr(b[:, 256 * tb + 128 * j:256 * tb + 128 * j + 128], xb[:, c2 + j, 128 * tb:128 * tb + 128], fr,
                                T["xb%d" % c2], T["xb%d" % (c2 + 1)], sig=(j == 1 and tb == 1))
                        fr = []
                t = vcopy(xs[:, :, c2 * 128:c2 * 128 + 256], v3(b, 256), tl, T["pe:dn13"])
                mfree[bi] = [t]
                T["xsT%d" % c2] = tl
                T["xs%d" % (c2 // 2)] = t
        return f
    hook("xb1", 3, turn_xs(0))
    hook("xb2", 3, turn_xs(1))

    def ssd_inputs(tb):
        def f():
            d3 = bc(dt_[:, 16 * tb:16 * tb + 16].unsqueeze(2), [128, 16, 64])
            T["xdt%d" % tb] = tt(v3(xdt[:, tb, :], 64), v3(xs[:, tb, :], 64), d3, ALU.mult,
                                 [T["xs%d" % j] for j in range(4)], T["dt"])
            k3 = bc(dsk.unsqueeze(2), [128, 16, 64])
            T["ys%d" % tb] = tt(v3(xs[:, tb, :], 64), v3(xs[:, tb, :], 64), k3, ALU.mult, T["xdt%d" % tb], t_dsk)
        return f
    hook("xb3", 3, ssd_inputs(0))
    hook("q20", 1, ssd_inputs(1))

    def ssd_cb(gs):
        for g in gs:
            bi, b, fr = bank()
            bT_, cT_ = xb[:, 8 + g, :], xb[:, 12 + g, :]
            w_ = [T["xb%d" % (8 + g)], T["xb%d" % (12 + g)]]
            mm(b[:, 0:256], bT_[:, 0:128], cT_, True, True, fr, w_)
            tl = mm(b[:, 256:384], bT_[:, 128:256], cT_[:, 128:256], True, True, sig=True)
            t1 = tt(v3(b, 256)[:, :, 0:128], v3(b, 256)[:, :, 0:128],
                    bc(triu.unsqueeze(1), [128, 2, 128]), ALU.mult, tl)
            t = vcopy(cbm[:, g, :], b[:, 0:384], t1, [T["xsT%d" % c] for c in (0, 2, 4, 6)])
            mfree[bi] = [t]
            T["cb%d" % g] = t
            T["cbpe"] = tl
    hook("q20", 2, lambda: ssd_cb((0, 1)))
    hook("q20", 3, lambda: ssd_cb((2, 3)))

    csh = at(G + 14, [16, 256], R)
    csl = at(G + 15, [16, 256], R)
    sel = at(M + 8, [16, 16, 128], R)
    ncs, suf = dl1, do1[:, 0:16]

    def ssd_sums():
        bi, b, fr = bank()
        mm(b[0:16, 0:128], adt[:, 0:16], triu, True, True, fr, T["adt"])
        tl = mm(b[0:16, 128:256], adt[:, 16:32], triu, True, True, sig=True)
        th = act(csh, b[0:16, 0:256], ACT.Copy, tl)
        t = tt(csl, b[0:16, 0:256], csh.bitcast(F), ALU.subtract, th)
        mfree[bi] = [t]
        T["csT"] = [th, t]
        bi, b, fr = bank()
        mm(b[:, 0:32], triu, adt, True, True, fr)
        tl = mm(b[:, 32:48], gt, adt[:, 0:16], True, True, sig=True)
        ts(ncs, b[:, 0:32], -1.0, ALU.mult, None, None, tl)
        t = vcopy(suf, b[:, 32:48])
        mfree[bi] = [t]
        T["ncs"] = t
    hook("q20", 0, ssd_sums)

    def ssd_rows():
        T["sel"] = act(sel, bc(ident[0:16, 0:16].unsqueeze(2), [16, 16, 128]), ACT.Copy, T["cbpe"])
    hook("q21", 0, ssd_rows)

    spread = {}

    def ssd_spread(g):
        def f():
            for j2 in (0, 2):
                bi, b, fr = bank()
                for j in range(2):
                    o, l = b[:, 256 * j:256 * j + 256], sel[:, 4 * g + j2 + j, :]
                    mm(o, l, csh, j == 0, False, fr, T["sel"], T["csT"], share=True)
                    tl = mm(o, l, csl, False, True, sig=(j == 1), share=True)
                spread[g, j2] = (bi, b, tl)
        return f

    def ssd_decays(g):
        def f():
            T["dec"] = []
            for j2 in (0, 2):
                bi, b, tl = spread[g, j2]
                for j in range(2):
                    h = 4 * g + j2 + j
                    for c, q, a in ((0, 0, ncs[:, h:h + 1]), (128, 128, suf[:, h:h + 1]),
                                    (256, 128, ncs[:, 16 + h:17 + h])):
                        t = ts(Wm[:, j2 + j, c:c + 128], b[:, 256 * j + q:256 * j + q + 128], a, ALU.add, 0.0, ALU.min,
                               tl, T["ncs"], T.get("wpe"))
                mfree[bi] = [t]
                T["dec"].append(act(Wm[:, j2:j2 + 2, :], Wm[:, j2:j2 + 2, :], ACT.Exp, t))
        return f

    def ssd_weigh(g):
        def f():
            T["W"] = tt(Wm, Wm, bc(cbm[:, g:g + 1, :], [128, 4, 384]), ALU.mult, T["dec"], T["cb%d" % g])
        return f

    def ssd_y(g):
        def f():
            bi, b, fr = bank()
            for j in range(4):
                h = 4 * g + j
                xd = lambda tb: xdt[:, tb, 64 * h:64 * h + 64]
                mm(b[:, 64 * j:64 * j + 64], Wm[:, j, 0:128], xd(0), True, True, fr, T["W"], T["xdt0"], T["xdt1"])
                fr = []
                mm(b[:, 256 + 64 * j:256 + 64 * j + 64], Wm[:, j, 128:256], xd(0), True, False)
                tl = mm(b[:, 256 + 64 * j:256 + 64 * j + 64], Wm[:, j, 256:384], xd(1), False, True, sig=(j == 3))
            T["wpe"] = tl
            y_ = xs[:, :, 256 * g:256 * g + 256]
            t = tt(y_, v3(b, 256), y_, ALU.add, tl, T["ys0"], T["ys1"])
            mfree[bi] = [t]
            T["y%d" % g] = t
        return f
    for n_, u_, fn in [
            ("q21", 1, ssd_spread(0)), ("q21", 1.5, ssd_decays(0)),
            ("q21", 2, ssd_weigh(0)), ("q21", 3, ssd_y(0)), ("q21", 3, ssd_spread(1)), ("q21", 3.5, ssd_decays(1)),
            ("zs0", 0, ssd_weigh(1)), ("zs0", 1, ssd_y(1)), ("zs0", 1, ssd_spread(2)), ("zs0", 1.5, ssd_decays(2)),
            ("zs0", 2, ssd_weigh(2)), ("zs0", 3, ssd_y(2)), ("zs0", 3, ssd_spread(3)), ("zs0", 3.5, ssd_decays(3)),
            ("zs1", 0, ssd_weigh(3)), ("zs1", 1, ssd_y(3))]:
        hook(n_, u_, fn)

    qa = at(A, [128, 2, 1024])
    qaT = at(A + 8, [128, 8, 256])
    pa = at(M, [128, 8, 256])
    paT = at(M + 8, [128, 2, 1024])
    oaT = at(A, [128, 8, 256])

    def evac_q2(i):
        def f(p, done):
            r = []
            for tb in range(2):
                o = qa[:, tb, 512 * i:512 * i + 512]
                t = vcopy(o, p[tb], done[tb])
                r.append(t)
                T["qa%d%d" % (i, tb)] = rope(v3(o, 128), 16, tb, C_CA, C_SA, 4, t)
            return r
        return f

    for i in range(2):
        group("q2%d" % i, w2, KC, [(512 * i, 512)], "tok", xth, xtl, h4, evac_q2(i))

    def turn_q(i):
        def f():
            for p2 in range(4 * i, 4 * i + 4, 2):
                bi, b, fr = bank()
                for j in range(2):
                    for tb in range(2):
                        tl = tr(b[:, 256 * j + 128 * tb:256 * j + 128 * tb + 128], qa[:, tb, (p2 + j) * 128:(p2 + j + 1) * 128],
                                fr, T["qa%d0" % i], T["qa%d1" % i], sig=(j == 1 and tb == 1))
                        fr = []
                t = vcopy(qaT[:, p2:p2 + 2, :], v3(b, 256), tl)
                mfree[bi] = [t]
                T["qaT%d" % p2] = T["qaT%d" % (p2 + 1)] = t
                T["qatr"] = tl
        return f
    hook("q21", 1, turn_q(0))
    hook("zs0", 1, turn_q(1))

    amx, anm, asm, arc = small(8), small(8), small(8), small(8)

    def at_scores(qb):
        def f():
            nk = 128 * (qb + 1)
            te = []
            for h2 in range(0, 8, 2):
                bi, b, fr = bank()
                for j in range(2):
                    h = h2 + j
                    tl = mm(b[:, 256 * j:256 * j + nk], qaT[:, h, 128 * qb:128 * qb + 128], kaT[:, h // 4, 0:nk], True, True,
                            fr, T["qaT%d" % h], T["kaT"], sig=(j == 1))
                    fr = []
                o = pa[:, h2:h2 + 2, 0:nk]
                t = tt(o, v3(b, 256)[:, :, 0:nk], bc(amask[:, qb:qb + 1, 0:nk], [128, 2, nk]), ALU.add, tl, T["w%d" % qb],
                       T["W"], T.get("paT"), T["wpe"])
                mfree[bi] = [t]
                t = reduce(amx[:, h2:h2 + 2], o, ALU.max, t, T.get("arc"))
                t = ts(anm[:, h2:h2 + 2], amx[:, h2:h2 + 2], -XS, ALU.mult, None, None, t)
                for j in range(2):
                    h = h2 + j
                    te.append(act(pa[:, h, 0:nk], pa[:, h, 0:nk], ACT.Exp, t, bias=anm[:, h:h + 1], scale=XS,
                                  accum=asm[:, h:h + 1]))
            T["arc"] = recip(arc, asm, te)
            T["pa"] = tt(pa[:, :, 0:nk], pa[:, :, 0:nk], bc(arc.unsqueeze(2), [128, 8, nk]), ALU.mult, T["arc"])
        return f

    def at_turn(qb):
        def f():
            for kb in range(qb + 1):
                for h4_ in (0, 4):
                    bi, b, fr = bank()
                    for j in range(4):
                        tl = tr(b[:, 128 * j:128 * j + 128], pa[:, h4_ + j, 128 * kb:128 * kb + 128], fr, T["pa"], sig=(j == 3))
                        fr = []
                    t = vcopy(paT[:, kb, 128 * h4_:128 * h4_ + 512], b, tl, T.get("opv"))
                    mfree[bi] = [t]
            T["paTd"] = t
            T["paT"] = tl
        return f

    def at_out(qb):
        def f():
            for h4_ in (0, 4):
                bi, b, fr = bank()
                for j in range(4):
                    h = h4_ + j
                    g = h // 4
                    for kb in range(qb + 1):
                        tl = mm(b[:, 128 * j:128 * j + 128], kv[:, kb, 256 + 128 * g:256 + 128 * g + 128],
                                paT[:, kb, 128 * h:128 * h + 128], kb == 0, kb == qb, fr, T["paTd"], T["kv0"], T["kv1"],
                                sig=(j == 3 and kb == qb))
                        fr = []
                t = vcopy(oaT[:, h4_:h4_ + 4, 128 * qb:128 * qb + 128], v3(b, 128), tl, T["qatr"])
                mfree[bi] = [t]
                T["oa%d%d" % (qb, h4_ // 4)] = t
            T["opv"] = tl
        return f
    for (n_, u_), fn in zip([("zs1", 1), ("zs1", 3), ("za0", 0), ("za0", 1), ("za0", 3), ("za1", 0)],
                            [at_scores(0), at_turn(0), at_out(0), at_scores(1), at_turn(1), at_out(1)]):
        hook(n_, u_, fn)

    def evac_zs(i):
        def f(p, done):
            r = []
            for tb in range(2):
                o = zs[:, tb, 512 * i:512 * i + 512]
                r.append(act(o, p[tb], ACT.Silu, done[tb], T["sc1"], T["w1"], T["adt"]))
            T["zs%d" % i] = r
            return r
        return f

    for i in range(2):
        group("zs%d" % i, w2, KC, [(3664 + 512 * i, 512)], "tok", xth, xtl, h4, evac_zs(i))

    gssq = small(8)
    junk_g = at(G + 8, [128, 256])

    def ssd_gate(i):
        def f():
            for tb in range(2):
                y_ = xs[:, tb, 512 * i:512 * i + 512]
                t = tt(y_, y_, zs[:, tb, 512 * i:512 * i + 512], ALU.mult, T["zs%d" % i], [T["y%d" % g] for g in range(4)])
                for g in (2 * i, 2 * i + 1):
                    T["gs%d%d" % (tb, g)] = square(junk_g, xs[:, tb, 256 * g:256 * g + 256],
                                                   gssq[:, 4 * tb + g:4 * tb + g + 1], t, T["wpe"])
        return f
    hook("za0", 0, ssd_gate(0))
    hook("za0", 2, ssd_gate(1))

    def ssd_norm():
        r, t = rstd_of(gssq, 256, LN_EPS, [T["gs%d%d" % (tb, g)] for tb in range(2) for g in range(4)])
        for tb in range(2):
            x4 = v3(xs[:, tb, :], 256)
            T["yn%d" % tb] = tt(x4, x4, bc(r[:, 4 * tb:4 * tb + 4].unsqueeze(2), [128, 4, 256]), ALU.mult, t)
    hook("za1", 1, ssd_norm)

    T["mix"] = {}
    zt = [at(G + 8 + 2 * i, [128, 512]) for i in range(2)]

    def evac_za(i):
        def f(p, done):
            r = []
            for b_ in range(2):
                c = slice(4 * i + 2 * b_, 4 * i + 2 * b_ + 2)
                t = act(zt[b_] if i else zk[b_], p[b_], ACT.Silu, done[b_], T["gs13"] if i else T["wpe"], T["W"])
                r.append(t)
                T["za%d%d" % (i, b_)] = t
            return r
        return f
    zk = [at(G + 12 + 2 * i, [128, 512]) for i in range(2)]

    for i in range(2):
        group("za%d" % i, w2, KC, [(1536 + 512 * i, 512)], "feat", xth, xtl, h4, evac_za(i))

    def mix_attn(i):
        def f():
            for b_ in range(2):
                z = (zt if i else zk)[b_]
                c0 = 4 * i + 2 * b_
                c = slice(c0, c0 + 2)
                z3 = v3(z, 256)
                t = tt(z3, z3, oaT[:, c, :], ALU.mult, T["za%d%d" % (i, b_)], T["oa00"], T["oa01"], T["oa10"], T["oa11"])
                th = act(xth[:, c, :], z3, ACT.Copy, t, T["pe:za1"])
                tl_ = tt(xtl[:, c, :], z3, xth[:, c, :].bitcast(F), ALU.subtract, th, T["pe:za1"])
                T["mix"][c0] = T["mix"][c0 + 1] = [th, tl_]
        return f

    def mix_ssd(k0):
        def f():
            rr = {}
            to_features(xs, lambda k: VT[:, 76 + k:77 + k], xth[:, 8:16, :], xtl[:, 8:16, :], rr, k0 + 4,
                        lambda k, tb: T["yn%d" % tb], T["pe:za1"], k0)
            for k in rr:
                T["mix"][8 + k] = rr[k]
        return f
    hook("za1", 3, mix_attn(0))
    hook("w20", 0, mix_attn(1))
    hook("w20", 0.5, mix_ssd(0))
    hook("w20", 1.5, mix_ssd(4))

    y5 = at(M, [128, 2, D])
    lg = at(DD, [128, D])
    lb = at(DD + 8, [128, D])
    bst = at(B, [128, 2, 24])

    def ln_loads():
        T["lg"] = load("pool", lg, on_all(I["ln_g_2"][0]), T["mix"][15])
        T["lb"] = load("pool", lb, on_all(I["ln_b_2"][0]), T["mix"][15])
    hook("w20", 2, ln_loads)

    o_dst = out_d[0].rearrange("(b p) d -> p b d", p=128)
    s_out = nc.alloc_semaphore("s_out")
    n_out = [0]
    ln = {}

    def ln_stats(tb):
        mv, nb = small(2), small(1)
        s3 = bst[:, tb, :]
        t = put("dve", lambda e: e.bn_aggr(mv, s3), [T["bs%d%d" % (tb, i)] for i in range(4)])
        r, t = rstd_of(mv[:, 1:2], 1.0, LN_EPS, t)
        ln[tb] = r, nb, stt(nb, mv[:, 0:1], -1.0, r, ALU.mult, ALU.mult, t)

    def ln_center(tb, q):
        r, nb, t = ln[tb]
        y_ = y5[:, tb, 512 * q:512 * q + 512]
        ln[tb, q] = act(y_, y_, ACT.Identity, t, bias=nb, scale=r)

    def ln_store(tb, q, on_pool):
        c = slice(512 * q, 512 * q + 512)
        y_, b_, d_ = y5[:, tb, c], lb[:, c], o_dst[:, tb, c]
        t = tt(y_, y_, lg[:, c], ALU.mult, ln[tb, q], T["lg"])
        if on_pool:
            t = put("pool", lambda e: e.tensor_tensor(y_, y_, b_, ALU.add), [t, T["lb"]])
        else:
            t = tt(y_, y_, b_, ALU.add, t, T["lb"])
        put("sp", lambda e: e.dma_start(d_, y_).then_inc(s_out, 16), [t], False)
        n_out[0] += 16

    def evac_w2(i):
        def f(p, done):
            r = []
            for tb in range(2):
                o = y5[:, tb, 512 * i:512 * i + 512]
                t = stt(o, xx[:, tb, 512 * i:512 * i + 512], ALPHA, p[tb], ALU.mult, ALU.add, done[tb], T["x3"], T["opv"],
                        T["paT"])
                r.append(t)
                so = bst[:, tb, 6 * i:6 * i + 6]
                T["bs%d%d" % (tb, i)] = put("dve", lambda e, so=so, o=o: e.bn_stats(so, o), [t])
                if i == 3:
                    ln_stats(tb)
                    for q in range(4):
                        ln_center(tb, q)
                        ln_store(tb, q, q < 3 - tb)
            return r
        return f

    for i in range(4):
        group("w2%d" % i, I["w_out_2"][0], KC, [(512 * i, 512)], "tok", xth, xtl, reader("mix"), evac_w2(i))

    run()

    put("sp", None, [(s_out, n_out[0])], False)

    def play(name, e):
        for todo, fn, signal in queue[name]:
            for s, n in todo:
                e.wait_ge(s, n)
            if fn is None:
                continue
            ins = fn(e)
            if signal:
                ins.then_inc(sem[name], 1)

    with nc.Block() as block:
        @block.sync
        def _(e):
            play("sp", e)

        @block.scalar
        def _(e):
            play("act", e)

        @block.gpsimd
        def _(e):
            play("pool", e)

        @block.vector
        def _(e):
            play("dve", e)

        @block.tensor
        def _(e):
            play("pe", e)


_OUT = ((1, SEQ, D), "float32")


def kernel(**inputs):
    import concourse.bacc as bacc
    from concourse.bass_utils import run_bass_kernel_spmd

    nc = bacc.Bacc("TRN2", target_bir_lowering=False, num_devices=1)
    arrays, aps = {}, {}
    for name in inputs:
        a = np.ascontiguousarray(inputs[name])
        arrays[f"in_{name}"] = a
        aps[name] = nc.dram_tensor(f"in_{name}", a.shape, mybir.dt.from_np(a.dtype), kind="ExternalInput").ap()
    c = shape_constants()
    arrays["in_shape_constants"] = c
    cst = nc.dram_tensor("in_shape_constants", c.shape, F, kind="ExternalInput").ap()
    out = nc.dram_tensor("out_0", _OUT[0], mybir.dt.from_np(np.dtype(_OUT[1])), kind="ExternalOutput").ap()
    build(nc, aps, cst, out)
    r = run_bass_kernel_spmd(nc, [arrays], core_ids=[0])
    return r.results[0]["out_0"]
```
